# Optimizing a Trainium2 kernel written in Bass

```python
import math
import jax, jax.numpy as jnp
from jax import lax
import numpy as np

D_MODEL = 1024
BATCH = 1
SEQ = 512
DEPTH = 2

N_A = max(1, DEPTH // 2)
N_B = DEPTH - N_A
HGRN_HEADS = 8
HGRN_DK = D_MODEL // HGRN_HEADS
HGRN_DV = D_MODEL // HGRN_HEADS
HGRN_FDIM = HGRN_HEADS * HGRN_DK
HGRN_CHUNK = 16
SB_HEADS = 8
SB_HEAD_DIM = 128
SB_DIM = SB_HEADS * SB_HEAD_DIM
SB_QBLOCK = 128
PEER_HEADS = 4
PEER_NKEYS = 128
PEER_N = PEER_NKEYS * PEER_NKEYS
PEER_DK = 256
PEER_TOPK = 16
PEER_TOKEN_BLOCK = 128
NORM_EPS = 1e-6


def rms_norm(x, g):
    xf = x.astype(jnp.float32)
    y = xf * lax.rsqrt(jnp.mean(xf * xf, axis=-1, keepdims=True) + NORM_EPS)
    return (y * g.astype(jnp.float32)).astype(x.dtype)

def modulate(xn, shift, scale):
    return xn * (1 + scale[:, None, :]) + shift[:, None, :]

def hgrn2_mixer(xn, w_in, lb, onorm_g, w_out):
    b, s, _ = xn.shape
    nc = s // HGRN_CHUNK
    proj = xn @ w_in
    q, f, i, g = jnp.split(proj, [HGRN_FDIM, 2 * HGRN_FDIM, 2 * HGRN_FDIM + D_MODEL], axis=-1)
    lbf = lb.astype(jnp.float32)
    fgate = lbf + (1 - lbf) * jax.nn.sigmoid(f.astype(jnp.float32))
    log_f = jnp.log(fgate)
    k = 1 - fgate
    q = jax.nn.silu(q.astype(jnp.float32))
    v = i.astype(jnp.float32)

    def to_chunks(t, d):
        return t.reshape(b, nc, HGRN_CHUNK, HGRN_HEADS, d).transpose(1, 0, 3, 2, 4)

    causal = jnp.tril(jnp.ones((HGRN_CHUNK, HGRN_CHUNK), dtype=bool))

    def step(state, inp):
        qc, kc, vc, lfc = inp
        cum = jnp.cumsum(lfc, axis=2)
        last = cum[:, :, -1:, :]
        qd = qc * jnp.exp(cum)
        kd = kc * jnp.exp(-cum)
        scores = jnp.where(causal, jnp.einsum('bhtk,bhsk->bhts', qd, kd), 0.0)
        o = (jnp.einsum('bhts,bhsv->bhtv', scores, vc)
             + jnp.einsum('bhtk,bhkv->bhtv', qd, state))
        new_state = (jnp.exp(last[:, :, 0, :])[..., None] * state
                     + jnp.einsum('bhsk,bhsv->bhkv', kc * jnp.exp(last - cum), vc))
        return new_state, o

    state0 = jnp.zeros((b, HGRN_HEADS, HGRN_DK, HGRN_DV), jnp.float32)
    _, o = lax.scan(step, state0, (to_chunks(q, HGRN_DK), to_chunks(k, HGRN_DK),
                                   to_chunks(v, HGRN_DV), to_chunks(log_f, HGRN_DK)))
    o = o.transpose(1, 0, 3, 2, 4).reshape(b, s, HGRN_HEADS, HGRN_DV)
    o = o * lax.rsqrt(jnp.mean(o * o, axis=-1, keepdims=True) + NORM_EPS)
    o = o.reshape(b, s, D_MODEL) * onorm_g.astype(jnp.float32) * jax.nn.silu(g.astype(jnp.float32))
    return o.astype(xn.dtype) @ w_out

def shared_kv(h, c_act, kv_ada_w, kv_ada_b, kv_norm_g, kv_w):
    b, s, _ = h.shape
    shift, scale = jnp.split(c_act @ kv_ada_w + kv_ada_b, 2, axis=-1)
    hn = modulate(rms_norm(h, kv_norm_g), shift, scale)
    kv = (hn @ kv_w).reshape(b, s, 2, SB_HEADS, SB_HEAD_DIM)
    k = kv[:, :, 0].transpose(0, 2, 1, 3)
    v = kv[:, :, 1].transpose(0, 2, 1, 3)
    return k, v

def stick_breaking_mixer(xn, k_sh, v_sh, w_q, w_out):
    b, s, _ = xn.shape
    nq = s // SB_QBLOCK
    q = (xn @ w_q).reshape(b, s, SB_HEADS, SB_HEAD_DIM).transpose(0, 2, 1, 3) * (1.0 / math.sqrt(SB_HEAD_DIM))
    loc = jnp.arange(SB_QBLOCK)
    tri = (loc[:, None] >= loc[None, :]).astype(jnp.float32)
    outs = []
    for i in range(nq):
        nk = i + 1
        qi = q[:, :, i * SB_QBLOCK:(i + 1) * SB_QBLOCK]
        kb = k_sh[:, :, :nk * SB_QBLOCK].reshape(b, SB_HEADS, nk, SB_QBLOCK, SB_HEAD_DIM)
        vb = v_sh[:, :, :nk * SB_QBLOCK].reshape(b, SB_HEADS, nk, SB_QBLOCK, SB_HEAD_DIM)
        z = jnp.einsum('bhqd,bhnsd->bhqns', qi, kb).astype(jnp.float32)
        s_pos = jnp.arange(nk * SB_QBLOCK).reshape(nk, SB_QBLOCK)
        t_pos = i * SB_QBLOCK + loc
        mask = s_pos[None, :, :] < t_pos[:, None, None]
        log_keep = jnp.where(mask, jax.nn.log_sigmoid(-z), 0.0)
        cs_in = jnp.einsum('bhqnj,js->bhqns', log_keep, tri)
        blk = cs_in[..., 0]
        after = lax.cumsum(blk, axis=3, reverse=True) - blk
        a = jnp.where(mask, jnp.exp(z + cs_in + after[..., None]), 0.0)
        outs.append(jnp.einsum('bhqns,bhnsd->bhqd', a.astype(vb.dtype), vb))
    o = jnp.concatenate(outs, axis=2)
    o = o.transpose(0, 2, 1, 3).reshape(b, s, SB_DIM)
    return o @ w_out

def peer_ffn(xn, w_q, subkeys, u, v):
    b, s, d = xn.shape
    t = b * s
    nb = t // PEER_TOKEN_BLOCK
    xt = xn.reshape(t, d)
    qr = (xt @ w_q).reshape(t, PEER_HEADS, 2, PEER_DK // 2)
    sc = jnp.einsum('thpd,hpnd->thpn', qr, subkeys).astype(jnp.float32)
    s1, i1 = lax.top_k(sc[:, :, 0], PEER_TOPK)
    s2, i2 = lax.top_k(sc[:, :, 1], PEER_TOPK)
    cand = (s1[..., :, None] + s2[..., None, :]).reshape(t, PEER_HEADS, PEER_TOPK * PEER_TOPK)
    best, flat = lax.top_k(cand, PEER_TOPK)
    e1 = jnp.take_along_axis(i1, flat // PEER_TOPK, axis=-1)
    e2 = jnp.take_along_axis(i2, flat % PEER_TOPK, axis=-1)
    experts = (e1 * PEER_NKEYS + e2).reshape(nb, PEER_TOKEN_BLOCK, PEER_HEADS * PEER_TOPK)
    gates = jax.nn.softmax(best, axis=-1).reshape(nb, PEER_TOKEN_BLOCK, PEER_HEADS * PEER_TOPK)

    def block(args):
        xc, ec, gc = args
        hid = jnp.einsum('cd,ced->ce', xc, jnp.take(u, ec, axis=0)).astype(jnp.float32)
        w = (gc * jax.nn.gelu(hid, approximate=False)).astype(xc.dtype)
        return jnp.einsum('ce,ced->cd', w, jnp.take(v, ec, axis=0))

    out = lax.map(block, (xt.reshape(nb, PEER_TOKEN_BLOCK, d), experts, gates))
    return out.reshape(b, s, d)

def first_inputs(seed: int = 0) -> dict:
    key = jax.random.key(seed)
    ks = jax.random.split(key, 22)
    D = D_MODEL

    def nrm(k, shape, std):
        return jax.random.normal(k, shape, jnp.float32) * std

    return {
        'x': nrm(ks[0], (BATCH, SEQ, D), 1.0),
        'c': nrm(ks[1], (BATCH, D), 1.0),
        'ada_w': nrm(ks[2], (DEPTH, D, 6 * D), 0.5 * D ** -0.5),
        'ada_b': nrm(ks[3], (DEPTH, 6 * D), 0.02),
        'norm_mix_g': 1.0 + nrm(ks[4], (DEPTH, D), 0.02),
        'norm_ffn_g': 1.0 + nrm(ks[5], (DEPTH, D), 0.02),
        'hgrn_w_in': nrm(ks[6], (N_A, D, 2 * HGRN_FDIM + 2 * D), D ** -0.5),
        'hgrn_lb_logits': nrm(ks[7], (N_A + 1, HGRN_FDIM), 0.5),
        'hgrn_onorm_g': 1.0 + nrm(ks[8], (N_A, D), 0.02),
        'hgrn_w_out': nrm(ks[9], (N_A, D, D), D ** -0.5),
        'kv_ada_w': nrm(ks[10], (D, 2 * D), 0.5 * D ** -0.5),
        'kv_ada_b': nrm(ks[11], (2 * D,), 0.02),
        'kv_norm_g': 1.0 + nrm(ks[12], (D,), 0.02),
        'kv_w': nrm(ks[13], (D, 2 * SB_DIM), D ** -0.5),
        'sb_w_q': nrm(ks[14], (N_B, D, SB_DIM), D ** -0.5),
        'sb_w_out': nrm(ks[15], (N_B, SB_DIM, D), SB_DIM ** -0.5),
        'peer_w_q': nrm(ks[16], (DEPTH, D, PEER_HEADS * PEER_DK), D ** -0.5),
        'peer_subkeys': nrm(ks[17], (DEPTH, PEER_HEADS, 2, PEER_NKEYS, PEER_DK // 2), (PEER_DK // 2) ** -0.5),
        'peer_u': nrm(ks[18], (DEPTH, PEER_N, D), D ** -0.5),
        'peer_v': nrm(ks[19], (DEPTH, PEER_N, D), PEER_HEADS ** -0.5),
        'final_norm_g': 1.0 + nrm(ks[20], (D,), 0.02),
    }

def first_block(x, c, ada_w, ada_b, norm_mix_g, norm_ffn_g, hgrn_w_in, hgrn_lb_logits,
              hgrn_onorm_g, hgrn_w_out, kv_ada_w, kv_ada_b, kv_norm_g, kv_w, sb_w_q,
              sb_w_out, peer_w_q, peer_subkeys, peer_u, peer_v, final_norm_g):
    c_act = jax.nn.silu(c)
    lb_all = jnp.cumsum(jax.nn.softmax(hgrn_lb_logits.astype(jnp.float32), axis=0), axis=0)
    h = x
    k_sh = None
    v_sh = None
    for l in range(DEPTH):
        mod = c_act @ ada_w[l] + ada_b[l]
        sh1, sc1, g1, sh2, sc2, g2 = jnp.split(mod, 6, axis=-1)
        hn = modulate(rms_norm(h, norm_mix_g[l]), sh1, sc1)
        if l < N_A:
            mix = hgrn2_mixer(hn, hgrn_w_in[l], lb_all[l], hgrn_onorm_g[l], hgrn_w_out[l])
        else:
            mix = stick_breaking_mixer(hn, k_sh, v_sh, sb_w_q[l - N_A], sb_w_out[l - N_A])
        h = h + g1[:, None, :] * mix
        hn = modulate(rms_norm(h, norm_ffn_g[l]), sh2, sc2)
        h = h + g2[:, None, :] * peer_ffn(hn, peer_w_q[l], peer_subkeys[l], peer_u[l], peer_v[l])
        if l == N_A - 1:
            k_sh, v_sh = shared_kv(h, c_act, kv_ada_w, kv_ada_b, kv_norm_g, kv_w)
    return rms_norm(h, final_norm_g)


DEPTH_2 = 1

H_A = 4
DK_A = 128
DV_A = 128
W_A = H_A * DV_A
CONV_W = 4
CHUNK = 64
H_B = 4
R_KV = 128
DV_B = 128
W_B = H_B * DV_B
H_IDX = 8
D_IDX = 64
TOPK_MAX = 256
Q_BLOCK = 128
N_BUCKETS = 32
MAX_EXACT = 16
MAX_DIST = 128
EPS = 1e-6
SPLITS = (3 * W_A, W_A, H_A, H_A, H_B * R_KV, R_KV, W_B, H_IDX * D_IDX, D_IDX, H_IDX)
SPLIT_OFFSETS = (3072 // 2, 2048, 2052, 2056, 2568, 2696, 3208, 3720, 3784)
D_IN = 3792


def rmsnorm(x, g):
    xf = x.astype(jnp.float32)
    xf = xf * lax.rsqrt(jnp.mean(xf * xf, axis=-1, keepdims=True) + EPS)
    return xf.astype(x.dtype) * g

def l2norm(x):
    return x * lax.rsqrt(jnp.sum(x * x, axis=-1, keepdims=True) + EPS)

def causal_conv(u, w):
    L = u.shape[1]
    up = jnp.pad(u, ((0, 0), (CONV_W - 1, 0), (0, 0)))
    out = up[:, 0:L] * w[0]
    for j in range(1, CONV_W):
        out = out + up[:, j:j + L] * w[j]
    return out

def t5_bucket(dist):
    n = jnp.maximum(dist, 0)
    nf = jnp.maximum(n, 1).astype(jnp.float32)
    large = MAX_EXACT + (jnp.log(nf / MAX_EXACT) / math.log(MAX_DIST / MAX_EXACT)
                         * (N_BUCKETS - MAX_EXACT)).astype(jnp.int32)
    large = jnp.minimum(large, N_BUCKETS - 1)
    return jnp.where(n < MAX_EXACT, n, large)

def gated_deltanet(qkv, z, b, a, conv_w, a_log, dt_bias, g_norm):
    Bsz, L, _ = qkv.shape
    n_chunks = L // CHUNK
    qkv = jax.nn.silu(causal_conv(qkv, conv_w))
    q, k, v = jnp.split(qkv, 3, axis=-1)

    def heads(t, d):
        t = t.reshape(Bsz, L, H_A, d).transpose(0, 2, 1, 3).astype(jnp.float32)
        return t.reshape(Bsz, H_A, n_chunks, CHUNK, d)

    q = l2norm(heads(q, DK_A)) * (DK_A ** -0.5)
    k = l2norm(heads(k, DK_A))
    v = heads(v, DV_A)
    beta = jax.nn.sigmoid(b.astype(jnp.float32)).transpose(0, 2, 1).reshape(Bsz, H_A, n_chunks, CHUNK)
    g = -jnp.exp(a_log.astype(jnp.float32)) * jax.nn.softplus(a.astype(jnp.float32) + dt_bias.astype(jnp.float32))
    g = g.transpose(0, 2, 1).reshape(Bsz, H_A, n_chunks, CHUNK)
    gc = jnp.cumsum(g, axis=-1)
    pos = jnp.arange(CHUNK)
    causal = pos[:, None] >= pos[None, :]
    strict = pos[:, None] > pos[None, :]
    decay = jnp.exp(jnp.where(causal, gc[..., :, None] - gc[..., None, :], -jnp.inf))
    kb = k * beta[..., None]
    vb = v * beta[..., None]
    lmat = jnp.where(strict, jnp.einsum('bhnik,bhnjk->bhnij', kb, k) * decay, 0.0)
    eye = jnp.eye(CHUNK, dtype=jnp.float32)
    tmat = lax.linalg.triangular_solve(lmat + eye, jnp.broadcast_to(eye, lmat.shape),
                                       left_side=True, lower=True, unit_diagonal=True)
    u = jnp.einsum('bhnij,bhnjd->bhnid', tmat, vb)
    w = jnp.einsum('bhnij,bhnjd->bhnid', tmat, kb * jnp.exp(gc)[..., None])
    attn = jnp.einsum('bhnik,bhnjk->bhnij', q, k) * decay
    qg = q * jnp.exp(gc)[..., None]
    kg = k * jnp.exp(gc[..., -1:] - gc)[..., None]
    glast = jnp.exp(gc[..., -1])
    xs = tuple(jnp.moveaxis(t, 2, 0) for t in (qg, kg, u, w, attn, glast))

    def step(S, inp):
        qg_c, kg_c, u_c, w_c, attn_c, gl_c = inp
        v_new = u_c - jnp.einsum('bhck,bhkv->bhcv', w_c, S)
        o = jnp.einsum('bhck,bhkv->bhcv', qg_c, S) + jnp.einsum('bhij,bhjv->bhiv', attn_c, v_new)
        S = S * gl_c[..., None, None] + jnp.einsum('bhck,bhcv->bhkv', kg_c, v_new)
        return S, o

    S0 = jnp.zeros((Bsz, H_A, DK_A, DV_A), jnp.float32)
    _, o = lax.scan(step, S0, xs)
    o = jnp.moveaxis(o, 0, 2).reshape(Bsz, H_A, L, DV_A).transpose(0, 2, 1, 3)
    o = rmsnorm(o, g_norm.astype(jnp.float32))
    o = o.reshape(Bsz, L, W_A) * jax.nn.silu(z.astype(jnp.float32))
    return o.astype(qkv.dtype)

def dsa_sparse_attention(q_b, ckv, iq, ik, iw, g_kv, w_uv, rel_bias, z):
    Bsz, L, _ = q_b.shape
    n_blocks = L // Q_BLOCK
    k_top = min(TOPK_MAX, L // 4)
    ckv = rmsnorm(ckv, g_kv)
    q_b = q_b.reshape(Bsz, L, H_B, R_KV)
    iq = iq.reshape(Bsz, L, H_IDX, D_IDX)
    iw = iw * (H_IDX ** -0.5 * D_IDX ** -0.5)
    key_pos = jnp.arange(L, dtype=jnp.int32)

    def to_blocks(t):
        return jnp.moveaxis(t.reshape((Bsz, n_blocks, Q_BLOCK) + t.shape[2:]), 1, 0)

    def block(args):
        qb, iqb, iwb, t0 = args
        t = t0 + jnp.arange(Q_BLOCK, dtype=jnp.int32)
        rel = jnp.einsum('bqhd,bsd->bqhs', iqb, ik)
        score = jnp.einsum('bqh,bqhs->bqs', iwb.astype(jnp.float32), jax.nn.relu(rel).astype(jnp.float32))
        score = jnp.where(key_pos[None, None, :] <= t[None, :, None], score, -jnp.inf)
        _, sel = lax.top_k(score, k_top)
        kv_sel = jax.vmap(lambda kv, i: kv[i])(ckv, sel)
        dist = t[None, :, None] - sel
        bias = jnp.moveaxis(rel_bias[t5_bucket(dist)], 3, 2)
        logits = (jnp.einsum('bqhr,bqkr->bqhk', qb, kv_sel).astype(jnp.float32) * (R_KV ** -0.5)
                  + bias.astype(jnp.float32))
        logits = jnp.where((dist >= 0)[:, :, None, :], logits, -jnp.inf)
        p = jax.nn.softmax(logits, axis=-1).astype(kv_sel.dtype)
        return jnp.einsum('bqhk,bqkr->bqhr', p, kv_sel)

    t0s = jnp.arange(n_blocks, dtype=jnp.int32) * Q_BLOCK
    o = lax.map(block, (to_blocks(q_b), to_blocks(iq), to_blocks(iw), t0s))
    o = jnp.moveaxis(o, 0, 1).reshape(Bsz, L, H_B, R_KV)
    o = jnp.einsum('blhr,hrd->blhd', o, w_uv).reshape(Bsz, L, W_B)
    return o * jax.nn.silu(z)

def second_inputs(seed: int = 0) -> dict:
    key = jax.random.key(seed)
    ks = jax.random.split(key, 16)
    nrm = jax.random.normal
    x = nrm(ks[0], (BATCH, SEQ, D_MODEL), jnp.float32)
    c = nrm(ks[1], (BATCH, D_MODEL), jnp.float32)
    w_ada = nrm(ks[2], (DEPTH_2, D_MODEL, 3 * D_MODEL), jnp.float32) * (0.5 * D_MODEL ** -0.5)
    b_ada = 0.01 * nrm(ks[3], (DEPTH_2, 3 * D_MODEL), jnp.float32)
    g_pre = 1.0 + 0.05 * nrm(ks[4], (DEPTH_2, D_MODEL), jnp.float32)
    w_in = nrm(ks[5], (DEPTH_2, D_MODEL, D_IN), jnp.float32) * (D_MODEL ** -0.5)
    conv_w = nrm(ks[6], (DEPTH_2, CONV_W, 3 * W_A), jnp.float32) * (CONV_W ** -0.5)
    a_log = jnp.log(jax.random.uniform(ks[7], (DEPTH_2, H_A), jnp.float32, 1.0, 16.0))
    dt = jnp.exp(jax.random.uniform(ks[8], (DEPTH_2, H_A), jnp.float32, math.log(1e-3), math.log(1e-1)))
    dt_bias = dt + jnp.log(-jnp.expm1(-dt))
    g_gdn = 1.0 + 0.05 * nrm(ks[9], (DEPTH_2, DV_A), jnp.float32)
    g_kv = 1.0 + 0.05 * nrm(ks[10], (DEPTH_2, R_KV), jnp.float32)
    w_uv = nrm(ks[11], (DEPTH_2, H_B, R_KV, DV_B), jnp.float32) * (R_KV ** -0.5)
    rel_bias = 0.5 * nrm(ks[12], (N_BUCKETS, H_B), jnp.float32)
    w_out = nrm(ks[13], (DEPTH_2, W_A + W_B, D_MODEL), jnp.float32) * ((W_A + W_B) ** -0.5)
    g_post = 1.0 + 0.05 * nrm(ks[14], (DEPTH_2, D_MODEL), jnp.float32)
    return {'x': x, 'c': c, 'w_ada': w_ada, 'b_ada': b_ada, 'g_pre': g_pre, 'w_in': w_in,
            'conv_w': conv_w, 'a_log': a_log, 'dt_bias': dt_bias, 'g_gdn': g_gdn, 'g_kv': g_kv,
            'w_uv': w_uv, 'rel_bias': rel_bias, 'w_out': w_out, 'g_post': g_post}

def second_block(x, c, w_ada, b_ada, g_pre, w_in, conv_w, a_log, dt_bias, g_gdn, g_kv, w_uv, rel_bias, w_out, g_post):
    for layer in range(DEPTH_2):
        mod = jax.nn.silu(c) @ w_ada[layer] + b_ada[layer]
        shift, scale, gate = jnp.split(mod, 3, axis=-1)
        h = rmsnorm(x, g_pre[layer]) * (1.0 + scale[:, None, :]) + shift[:, None, :]
        proj = h @ w_in[layer]
        (qkv_a, z_a, b_a, a_a, q_b, ckv, z_b, iq, ik, iw) = jnp.split(proj, list(SPLIT_OFFSETS), axis=-1)
        o_a = gated_deltanet(qkv_a, z_a, b_a, a_a, conv_w[layer], a_log[layer], dt_bias[layer], g_gdn[layer])
        o_b = dsa_sparse_attention(q_b, ckv, iq, ik, iw, g_kv[layer], w_uv[layer], rel_bias, z_b)
        mix = jnp.concatenate([o_a, o_b], axis=-1) @ w_out[layer]
        x = x + gate[:, None, :] * rmsnorm(mix, g_post[layer])
    return x


def setup_inputs(seed=0):
    out = dict(first_inputs(seed))
    for name, value in second_inputs(seed + 1).items():
        if name != "x":
            out[name + "_2"] = value
    return out


def reference(
    x, c, ada_w, ada_b, norm_mix_g, norm_ffn_g, hgrn_w_in, hgrn_lb_logits, hgrn_onorm_g,
    hgrn_w_out, kv_ada_w, kv_ada_b, kv_norm_g, kv_w, sb_w_q, sb_w_out, peer_w_q, peer_subkeys,
    peer_u, peer_v, final_norm_g, c_2, w_ada_2, b_ada_2, g_pre_2, w_in_2, conv_w_2, a_log_2,
    dt_bias_2, g_gdn_2, g_kv_2, w_uv_2, rel_bias_2, w_out_2, g_post_2,
):
    x = first_block(
        x, c, ada_w, ada_b, norm_mix_g, norm_ffn_g, hgrn_w_in, hgrn_lb_logits, hgrn_onorm_g,
        hgrn_w_out, kv_ada_w, kv_ada_b, kv_norm_g, kv_w, sb_w_q, sb_w_out, peer_w_q,
        peer_subkeys, peer_u, peer_v, final_norm_g,
    )
    return second_block(
        x, c_2, w_ada_2, b_ada_2, g_pre_2, w_in_2, conv_w_2, a_log_2, dt_bias_2, g_gdn_2,
        g_kv_2, w_uv_2, rel_bias_2, w_out_2, g_post_2,
    )


_drawn_inputs = setup_inputs


def setup_inputs(seed=0):
    import zlib

    import numpy as np

    out = dict(_drawn_inputs(seed))
    spreads = {}
    factors = {'norm_mix_g': 5.547,
     'norm_ffn_g': 11.333,
     'hgrn_lb_logits': 3.596,
     'hgrn_onorm_g': 7.281,
     'kv_ada_b': 5.399,
     'kv_norm_g': 7.911,
     'final_norm_g': 2.695,
     'b_ada_2': 4.402,
     'g_gdn_2': 27.914,
     'g_kv_2': 8.0,
     'rel_bias_2': 2.828,
     'g_post_2': 10.834}
    for name, (base, spread) in spreads.items():
        noise = np.random.default_rng([zlib.crc32(name.encode()), seed]).standard_normal(out[name].shape)
        drawn = base * np.exp(spread * noise) if base else spread * noise
        out[name] = __import__('jax').numpy.asarray(drawn.astype(out[name].dtype))
    for name, factor in factors.items():
        out[name] = (out[name] * factor).astype(out[name].dtype)
    return out
```

```python
from contextlib import ExitStack

import concourse.bass as bass
import numpy as np
from concourse import mybir
from concourse.alu_op_type import AluOpType as ALU

ACT = mybir.ActivationFunctionType
F32 = mybir.dt.float32
U32 = mybir.dt.uint32
AX = mybir.AxisListType.X

P = 128
D = 1024
S = 512
KC = D // P
NB = S // P
NH = 8
NE = 64
NKEY = 128
EPS = 1e-6
BIG = 3.0e38

CHUNKS_A = [(0, 1), (2, 3)]
CHUNKS_C = [(0, 1), (2, 3)]
CHUNKS_E = [(0, 1), (2,), (3,)]
TM = 256
NGATHER = 8
NWEIGHT = 8


def bucket(n):
    n = np.maximum(n, 0)
    nf = np.maximum(n, 1).astype(np.float32)
    large = 16 + (np.log(nf / np.float32(16)) / np.float32(np.log(128 / 16)) * np.float32(16)).astype(np.int32)
    return np.where(n < 16, n, np.minimum(large, 31))


CONSTS = ["ident", "ones", "cols", "strict", "nones", "mask16", "ntri", "reset", "negm", "iota"]
CONSTS_E = ["tri64", "sup64", "str64", "m1", "m1t", "m2", "m4", "m8", "m16", "m32"]


def constants():
    r = np.arange(P)
    i, j = r[:, None], r[None, :]
    same = lambda n: (i // n) == (j // n)
    c = {}
    c["ident"] = i == j
    c["ones"] = np.ones((P, P))
    c["nones"] = -np.ones((P, P))
    c["mask16"] = same(16) & (i <= j)
    c["ntri"] = -1.0 * (i >= j)
    c["strict"] = i < j
    c["negm"] = np.where(i < j, 0.0, -1e30)
    c["reset"] = (j % 16 != 0) & (i >= 0)
    c["iota"] = np.tile(np.arange(16), (P, 1))
    c["cols"] = np.tile(np.array([EPS, 1.0, -0.5 * np.log(128.0), 0.0]), (P, 1))
    c["tri64"] = same(64) & (i <= j)
    c["sup64"] = same(64) & (i > j)
    c["str64"] = same(64) & (i < j)
    for m in (1, 2, 4, 8, 16, 32):
        c[f"m{m}"] = same(2 * m) & (i % (2 * m) >= m) & (j % (2 * m) < m)
    c["m1t"] = c["m1"].T
    hot = np.zeros((P, 384))
    hot[bucket(255 - np.arange(384)), np.arange(384)] = 1.0
    c["hot"] = hot
    return {k: np.asarray(v, np.float32) for k, v in c.items()}


def const_array(names):
    c = constants()
    return np.ascontiguousarray(np.concatenate([c[k] for k in names], axis=1))


class Mark:

    def __init__(self, sem):
        self.sem, self.value = sem, 0


class Step:
    def __init__(self, unit, emit, after, us, nbytes=0, mark=None):
        self.unit, self.emit, self.after, self.us = unit, emit, after, us
        self.nbytes, self.mark, self.value = nbytes, mark, 0
        self.rank, self.place, self.lane, self.func = 0.0, 0, None, None


def flat(after):
    out = []
    for a in after:
        if a is None:
            continue
        if isinstance(a, (list, tuple)):
            out += flat(a)
        else:
            out.append(a)
    return out


def cols(ap):
    n = 1
    for s in ap.shape[1:]:
        n *= s
    return n


class Plan:
    UNITS = ("sp", "pool", "pe", "act", "dve")

    def __init__(self):
        self.steps = []

    def add(self, unit, emit, after, us, nbytes=0, mark=None, lane=None):
        s = Step(unit, emit, flat(after), us, nbytes, mark)
        if mark is not None:
            mark.value += 16
            s.value = mark.value
        s.lane = lane
        self.steps.append(s)
        return s

    def mm(self, bank, out, lhsT, rhs, start, stop, after=(), share=False):
        us = 4 * max(cols(rhs), 64) / 2400
        return self.add("pe", lambda e: e.matmul(out, lhsT, rhs, start=start, stop=stop, skip_group_check=share),
                        after, us, lane=bank)

    def tr(self, bank, out, in_, ident, after=()):
        return self.add("pe", lambda e: e.transpose(out, in_, ident), after, 0.11, lane=bank)

    def act(self, out, in_, func, after=(), bias=0.0, scale=1.0, accum=None):
        us = 0.1 + cols(in_) * 0.833e-3 + 0.093 * (not isinstance(scale, float)) + 0.093 * (not isinstance(bias, float))
        if accum is not None:
            s = self.add("act", lambda e: e.activation(out, in_, func, bias=bias, scale=scale, accum_out=accum),
                         after, us + 0.1)
        else:
            s = self.add("act", lambda e: e.activation(out, in_, func, bias=bias, scale=scale), after, us)
        s.func = func
        return s

    def vec(self, emit, n, after, rate=1.0):
        return self.add("dve", emit, after, 0.07 + n * rate * 1.04e-3)

    def tt(self, out, a, b, op, after=()):
        return self.vec(lambda e: e.tensor_tensor(out, a, b, op), cols(out), after)

    def ts(self, out, a, s1, s2, op0, op1=None, after=()):
        if op1 is None:
            return self.vec(lambda e: e.tensor_scalar(out, a, s1, None, op0), cols(out), after)
        return self.vec(lambda e: e.tensor_scalar(out, a, s1, s2, op0, op1), cols(out), after)

    def stt(self, out, a, s, b, op0, op1, after=()):
        return self.vec(lambda e: e.scalar_tensor_tensor(out, a, s, b, op0, op1), cols(out), after)

    def cp(self, out, a, after=()):
        return self.vec(lambda e: e.tensor_copy(out, a), cols(out), after)

    def fill(self, out, value, after=()):
        return self.vec(lambda e: e.memset(out, value), cols(out), after)

    def dma(self, unit, out, in_, mark, nbytes, after=(), lane=None):
        return self.add(unit, lambda e: e.dma_start(out, in_), after, 0.6, nbytes, mark, lane)

    def gather(self, out, table, idx, mark, after=()):
        return self.add("pool", lambda e: e.indirect_dma_start(out, None, table, bass.IndirectOffsetOnAxis(idx, 0)),
                        after, 1.04, P * D * 4, mark, "gather")

    def order(self):
        steps = self.steps
        follow = {id(s): [] for s in steps}
        pending = {}
        lanes = {}
        for s in steps:
            before = {id(a): a for a in s.after}
            if s.lane is not None:
                prev = lanes.get((s.unit, s.lane))
                if prev is not None:
                    before[id(prev)] = prev
                lanes[(s.unit, s.lane)] = s
            pending[id(s)] = len(before)
            for a in before.values():
                follow[id(a)].append(s)
        for s in reversed(steps):
            us = max(s.us, s.nbytes / 360e3)
            s.rank = us + max([f.rank for f in follow[id(s)]], default=0.0)
        queues = {u: [] for u in self.UNITS}
        ready = {u: [] for u in self.UNITS}
        coming = {u: [] for u in self.UNITS}
        free = {u: 0.0 for u in self.UNITS}
        reach, bus, now, left = {}, 0.0, 0.0, len(steps)
        for k, s in enumerate(steps):
            s.place = k
            if pending[id(s)] == 0:
                ready[s.unit].append(s)
        while left:
            for u in self.UNITS:
                if free[u] > now + 1e-9:
                    continue
                if coming[u]:
                    ready[u] += [s for at, s in coming[u] if at <= now + 1e-9]
                    coming[u] = [(at, s) for at, s in coming[u] if at > now + 1e-9]
                if not ready[u]:
                    continue
                s = max(ready[u], key=lambda s: (s.rank, -s.place))
                ready[u].remove(s)
                queues[u].append(s)
                left -= 1
                free[u] = end = now + s.us
                if s.mark is not None:
                    bus = max(bus, end) + s.nbytes / 360e3
                    end = bus + 2.0
                for f in follow[id(s)]:
                    at = end + 0.13 if s in f.after else free[u]
                    reach[id(f)] = max(reach.get(id(f), 0.0), at)
                    pending[id(f)] -= 1
                    if pending[id(f)] == 0:
                        coming[f.unit].append((reach[id(f)], f))
            times = [free[u] for u in self.UNITS if ready[u]]
            times += [max(free[u], min(at for at, _ in coming[u])) for u in self.UNITS if coming[u]]
            if left:
                now = max(now, min(times))
        self.end = now
        for u in self.UNITS:
            for k, s in enumerate(queues[u]):
                s.place = k
        return queues

    def emit(self, nc, sems, last):
        queues = self.order()
        for u in self.UNITS:
            n = 0
            for s in queues[u]:
                if s.mark is None:
                    n += 1
                    s.value = n

        def run(eng, unit):
            seen = {}
            table = None
            for s in queues[unit]:
                if s.func in (ACT.Exp, ACT.Ln) and table != "exp_ln":
                    eng.preload_act_table_set("natural_log_exp_and_others")
                    table = "exp_ln"
                if s.func == ACT.Gelu:
                    table = "gelu"
                need = {}
                for a in s.after:
                    key = a.unit if a.mark is None else a.mark
                    need[key] = max(need.get(key, 0), a.value)
                for key, value in need.items():
                    if seen.get(key, 0) < value:
                        seen[key] = value
                        eng.wait_ge(sems[key] if isinstance(key, str) else key.sem, value)
                ins = s.emit(eng)
                if s.mark is None:
                    ins.then_inc(sems[unit], 1)
                else:
                    ins.then_inc(s.mark.sem, 16)
            if unit == "sp":
                for s in last:
                    eng.wait_ge(s.mark.sem, s.value)

        with nc.Block() as block:
            @block.sync
            def _(e):
                run(e, "sp")

            @block.gpsimd
            def _(e):
                run(e, "pool")

            @block.tensor
            def _(e):
                run(e, "pe")

            @block.scalar
            def _(e):
                run(e, "act")

            @block.vector
            def _(e):
                run(e, "dve")


class Ring:

    def __init__(self, n):
        self.n, self.next, self.free = n, 0, [[] for _ in range(n)]

    def take(self):
        i, fr = self.next, self.free[self.next]
        assert fr is not None, "slot still in use"
        self.next, self.free[i] = (i + 1) % self.n, None
        return i, fr

    def done(self, i, steps):
        self.free[i] = list(steps)


VECS = {}


def _vec_cols():
    at = 0
    for name, n in (("ada_b0", 48), ("ada_b1", 48), ("mix0", 8), ("mix1", 8), ("ffn0", 8),
                    ("ffn1", 8), ("lb0", 8), ("lb1", 8), ("onorm", 8), ("kv_b", 16), ("kv_g", 8), ("fin", 8),
                    ("b_2", 24), ("pre", 8), ("post", 8), ("conv", 48), ("gdn", 1), ("gkv", 1)):
        VECS[name] = (at, n)
        at += n
    return at


NVEC = _vec_cols()


def layer_stack_kernel(nc: bass.Bass, t: dict, out: bass.AP, upto: str = "E", probes=None):
    ctx = ExitStack()
    sb = lambda name, shape, dt=F32: ctx.enter_context(nc.sbuf_tensor(name, shape, dt))
    sem = lambda name: ctx.enter_context(nc.semaphore(name))
    mark = lambda name: Mark(sem(name))
    sems = {u: sem("s_" + u) for u in ("pool", "pe", "act", "dve")}
    p = Plan()

    ps = ctx.enter_context(nc.psum_tensor("ps", [P, 8, 512], F32))
    cc = {k: v.shape[1] for k, v in constants().items()}
    cst = sb("cst", [P, sum(cc[k] for k in CONSTS)])
    vec = sb("vec", [P, NVEC])
    h = sb("h", [P, NB, D])
    hn = sb("hn", [P, KC, TM])
    oT = sb("oT", [P, KC, TM])
    X = [sb(f"X{i}", [P, D]) for i in range(2)]
    xs = sb("xs", [P, D])
    acc = sb("acc", [P, D])
    gat = [sb(f"gat{i}", [P, D]) for i in range(NGATHER)]
    wbuf = sb("wbuf", [P, NWEIGHT, 2, 512])
    row = [sb(f"row{i}", [P, D]) for i in range(3)]
    dgb = [sb(f"dg{i}", [P, P]) for i in range(5)]
    mod = [sb("mod0", [P, 48]), sb("mod1", [P, 48])]
    kvm = sb("kvm", [P, 16])
    mod2 = sb("mod2", [P, 24])
    gT = sb("gT", [P, 6, 8])
    spot = sb("spot", [P, 1])
    small = sb("small", [P, 16, 4])
    idxb = sb("idx", [P, NB, NE], U32)
    gate = sb("gate", [P, NB, NE])
    hid = sb("hid", [P, 2, NE])
    wgt = sb("wgt", [P, 2, NE])
    NWS = 18400
    ws = sb("ws", [P, NWS])

    def region(base):
        at = [base]

        def take(*shape):
            n = 1
            for k in shape:
                n *= k
            v = ws[:, at[0]:at[0] + n]
            at[0] += n
            assert at[0] <= NWS, at[0]
            if len(shape) == 2:
                v = v.rearrange("p (a b) -> p a b", a=shape[0])
            elif len(shape) == 3:
                v = v.rearrange("p (a b c) -> p a b c", a=shape[0], b=shape[1])
            return v

        return take, at

    C = {}
    at = 0
    for k in CONSTS:
        C[k] = cst[:, at:at + cc[k]]
        at += cc[k]
    eps, one, nhl = C["cols"][:, 0:1], C["cols"][:, 1:2], C["cols"][:, 2:3]

    def V(name, lo=0, n=None):
        a0, k = VECS[name]
        return vec[:, a0 + lo:a0 + lo + (k - lo if n is None else n)]

    m_c, m_v = mark("m_c"), mark("m_v")
    m_h = [mark(f"m_h{b}") for b in range(NB)]
    ld_v = p.dma("sp", vec[:, :], t["vecs"], m_v, P * NVEC * 4)
    ld_c = p.dma("sp", cst[:, :], t["cst"], m_c, P * cst.shape[1] * 4)
    ld_h = [p.dma("sp", h[:, b, :], t["x"][b * P:(b + 1) * P, :], m_h[b], P * D * 4) for b in range(NB)]
    hw = [[s] for s in ld_h]
    hr = [[] for _ in range(NB)]

    bankD, bankX, bankO = Ring(3), Ring(2), Ring(1)
    DB, XB, OB, VB = (0, 1, 2), (3, 4), (5,), 6
    ringW, ringG, ringV, ringR = Ring(NWEIGHT), Ring(NGATHER), Ring(3), Ring(2)
    ringS = Ring(16)
    mW = [mark(f"m_w{i}") for i in range(NWEIGHT)]
    mG = [mark(f"m_g{i}") for i in range(NGATHER)]
    mA = [mark(f"m_a{i}") for i in range(NGATHER)]
    free = {"hn": [], "oT": [], "xs": [], "acc": [], "X0": [], "X1": [], "V": []}

    row_users = {0: [], 1: [], 2: []}
    hn_users = []

    def hn_again():
        free["hn"] = list(hn_users)
        hn_users.clear()

    class Weights:

        def __init__(self, name, g):
            self.slots, self.loads = [], []
            for q in range(4):
                i, fr = ringW.take()
                self.slots.append(i)
                self.loads.append(p.dma("sp", wbuf[:, i, :, :], t[name][g, q], mW[i], P * D * 4, fr, "w"))
            self.used = [[] for _ in range(4)]

        def at(self, kc, lo, n):
            return wbuf[:, self.slots[kc // 2], kc % 2, lo:lo + n]

        def load(self, kc):
            return self.loads[kc // 2]

        def use(self, kc, step):
            self.used[kc // 2].append(step)

        def done(self):
            for i, u in zip(self.slots, self.used):
                ringW.done(i, u)

    def silu_of(outp, z, tmp, after):
        a = p.act(tmp, z, ACT.Exp, after, scale=-1.0)
        a = p.act(tmp, tmp, ACT.Ln, [a, ld_c], bias=one)
        a = p.act(tmp, tmp, ACT.Exp, [a], scale=-1.0)
        return p.tt(outp, z, tmp, ALU.mult, [a])

    crow = [acc, row[2]]
    c_ready = []
    for k in range(2):
        cr = t["cc"]
        ld = p.dma("sp", crow[k][:, :], bass.AP(cr.tensor, k * D, [[0, P], [1, D]]), mark(f"m_r{k}"), P * D * 4)
        c_ready.append(silu_of(crow[k][:, :], crow[k][:, :], xs[:, :], [ld, free["xs"]]))
        free["xs"] = [c_ready[k]]
    crow_users = [[], []]

    def matvec(name, g, k, dst, bias):
        n = dst.shape[1]
        dots = []
        for m in range(n):
            s_, fr = ringG.take()
            ld = p.dma("sp", gat[s_][:, :], t[name][g + m], mA[s_], P * D * 4, fr, "ada")
            d = p.vec(lambda e, g_=gat[s_], c_=crow[k], o=dst[:, m:m + 1]:
                      e.tensor_tensor_reduce(g_[:, :], g_[:, :], c_[:, :], 1.0, 0.0, ALU.mult, ALU.add, o),
                      D, [ld, c_ready[k]])
            ringG.done(s_, [d])
            dots.append(d)
        crow_users[k] += dots
        return p.tt(dst, dst, bias, ALU.add, [dots, ld_v])

    def modvec(l, part):
        return [matvec(f"ada{l}", 8 * part, 0, mod[l][:, 8 * part:8 * part + 8], V(f"ada_b{l}", 8 * part, 8))]

    def gain(k, scale, g, after):
        return p.stt(gT[:, k, :], scale, 1.0, g, ALU.add, ALU.mult, [after, ld_v])

    def broadcast_row(k, col8, after):
        out_steps, fr_row = [], list(row_users[k])
        row_users[k].clear()
        for half in range(2):
            i, fr = bankD.take()
            for q in range(4):
                d, dfr = ringR.take()
                d += 3
                a = p.act(dgb[d][:, :], C["ident"], ACT.Identity, [after, dfr, ld_c], scale=col8[:, 4 * half + q:4 * half + q + 1])
                mmv = p.mm(DB[i], ps[:, DB[i], q * P:(q + 1) * P], C["ones"], dgb[d][:, :], True, True, [a, fr])
                ringR.done(d - 3, [mmv])
            e = p.act(row[k][:, half * 512:half * 512 + 512], ps[:, DB[i], :], ACT.Identity, [mmv, fr_row])
            bankD.done(i, [e])
            out_steps.append(e)
        return out_steps

    def rms(src, dst, n, after):
        s, sfr = ringS.take()
        c = small[:, s, 0:1]
        a = p.act(dst, src, ACT.Square, [after, sfr], accum=c)
        a = p.act(c, c, ACT.Ln, [a], bias=eps, scale=1.0 / n)
        return p.act(c, c, ACT.Exp, [a], scale=-0.5), c, s

    def normed(src, after):
        a, c, s = rms(src, xs[:, :], D, [after, free["xs"]])
        a = p.act(xs[:, :], src, ACT.Identity, [a], scale=c)
        ringS.done(s, [a])
        return a

    def spread(a, j, targets):
        trs, evs = [], [[] for _ in targets]
        for half in range(2):
            i, fr = bankD.take()
            for q in range(4):
                kc = 4 * half + q
                trs.append(p.tr(DB[i], ps[:, DB[i], q * P:(q + 1) * P], xs[:, kc * P:(kc + 1) * P], C["ident"], [a, fr, ld_c]))
            last = []
            for q in range(4):
                kc = 4 * half + q
                for n, (dst, g, sh, after) in enumerate(targets):
                    last.append(p.ts(dst[:, kc, j * P:(j + 1) * P], ps[:, DB[i], q * P:(q + 1) * P], g[:, kc:kc + 1],
                                     sh[:, kc:kc + 1], ALU.mult, ALU.add, [trs[-1], after]))
                    evs[n].append(last[-1])
            bankD.done(i, last)
        return trs, evs

    def project(w, m, T, after, src=hn):
        i, fr = bankD.take()
        for kc in range(KC):
            last = p.mm(DB[i], ps[:, DB[i], 0:T], w.at(kc, m * P, P), src[:, kc, 0:T], kc == 0, kc == KC - 1,
                        [after, w.load(kc), fr])
            w.use(kc, last)
        return i, last

    def add_mix(w2, b, j, src, after, grow, gready):
        used = []
        new = []
        for n in range(2):
            i, fr = bankD.take()
            for kc in range(KC):
                last = p.mm(DB[i], ps[:, DB[i], :], src[:, kc, j * P:(j + 1) * P], w2[n].at(kc, 0, 512), kc == 0, kc == KC - 1,
                            [after, w2[n].load(kc), fr])
                w2[n].use(kc, last)
            used.append(last)
            k, tfr = ringT.take()
            e = p.tt(tmpb[k], ps[:, DB[i], :], row[grow][:, n * 512:n * 512 + 512], ALU.mult, [last, gready, tfr])
            bankD.done(i, [e])
            row_users[grow].append(e)
            f = p.tt(h[:, b, n * 512:n * 512 + 512], h[:, b, n * 512:n * 512 + 512], tmpb[k], ALU.add, [e, hw[b], hr[b]])
            ringT.done(k, [f])
            new.append(f)
        hw[b], hr[b] = new, []
        return used

    tw, at_ = region(0)
    tmpb = [tw(512) for _ in range(2)]
    ringT = Ring(2)
    scs = tw(8, P)
    cand = tw(4, 256)
    s16 = tw(8, 16)
    i16 = tw(8, 16).bitcast(U32)
    i16f = tw(8, 16)
    b16 = tw(4, 16)
    f16 = tw(4, 16).bitcast(U32)
    fa = tw(4, 16).bitcast(U32)
    fb = tw(4, 16).bitcast(U32)
    faf = tw(4, 16)
    fbf = tw(4, 16)
    e1 = tw(4, 16)
    e2 = tw(4, 16)
    gm = tw(4, 1)
    selfree = {"scs": [], "rest": []}
    COMMON = at_[0]

    ready = {}

    def bc(ap, *shape):
        return ap.broadcast_to([P, *shape])

    def select(l, chunk, hn_ready):
        T = P * len(chunk)
        qw = []
        for g in range(2):
            w = Weights(f"pq{l}", g)
            for m in range(4):
                i, last = project(w, m, T, hn_ready)
                hn_users.append(last)
                e = p.act(oT[:, 4 * g + m, 0:T], ps[:, DB[i], 0:T], ACT.Identity, [last, free["oT"]])
                bankD.done(i, [e])
                qw.append(e)
            w.done()
        free["oT"] = None
        si, sfr = ringW.take()
        sk = wbuf[:, si, :, :].rearrange("p a (b n) -> p (a b) n", b=4)
        ld = p.dma("sp", wbuf[:, si, :, :], t[f"sub{l}"], mW[si], P * D * 4, sfr, "w")
        scm = []
        for j, b in enumerate(chunk):
            ev = []
            for half in range(2):
                i, fr = bankD.take()
                for q in range(4):
                    hp = 4 * half + q
                    last = p.mm(DB[i], ps[:, DB[i], q * P:(q + 1) * P], oT[:, hp, j * P:(j + 1) * P], sk[:, hp, :], True, True,
                                [qw, ld, fr])
                scm.append(last)
                e = p.act(scs[:, 4 * half:4 * half + 4, :].rearrange("p a b -> p (a b)"), ps[:, DB[i], :], ACT.Identity,
                          [last, selfree["scs"]])
                bankD.done(i, [e])
                ev.append(e)
            fr = selfree["rest"]
            tops = []
            for hp in range(8):
                s_, v8, u8 = scs[:, hp, :], s16[:, hp, :], i16[:, hp, :]
                a = p.vec(lambda e, o=v8[:, 0:8], i_=s_: e.max(o, i_), P, [ev, fr])
                a = p.vec(lambda e, o=u8[:, 0:8], m=v8[:, 0:8], i_=s_: e.max_index(o, m, i_), P, [a])
                a = p.vec(lambda e, m=v8[:, 0:8], i_=s_: e.match_replace(i_, m, i_, -BIG), P, [a])
                a = p.vec(lambda e, o=v8[:, 8:16], i_=s_: e.max(o, i_), P, [a])
                a = p.vec(lambda e, o=u8[:, 8:16], m=v8[:, 8:16], i_=s_: e.max_index(o, m, i_), P, [a])
                tops.append(a)
            selfree["scs"] = tops
            ic = p.cp(i16f, i16, [tops])
            t2 = []
            for hh in range(4):
                c3 = cand[:, hh, :].rearrange("p (a b) -> p a b", a=16)
                a = p.tt(c3, bc(s16[:, 2 * hh, :].rearrange("p (a b) -> p a b", b=1), 16, 16),
                         bc(s16[:, 2 * hh + 1, :].rearrange("p (a b) -> p a b", a=1), 16, 16), ALU.add, [tops, fr])
                s_, v8, u8 = cand[:, hh, :], b16[:, hh, :], f16[:, hh, :]
                a = p.vec(lambda e, o=v8[:, 0:8], i_=s_: e.max(o, i_), 256, [a])
                a = p.vec(lambda e, o=u8[:, 0:8], m=v8[:, 0:8], i_=s_: e.max_index(o, m, i_), 256, [a])
                a = p.vec(lambda e, m=v8[:, 0:8], i_=s_: e.match_replace(i_, m, i_, -BIG), 256, [a])
                a = p.vec(lambda e, o=v8[:, 8:16], i_=s_: e.max(o, i_), 256, [a])
                a = p.vec(lambda e, o=u8[:, 8:16], m=v8[:, 8:16], i_=s_: e.max_index(o, m, i_), 256, [a])
                t2.append(a)
            gb = gate[:, b, :].rearrange("p (a b) -> p a b", a=4)
            g1_ = p.tt(gb, b16, bc(b16[:, :, 0:1], 4, 16), ALU.subtract, [t2, free.get(("gate", b), [])])
            g2_ = p.act(gb, gb, ACT.Exp, [g1_])
            g3_ = p.vec(lambda e, o=gm, i_=gb: e.tensor_reduce(o, i_, AX, ALU.add), 64, [g2_, fr])
            g4_ = p.vec(lambda e, o=gm: e.reciprocal(o, o), 4, [g3_], 8.0)
            g5_ = p.tt(gb, gb, bc(gm, 4, 16), ALU.mult, [g4_])
            a1 = p.ts(fa, f16, 4, None, ALU.logical_shift_right, None, [t2, fr])
            b1 = p.ts(fb, f16, 15, None, ALU.bitwise_and, None, [t2, fr])
            a2 = p.cp(faf, fa, [a1])
            b2 = p.cp(fbf, fb, [b1])
            oh = cand.rearrange("p h (k n) -> p h k n", k=16)
            io = bc(C["iota"].rearrange("p (a b n) -> p a b n", a=1, b=1), 4, 16, 16)
            prev = t2
            es = []
            for half, src, dst, rd in ((0, faf, e1, a2), (1, fbf, e2, b2)):
                nums = i16f.rearrange("p (h q) n -> p h q n", q=2)[:, :, half:half + 1, :]
                x1 = p.tt(oh, bc(src.rearrange("p h (k n) -> p h k n", n=1), 4, 16, 16), io, ALU.is_equal, [rd, prev, ic])
                x2 = p.tt(oh, oh, bc(nums, 4, 16, 16), ALU.mult, [x1])
                x3 = p.vec(lambda e, o=dst, i_=oh: e.tensor_reduce(o, i_, AX, ALU.add), 1024, [x2])
                prev = [x3]
                es.append(x3)
            x4 = p.stt(e2, e1, float(NKEY), e2, ALU.mult, ALU.add, [es])
            x5 = p.ts(idxb[:, b, :].rearrange("p (a b) -> p a b", a=4), e2, float(l * NKEY * NKEY), None, ALU.add, None,
                      [x4, free.get(("idx", b), [])])
            selfree["rest"] = [x5, g5_]
            ready[b] = {"idx": x5, "gate": g5_}
        ringW.done(si, scm)
        free["oT"] = scm

    def keep_rows(chunk, hn_ready):
        for j, b in enumerate(chunk):
            evs = []
            for half in range(2):
                i, fr = bankD.take()
                for q in range(4):
                    kc = 4 * half + q
                    last = p.tr(DB[i], ps[:, DB[i], q * P:(q + 1) * P], hn[:, kc, j * P:(j + 1) * P], C["ident"], [hn_ready, fr])
                hn_users.append(last)
                e = p.act(X[b % 2][:, half * 512:half * 512 + 512], ps[:, DB[i], :], ACT.Identity, [last, free[f"X{b % 2}"]])
                bankD.done(i, [e])
                evs.append(e)
            free[f"X{b % 2}"] = None
            ready[b]["X"] = evs

    vstart = {}

    def experts(l, blocks, grow, gready):
        seq = []
        us = [("u", b, e) for b in blocks for e in range(NE)]
        vs = [("v", b, e) for b in blocks for e in range(NE)]
        seq += us[:16]
        for k in range(16, len(us)):
            seq += [us[k], vs[k - 16]]
        seq += vs[-16:]
        dots = {}
        accs = {b: [] for b in blocks}
        wsteps = {}
        for kind, b, e in seq:
            s, fr = ringG.take()
            rd = ready[b]
            g = p.gather(gat[s][:, :], t["peer_" + kind], idxb[:, b, e:e + 1], mG[s], [fr, rd["idx"]])
            if kind == "u":
                first = [] if e else free.get(("hid", b % 2), [])
                d = p.vec(lambda en, g_=gat[s], x_=X[b % 2], o=hid[:, b % 2, e:e + 1]:
                          en.tensor_tensor_reduce(g_[:, :], g_[:, :], x_[:, :], 1.0, 0.0, ALU.mult, ALU.add, o),
                          D, [g, rd["X"], free.get(("hid", b % 2), [])])
                ringG.done(s, [d])
                dots.setdefault(b, []).append(d)
                if e % 16 == 15:
                    lo = e - 15
                    hsl, wsl = hid[:, b % 2, lo:e + 1], wgt[:, b % 2, lo:e + 1]
                    a = p.act(hsl, hsl, ACT.Gelu, [dots[b][lo:]])
                    a = p.tt(wsl, hsl, gate[:, b, lo:e + 1], ALU.mult, [a, rd["gate"], free.get(("wgt", b % 2), [])])
                    for k in range(lo, e + 1):
                        wsteps[(b, k)] = a
                if e == NE - 1:
                    free[f"X{b % 2}"] = dots[b]
                    free[("hid", b % 2)] = [a]
                    free[("gate", b)] = [a]
            else:
                wc = wgt[:, b % 2, e:e + 1]
                wst = wsteps[(b, e)]
                if e % 2 == 0:
                    if e == 0:
                        a = p.ts(acc[:, :], gat[s][:, :], wc, None, ALU.mult, None, [g, wst, free["acc"]])
                    else:
                        a = p.stt(acc[:, :], gat[s][:, :], wc, acc[:, :], ALU.mult, ALU.add, [g, wst, prev_acc])
                    prev_acc = a
                    ringG.done(s, [a])
                else:
                    k, dfr = ringV.take()
                    a = p.act(dgb[k][:, :], C["ident"], ACT.Identity, [wst, dfr], scale=wc)
                    m = []
                    for half in range(2):
                        m.append(p.mm(VB + half, ps[:, VB + half, :], dgb[k][:, :], gat[s][:, half * 512:half * 512 + 512], e == 1, e == NE - 1,
                                      [a, g, free["V"]]))
                    ringV.done(k, m)
                    ringG.done(s, m)
                    lastd = a
                    lastm = m
                if e == NE - 1:
                    free[("idx", b)] = [g]
                    free[("wgt", b % 2)] = [prev_acc, lastd]
                    pv = ps[:, VB:VB + 2, :].rearrange("p a b -> p (a b)")
                    x1 = p.tt(acc[:, :], pv, acc[:, :], ALU.add, [prev_acc, lastm])
                    x2 = p.tt(acc[:, :], acc[:, :], row[grow][:, :], ALU.mult, [x1, gready])
                    x3 = p.tt(h[:, b, :], h[:, b, :], acc[:, :], ALU.add, [x2, hw[b], hr[b]])
                    hw[b], hr[b] = [x3], []
                    free["acc"], free["V"] = [x3], [x1]
                    row_users[grow].append(x2)

    tA, atA = region(COMMON)
    lbv, oml, noml, lt0, lt1 = (tA(8) for _ in range(5))
    SA = tA(8, P)
    hset = [{k: tA(3, TM) if k == "sg" else tA(2, P) if k == "v" else tA(TM)
             for k in ("sg", "kk", "cum", "ecum", "kd", "dl", "qd", "v", "sq", "o1")} for _ in range(2)]
    kset = [{"KM": tA(8 * 144), "qP": tA(P), "sc": tA(P), "KT": tA(P), "pre": tA(16)} for _ in range(2)]
    ringH, ringK = Ring(2), Ring(2)
    stateA = {}

    def hgrn_setup():
        m = p.tt(lt0, V("lb0"), V("lb1"), ALU.max, [ld_v])
        a = p.tt(lbv, V("lb0"), lt0, ALU.subtract, [m])
        b = p.tt(lt1, V("lb1"), lt0, ALU.subtract, [m])
        a = p.act(lbv, lbv, ACT.Exp, [a])
        b = p.act(lt1, lt1, ACT.Exp, [b])
        s = p.tt(lt0, lbv, lt1, ALU.add, [a, b])
        s = p.vec(lambda e: e.reciprocal(lt0, lt0), 8, [s], 8.0)
        a = p.tt(lbv, lbv, lt0, ALU.mult, [s])
        b = p.tt(oml, lt1, lt0, ALU.mult, [s])
        c = p.ts(noml, oml, -1.0, None, ALU.mult, None, [b])
        lb_ready = [a, b, c]
        for k in kset:
            ringK.done(kset.index(k), [p.fill(k["KM"], 0.0), p.fill(k["sc"], 0.0), p.fill(k["pre"], 1.0)])
        return lb_ready

    def sigmoid_ps(dst, src, after):
        a = p.act(dst, src, ACT.Exp, after, scale=-1.0)
        b = p.act(dst, dst, ACT.Ln, [a], bias=one)
        return a, p.act(dst, dst, ACT.Exp, [b], scale=-1.0)

    def hgrn(chunk, hn_ready, lb_ready):
        T = P * len(chunk)
        nb = len(chunk)
        done = []
        for hh in range(NH):
            k, fr = ringH.take()
            q = hset[k]
            sg = q["sg"][:, :, 0:T]
            w = Weights("win", hh)
            i, last = project(w, 1, T, hn_ready)
            hn_users.append(last)
            a, sf = sigmoid_ps(sg[:, 1, :], ps[:, DB[i], 0:T], [last, fr, ld_c])
            bankD.done(i, [a])
            kk, cum, ecum, kd, dl, qd = (q[n][:, 0:T] for n in ("kk", "cum", "ecum", "kd", "dl", "qd"))
            k1 = p.ts(kk, sg[:, 1, :], noml[:, hh:hh + 1], oml[:, hh:hh + 1], ALU.mult, ALU.add, [sf, lb_ready, fr])
            lf = p.act(cum, sg[:, 1, :], ACT.Ln, [sf, lb_ready, fr], bias=lbv[:, hh:hh + 1], scale=oml[:, hh:hh + 1])
            cu = [p.vec(lambda e, o=cum[:, j * P:(j + 1) * P]:
                        e.tensor_tensor_scan(o, C["reset"], o, 0.0, ALU.mult, ALU.add), P, [lf, ld_c], 2.0)
                  for j in range(nb)]
            c16 = cum.rearrange("p (n c) -> p n c", c=16)
            d0 = p.tt(dl.rearrange("p (n c) -> p n c", c=16), bc(c16[:, :, 15:16], T // 16, 16), c16, ALU.subtract, [cu, fr])
            ec = p.act(ecum, cum, ACT.Exp, [cu, fr])
            en = p.act(kd, cum, ACT.Exp, [cu, fr], scale=-1.0)
            d1 = p.act(dl, dl, ACT.Exp, [d0])
            kd1 = p.tt(kd, kd, kk, ALU.mult, [en, k1])
            i, last = project(w, 0, T, hn_ready)
            hn_users.append(last)
            a, sq_ = sigmoid_ps(sg[:, 0, :], ps[:, DB[i], 0:T], [last, fr])
            a = p.tt(sg[:, 0, :], sg[:, 0, :], ps[:, DB[i], 0:T], ALU.mult, [sq_])
            bankD.done(i, [a])
            qd1 = p.tt(qd, sg[:, 0, :], ecum, ALU.mult, [a, ec, fr])
            i, bfr = bankD.take()
            for j in range(nb):
                for kc in range(KC):
                    last = p.mm(DB[i], ps[:, DB[i], j * P:(j + 1) * P], hn[:, kc, j * P:(j + 1) * P], w.at(kc, 3 * P, P),
                                kc == 0, kc == KC - 1, [hn_ready, w.load(kc), bfr])
                    w.use(kc, last)
            hn_users.append(last)
            vv = p.act(q["v"][:, 0:nb, :].rearrange("p a b -> p (a b)"), ps[:, DB[i], 0:T], ACT.Identity, [last, fr])
            bankD.done(i, [vv])
            i, last = project(w, 2, T, hn_ready)
            hn_users.append(last)
            a, sg_ = sigmoid_ps(sg[:, 2, :], ps[:, DB[i], 0:T], [last, fr])
            gs = p.tt(sg[:, 2, :], sg[:, 2, :], ps[:, DB[i], 0:T], ALU.mult, [sg_])
            bankD.done(i, [gs])
            w.done()
            o, ofr = bankO.take()
            po = ps[:, OB[o], 0:T]
            users = []
            for j, b in enumerate(chunk):
                x, kfr = ringK.take()
                z = kset[x]
                KM, qP, sc, KT, pre = z["KM"], z["qP"], z["sc"], z["KT"], z["pre"]
                sl = slice(j * P, (j + 1) * P)
                ed = ecum[:, sl].rearrange("p (n c) -> p n c", c=16)[:, :, 15]
                km = [p.tt(KM.rearrange("p (r c) -> p r c", c=144)[:, :, 0:16], dl[:, sl].rearrange("p (r c) -> p r c", c=16),
                           kk[:, sl].rearrange("p (r c) -> p r c", c=16), ALU.mult, [d1, k1, kfr])]
                for r in range(1, 8):
                    km.append(p.ts(KM[:, r * P:r * P + 16 * r], KM[:, (r - 1) * P:(r - 1) * P + 16 * r], ed[:, r:r + 1], None,
                                   ALU.mult, None, [km[-1], ec]))
                pr = p.vec(lambda e, o=pre[:, 1:9], d=ed: e.tensor_tensor_scan(o, d, C["ones"][:, 0:8], 1.0, ALU.mult, ALU.mult),
                           8, [ec, kfr], 2.0)
                qp = p.tt(qP.rearrange("p (n c) -> p n c", c=16), qd[:, sl].rearrange("p (n c) -> p n c", c=16),
                          bc(pre[:, 0:8].rearrange("p (n c) -> p n c", c=1), 8, 16), ALU.mult, [pr, qd1])
                i, xfr = bankX.take()
                B = XB[i]
                for r in range(1, 8):
                    m1 = p.mm(B, ps[:, B, 16 * r:16 * r + 16], KM[:, (r - 1) * P:r * P], qd[:, j * P + 16 * r:j * P + 16 * r + 16],
                              True, True, [km[r - 1], qd1, xfr])
                m2 = p.mm(B, ps[:, B, P:2 * P], kd[:, sl], qd[:, sl], True, True, [kd1, qd1, xfr])
                m3 = p.tr(B, ps[:, B, 2 * P:3 * P], KM[:, 7 * P:8 * P], C["ident"], [km[7], ld_c, xfr])
                s1 = p.act(sc[:, 16:P], ps[:, B, 16:P], ACT.Identity, [m1, m2, m3, kfr])
                s2 = p.act(KT, ps[:, B, 2 * P:3 * P], ACT.Identity, [m3, m2, m1, kfr])
                s3 = p.vec(lambda e, o=sc, m=C["mask16"].bitcast(U32), d=ps[:, B, P:2 * P]: e.copy_predicated(o, m, d),
                           P, [s1, s2, ld_c])
                o1 = p.mm(OB[o], po[:, sl], q["v"][:, j, :], sc, True, b == 0, [vv, s3, ofr])
                if b > 0:
                    o1 = p.mm(OB[o], po[:, sl], SA[:, hh, :], qP, False, True, [stateA[hh], qp])
                users += [o1, km[-1], qp]
                if b < NB - 1:
                    m4 = p.mm(B, ps[:, B, 3 * P:4 * P], KT, q["v"][:, j, :], True, True, [s2, s3, vv])
                    if b == 0:
                        st = p.cp(SA[:, hh, :], ps[:, B, 3 * P:4 * P], [m4])
                    else:
                        st = p.stt(SA[:, hh, :], SA[:, hh, :], pre[:, 8:9], ps[:, B, 3 * P:4 * P], ALU.mult, ALU.add, [m4, o1])
                    stateA[hh] = st
                    users.append(st)
                    bankX.done(i, [st])
                    ringK.done(x, [st, o1, m2, m3])
                else:
                    bankX.done(i, [s3])
                    ringK.done(x, [o1, m2, m3])
            sqv, o1v = q["sq"][:, 0:T], q["o1"][:, 0:T]
            a = p.act(sqv, po, ACT.Square, [o1, fr])
            i, xfr = bankX.take()
            m = p.mm(XB[i], ps[:, XB[i], 0:T], C["ones"], sqv, True, True, [a, xfr])
            b1 = p.act(sqv, ps[:, XB[i], 0:T], ACT.Ln, [m], bias=eps, scale=1.0 / P)
            bankX.done(i, [b1])
            b2 = p.act(sqv, sqv, ACT.Exp, [b1], scale=-0.5)
            b3 = p.stt(o1v, po, V("onorm", hh, 1), sg[:, 2, :], ALU.mult, ALU.mult, [gs, o1, a, fr])
            bankO.done(o, [b3])
            b4 = p.tt(oT[:, hh, 0:T], o1v, sqv, ALU.mult, [b2, b3, free["oT"]])
            ringH.done(k, [b4, users])
            done.append(b4)
        free["oT"] = None
        return done

    mod0 = [modvec(0, k) for k in range(6)]
    kvm_s = [matvec("kvada", 0, 0, kvm[:, :], V("kv_b"))]
    mod1 = [modvec(1, k) for k in range(6)]
    mv = [matvec("ada_2", 8 * k, 1, mod2[:, 8 * k:8 * k + 8], V("b_2", 8 * k, 8)) for k in range(3)]
    free["acc"] = crow_users[0]
    row_users[2] += crow_users[1]
    usersA, usersC, usersE = [], [], []
    at0 = len(p.steps)
    lb_ready = hgrn_setup()
    usersA += p.steps[at0:]
    for n, chunk in enumerate(CHUNKS_A):
        if n == 0:
            (sh, scl, g1, sh2, sc2, g2) = mod0
            g_a = gain(0, mod[0][:, 8:16], V("mix0"), scl)
        hn_again()
        hr1 = []
        for j, b in enumerate(chunk):
            a = normed(h[:, b, :], [hw[b]])
            hr[b].append(a)
            trs, evs = spread(a, j, [(hn, gT[:, 0, :], mod[0][:, 0:8], [g_a, sh, free["hn"]])])
            free["xs"] = trs
            hr1 += evs[0]
        at0 = len(p.steps)
        done = hgrn(chunk, hr1, lb_ready)
        usersA += p.steps[at0:]
        if n == 0:
            r1 = broadcast_row(0, mod[0][:, 16:24], g1)
        w2 = [Weights("wout", 0), Weights("wout", 1)]
        used = []
        for j, b in enumerate(chunk):
            used += add_mix(w2, b, j, oT, done, 0, r1)
        for w in w2:
            w.done()
        free["oT"] = used
        if n == 0:
            g_f = gain(1, mod[0][:, 32:40], V("ffn0"), sc2)
        hn_again()
        hr2 = []
        for j, b in enumerate(chunk):
            a = normed(h[:, b, :], [hw[b]])
            hr[b].append(a)
            trs, evs = spread(a, j, [(hn, gT[:, 1, :], mod[0][:, 24:32], [g_f, sh2, free["hn"]])])
            free["xs"] = trs
            hr2 += evs[0]
        select(0, chunk, hr2)
        keep_rows(chunk, hr2)
        if n == 0:
            r2 = broadcast_row(1, mod[0][:, 40:48], g2)
        if upto == "A":
            continue
        experts(0, chunk, 1, r2)

    tC, atC = region(COMMON)
    kT, vS, qT = tC(NH, S), tC(NB, D), tC(NH, TM)
    cset = [{k: tC(S) for k in ("e", "lk", "a")} for _ in range(2)]
    ringC = Ring(2)

    def attend(chunk, kv_done, q_done):
        done, used = [], []
        for j, b in enumerate(chunk):
            W = (b + 1) * P
            for hh in range(NH):
                c, fr = ringC.take()
                e, lk, a = (cset[c][k][:, 0:W] for k in ("e", "lk", "a"))
                i, bfr = bankD.take()
                B = DB[i]
                z = ps[:, B, 0:W]
                qh = qT[:, hh, j * P:(j + 1) * P]
                for n in range(b + 1):
                    m1 = p.mm(B, z[:, n * P:(n + 1) * P], kT[:, hh, n * P:(n + 1) * P], qh, n == 0, True,
                              [kv_done, q_done, bfr], True)
                a1 = p.act(e, z, ACT.Abs, [m1, fr])
                a2 = p.act(e, e, ACT.Exp, [a1], scale=-1.0)
                a3 = p.act(e, e, ACT.Ln, [a2], bias=one)
                d1 = p.stt(lk, z, 0.0, e, ALU.max, ALU.add, [a3, fr])
                d2 = p.tt(lk[:, b * P:W], lk[:, b * P:W], C["strict"], ALU.mult, [d1])
                for n in range(b + 1):
                    m2 = p.mm(B, z[:, n * P:(n + 1) * P], C["ntri"], lk[:, n * P:(n + 1) * P], False, True, [d2, d1], True)
                for n in range(1, b + 1):
                    m2 = p.mm(B, z[:, 0:n * P].rearrange("p (a b) -> p a b", b=P), C["nones"],
                              bc(lk[:, n * P:(n + 1) * P].rearrange("p (a b) -> p a b", a=1), n, P), False, True, [d2, d1], True)
                m2 = p.mm(B, z[:, b * P:W], C["ident"], C["negm"], False, True, [d1], True)
                a4 = p.act(a, z, ACT.Exp, [m2, fr])
                bankD.done(i, [a4])
                x, xfr = bankX.take()
                po = ps[:, XB[x], 0:P]
                for n in range(b + 1):
                    m3 = p.mm(XB[x], po, vS[:, n, hh * P:(hh + 1) * P], a[:, n * P:(n + 1) * P], n == 0, n == b, [a4, xfr])
                o = p.act(oT[:, hh, j * P:(j + 1) * P], po, ACT.Identity, [m3, free["oT"]])
                bankX.done(x, [o])
                ringC.done(c, [m3, m2])
                done.append(o)
                used.append(m1)
        return done, used

    gate_c = None
    if upto in "CDE":
        gate_c = p.fill(spot[:, :], 0.0, [usersA])
        g_kv = gain(2, kvm[:, 8:16], V("kv_g"), kvm_s)
        (sh, scl, g1, sh2, sc2, g2) = mod1
        g_a = gain(3, mod[1][:, 8:16], V("mix1"), scl)
    kv_done, qused = [], []
    for n, chunk in enumerate(CHUNKS_C if upto in "CDE" else []):
        T = P * len(chunk)
        t0 = chunk[0] * P
        at0 = len(p.steps)
        hn_again()
        rk, rq = [], []
        for j, b in enumerate(chunk):
            a = normed(h[:, b, :], [hw[b]])
            hr[b].append(a)
            trs, evs = spread(a, j, [(hn, gT[:, 2, :], kvm[:, 0:8], [g_kv, kvm_s, free["hn"]]),
                                     (oT, gT[:, 3, :], mod[1][:, 0:8], [g_a, sh, free["oT"]])])
            free["xs"] = trs
            rk += evs[0]
            rq += evs[1]
        for g in range(2):
            w = Weights("kvw", g)
            for m in range(4):
                i, last = project(w, m, T, rk)
                hn_users.append(last)
                e = p.act(kT[:, 4 * g + m, t0:t0 + T], ps[:, DB[i], 0:T], ACT.Identity, [last, gate_c])
                bankD.done(i, [e])
                kv_done.append(e)
            w.done()
        for g in range(2):
            w = Weights("kvw", 2 + g)
            for j, b in enumerate(chunk):
                i, fr = bankD.take()
                for kc in range(KC):
                    last = p.mm(DB[i], ps[:, DB[i], :], hn[:, kc, j * P:(j + 1) * P], w.at(kc, 0, 512), kc == 0, kc == KC - 1,
                                [rk, w.load(kc), fr])
                    w.use(kc, last)
                hn_users.append(last)
                e = p.act(vS[:, b, g * 512:g * 512 + 512], ps[:, DB[i], :], ACT.Identity, [last, gate_c])
                bankD.done(i, [e])
                kv_done.append(e)
            w.done()
        q_done, qin = [], []
        for g in range(2):
            w = Weights("sbq", g)
            for m in range(4):
                i, last = project(w, m, T, rq, oT)
                qin.append(last)
                e = p.act(qT[:, 4 * g + m, 0:T], ps[:, DB[i], 0:T], ACT.Identity, [last, gate_c, qused], scale=float(P) ** -0.5)
                bankD.done(i, [e])
                q_done.append(e)
            w.done()
        free["oT"] = qin
        done, qused = attend(chunk, kv_done, q_done)
        free["oT"] = None
        if n == 0:
            r1 = broadcast_row(0, mod[1][:, 16:24], g1)
        w2 = [Weights("sbo", 0), Weights("sbo", 1)]
        used = []
        for j, b in enumerate(chunk):
            used += add_mix(w2, b, j, oT, done, 0, r1)
        for w in w2:
            w.done()
        free["oT"] = used
        if n == 0:
            g_f = gain(4, mod[1][:, 32:40], V("ffn1"), sc2)
        hn_again()
        hr2 = []
        for j, b in enumerate(chunk):
            a = normed(h[:, b, :], [hw[b]])
            hr[b].append(a)
            trs, evs = spread(a, j, [(hn, gT[:, 4, :], mod[1][:, 24:32], [g_f, sh2, free["hn"]])])
            free["xs"] = trs
            hr2 += evs[0]
        select(1, chunk, hr2)
        keep_rows(chunk, hr2)
        if n == 0:
            r2 = broadcast_row(2, mod[1][:, 40:48], g2)
        usersC += p.steps[at0:]
        if upto == "C":
            continue
        experts(1, chunk, 2, r2)

    tE, atE = region(0)
    cste = tE(cc["tri64"] * len(CONSTS_E))
    CE = {k: cste[:, n * P:(n + 1) * P] for n, k in enumerate(CONSTS_E)}
    SG = tE(4, P)
    carry = tE(12, 3)
    ckvT, ckvR, ikT, toep = tE(S), tE(NB, P), tE(S), tE(4, 256)
    cin, sgE = tE(3, TM + 3), tE(3, TM)
    Q2, K2, V2 = tE(4, TM), tE(4, TM), tE(4, TM)
    MA = [tE(4, P) for _ in range(9)]
    iqT, qbT = tE(4, TM), tE(4, TM)
    score, Wk, lg0, pT = tE(S), tE(S), tE(S), tE(S)
    lg1 = tE(S)
    sm = tE(96)
    ob = cst[:, cc["ident"] + cc["ones"] + cc["cols"] + cc["strict"] + 512:][:, 0:P]
    abr, nea = sm[:, 0:8], sm[:, 8:12]
    bawb = [sm[:, 80:96], sm[:, 16:32]]
    sc4 = [sm[:, 32 + 4 * k:36 + 4 * k] for k in range(8)]
    glc = sm[:, 64:72].rearrange("p (a b) -> p a b", a=4)
    m8 = sm[:, 72:80]
    at = cc["ident"] + cc["ones"] + cc["cols"] + cc["strict"]
    wuv = cst[:, at:at + 512].rearrange("p (a b) -> p a b", a=4)

    def b4(ap):
        return bc(ap.rearrange("p (a b) -> p a b", a=1), 4, P)

    def b4c(ap):
        return bc(ap.rearrange("p (a b) -> p a b", b=1), 4, P)

    def gated_heads(chunk, rh):
        T = P * len(chunk)
        out_ = []
        for hh in range(4):
            w = Weights("win2", hh)
            ins, rd = [], []
            for ty in range(3):
                i, last = project(w, ty, T, rh)
                hn_users.append(last)
                ins.append(p.act(cin[:, ty, 3:3 + T], ps[:, DB[i], 0:T], ACT.Identity, [last, E["cin"], gate_e]))
                bankD.done(i, [ins[-1]])
            cr = p.cp(cin[:, :, 0:3], carry[:, 3 * hh:3 * hh + 3, :], [E["carry"], E["cin"]])
            rel = []
            cw = [V("conv", 12 * tap, 12) for tap in range(4)]
            for ty, dst in enumerate((Q2, K2, V2)):
                tile_ = 4 * ty + hh
                d = dst[:, hh, 0:T]
                a = p.ts(d, cin[:, ty, 0:T], cw[0][:, tile_:tile_ + 1], None, ALU.mult, None, [ins[ty], cr, E["QKV"]])
                for tap in range(1, 4):
                    a = p.stt(d, cin[:, ty, tap:tap + T], cw[tap][:, tile_:tile_ + 1], d, ALU.mult, ALU.add, [a])
                rel.append(a)
            ca = p.cp(carry[:, 3 * hh:3 * hh + 3, :], cin[:, :, T:T + 3], [ins, cr])
            E["cin"], E["carry"] = rel + [ca], [ca]
            sgs = []
            for ty, dst in enumerate((Q2, K2, V2)):
                s_ = sgE[:, ty, 0:T]
                _, a = sigmoid_ps(s_, dst[:, hh, 0:T], [rel[ty], E["sgE"]])
                sgs.append(p.tt(dst[:, hh, 0:T], dst[:, hh, 0:T], s_, ALU.mult, [a]))
            sq = [p.act(sgE[:, ty, 0:T], dst[:, hh, 0:T], ACT.Square, [sgs[ty]]) for ty, dst in enumerate((Q2, K2))]
            i, fr = bankD.take()
            B = DB[i]
            mq = p.mm(B, ps[:, B, 0:T], C["ones"], sgE[:, 0, 0:T], True, True, [sq[0], fr])
            mk = p.mm(B, ps[:, B, TM:TM + T], C["ones"], sgE[:, 1, 0:T], True, True, [sq[1], fr])
            lq = p.act(sgE[:, 0, 0:T], ps[:, B, 0:T], ACT.Ln, [mq, mk], bias=eps)
            lk = p.act(sgE[:, 1, 0:T], ps[:, B, TM:TM + T], ACT.Ln, [mk], bias=eps)
            bankD.done(i, [lq, lk])
            lq = p.act(sgE[:, 0, 0:T], sgE[:, 0, 0:T], ACT.Exp, [lq], bias=nhl, scale=-0.5)
            lk = p.act(sgE[:, 1, 0:T], sgE[:, 1, 0:T], ACT.Exp, [lk], scale=-0.5)
            aq = p.tt(Q2[:, hh, 0:T], Q2[:, hh, 0:T], sgE[:, 0, 0:T], ALU.mult, [lq])
            ak = p.tt(K2[:, hh, 0:T], K2[:, hh, 0:T], sgE[:, 1, 0:T], ALU.mult, [lk])
            E["sgE"] = [aq, ak, sgs[2]]
            out_ += [aq, ak, sgs[2]]
            i, last = project(w, 3, T, rh)
            hn_users.append(last)
            _, a = sigmoid_ps(oT[:, hh, 0:T], ps[:, DB[i], 0:T], [last, free["oT"]])
            a = p.tt(oT[:, hh, 0:T], oT[:, hh, 0:T], ps[:, DB[i], 0:T], ALU.mult, [a])
            bankD.done(i, [a])
            out_.append(a)
            w.done()
        return out_

    def gated_block(b, j, heads, bw):
        sl = slice(j * P, (j + 1) * P)
        A0, A1, A2, A3, A4, A5, A6, A7, A8 = MA
        beta, gg, eg, el, be, x0, x1, gcl = sc4
        fr = E["blk"]
        baw = bawb[j]

        def four(mms, after):
            i, bfr = bankD.take()
            for q in range(4):
                o_, l_, r_ = mms(q, ps[:, DB[i], q * P:(q + 1) * P])
                last = p.mm(DB[i], o_, l_, r_, True, True, [after, bfr])
            return i, ps[:, DB[i], :].rearrange("p (a b) -> p a b", a=4), last

        a = p.act(beta, baw[:, 0:4], ACT.Exp, [bw, fr], scale=-1.0)
        a = p.ts(beta, beta, 1.0, None, ALU.add, None, [a])
        beta_ok = p.vec(lambda e: e.reciprocal(beta, beta), 4, [a], 8.0)
        a = p.tt(x0, baw[:, 4:8], abr[:, 4:8], ALU.add, [bw, abr_ok, fr])
        c = p.act(x1, x0, ACT.Abs, [a])
        c = p.act(x1, x1, ACT.Exp, [c], scale=-1.0)
        c = p.act(x1, x1, ACT.Ln, [c], bias=one)
        c = p.stt(x1, x0, 0.0, x1, ALU.max, ALU.add, [c])
        g_ok = p.tt(gg, x1, nea, ALU.mult, [c, nea_ok])
        i, bfr = bankD.take()
        B = DB[i]
        m = p.mm(B, ps[:, B, 0:4], CE["tri64"], gg, True, True, [g_ok, cste_ok, bfr])
        m = p.mm(B, ps[:, B, 4:8], CE["sup64"], gg, True, True, [g_ok])
        gc_ok = p.cp(gcl, ps[:, B, 0:4], [m])
        e1_ = p.act(eg, ps[:, B, 0:4], ACT.Exp, [gc_ok])
        e2_ = p.act(el, ps[:, B, 4:8], ACT.Exp, [gc_ok])
        bankD.done(i, [gc_ok, e1_, e2_])
        be_ok = p.tt(be, beta, eg, ALU.mult, [e1_, beta_ok])
        a = p.tt(A2, b4(CE["tri64"]), b4c(gg), ALU.mult, [g_ok, cste_ok, fr])
        i, bfr = bankD.take()
        PR = ps[:, DB[i], :].rearrange("p (a b) -> p a b", a=4)
        m = p.mm(DB[i], ps[:, DB[i], :], C["ones"], A2.rearrange("p a b -> p (a b)"), True, True, [a, bfr])
        eg_ok = p.act(A6, PR, ACT.Exp, [m, fr])
        a = p.tt(A0, PR, b4c(gcl), ALU.subtract, [m, eg_ok, gc_ok, fr])
        bankD.done(i, [a, eg_ok])
        a = p.ts(A0, A0, 0.0, None, ALU.min, None, [a])
        a = p.act(A0, A0, ACT.Exp, [a])
        dec = p.tt(A0, A0, b4(CE["tri64"]), ALU.mult, [a])
        a = p.tt(A1, b4(C["ident"]), b4c(beta), ALU.mult, [beta_ok, fr])
        i, bfr = bankD.take()
        PBt = ps[:, DB[i], :].rearrange("p (a b) -> p a b", a=4)
        mb = p.mm(DB[i], ps[:, DB[i], :], C["ones"], A1.rearrange("p a b -> p (a b)"), True, True, [a, bfr])
        ib = i
        i, pk, m = four(lambda q, o: (o, K2[:, q, sl], K2[:, q, sl]), [heads])
        a = p.tt(A1, pk, A0, ALU.mult, [m, dec, mb])
        bankD.done(i, [a])
        a = p.tt(A1, A1, b4(CE["str64"]), ALU.mult, [a])
        lt = p.tt(A1, A1, PBt, ALU.mult, [a, mb])
        bankD.done(ib, [lt])
        i, bfr = bankD.take()
        for q in range(4):
            m = p.tr(DB[i], ps[:, DB[i], q * P:(q + 1) * P], A1[:, q, :], C["ident"], [lt, bfr])
        ll = p.act(A2, ps[:, DB[i], :].rearrange("p (a b) -> p a b", a=4), ACT.Identity, [m])
        bankD.done(i, [ll])
        i, pq, m = four(lambda q, o: (o, K2[:, q, sl], Q2[:, q, sl]), [heads])
        at_ok = p.tt(A5, pq, A0, ALU.mult, [m, dec, fr])
        bankD.done(i, [at_ok])
        qg_ok = p.tt(Q2[:, :, sl], Q2[:, :, sl], A6, ALU.mult, [m, eg_ok])
        gl_ok = p.cp(glc, A6.rearrange("p a (c t) -> p a c t", t=64)[:, :, :, 63], [eg_ok, fr])
        a = p.tt(A3, A2, b4(CE["m1"]), ALU.mult, [ll, fr])
        x_ok = p.tt(A3, b4(C["ident"]), A3, ALU.subtract, [a])
        a = p.tt(A4, A1, b4(CE["m1t"]), ALU.mult, [lt, fr])
        n_ok = p.tt(A4, b4(C["ident"]), A4, ALU.subtract, [a])
        y_free = [at_ok, a]
        for lev in (2, 4, 8, 16, 32):
            i, py, m = four(lambda q, o: (o, A1[:, q, :], A3[:, q, :]), [x_ok])
            y = p.tt(A0, py, b4(CE[f"m{lev}"]), ALU.mult, [m, y_free])
            bankD.done(i, [y])
            mx = None
            if lev < 32:
                i2, px, mx = four(lambda q, o: (o, A4[:, q, :], A0[:, q, :]), [y, n_ok])
            i3, pn, mn = four(lambda q, o: (o, A0[:, q, :], A4[:, q, :]), [y, n_ok])
            if lev < 32:
                x_ok = p.tt(A3, A3, px, ALU.subtract, [mx, m])
                bankD.done(i2, [x_ok])
            n_ok = p.tt(A4, A4, pn, ALU.subtract, [mn, mx])
            bankD.done(i3, [n_ok])
            y_free = [mn, mx]
        i, bfr = bankD.take()
        for q in range(4):
            m = p.tr(DB[i], ps[:, DB[i], q * P:(q + 1) * P], K2[:, q, sl], C["ident"], [heads, bfr])
        pk = ps[:, DB[i], :].rearrange("p (a b) -> p a b", a=4)
        kb_ok = p.tt(A6, pk, b4c(be), ALU.mult, [m, be_ok, gl_ok, qg_ok])
        kg_ok = p.tt(A7, pk, b4c(el), ALU.mult, [m, e2_, fr])
        bankD.done(i, [kb_ok, kg_ok])
        i, bfr = bankD.take()
        for q in range(4):
            m = p.tr(DB[i], ps[:, DB[i], q * P:(q + 1) * P], V2[:, q, sl], C["ident"], [heads, bfr])
        vb_ok = p.tt(A8, ps[:, DB[i], :].rearrange("p (a b) -> p a b", a=4), b4c(beta), ALU.mult, [m, beta_ok, fr])
        bankD.done(i, [vb_ok])
        i, pw, m = four(lambda q, o: (o, A6[:, q, :], A4[:, q, :]), [kb_ok, n_ok])
        w_ok = p.act(A2, pw, ACT.Identity, [m, x_ok], scale=-1.0)
        bankD.done(i, [w_ok])
        o, ofr = bankO.take()
        PO = ps[:, OB[o], :].rearrange("p (a b) -> p a b", a=4)
        for c in range(2):
            r = slice(64 * c, 64 * c + 64)
            qsl = slice(j * P + 64 * c, j * P + 64 * c + 64)
            first = b == 0 and c == 0
            i, bfr = bankD.take()
            B = DB[i]
            for q in range(4):
                m = p.mm(B, ps[r, B, q * P:(q + 1) * P], A4[:, q, r], A8[:, q, :], True, first, [vb_ok, n_ok, bfr])
                if not first:
                    m = p.mm(B, ps[r, B, q * P:(q + 1) * P], A2[:, q, r], SG[:, q, :], False, True, [w_ok, E["S"]])
            vn = p.act(A3[r, :, :], ps[r, B, :].rearrange("p (a b) -> p a b", a=4), ACT.Identity, [m, x_ok])
            bankD.done(i, [vn])
            for q in range(4):
                m = p.mm(OB[o], PO[:, q, r], A3[r, q, :], A5[r, q, r], True, first, [vn, at_ok, ofr])
                if not first:
                    m = p.mm(OB[o], PO[:, q, r], SG[:, q, :], Q2[:, q, qsl], False, True, [qg_ok, E["S"]])
            mo = m
            if b == NB - 1 and c == 1:
                break
            i, bfr = bankD.take()
            B = DB[i]
            new = []
            for q in range(4):
                m = p.mm(B, ps[:, B, q * P:(q + 1) * P], A7[r, q, :], A3[r, q, :], True, True, [kg_ok, vn, bfr])
            for q in range(4):
                if first:
                    new.append(p.cp(SG[:, q, :], ps[:, B, q * P:(q + 1) * P], [m, gate_e]))
                else:
                    new.append(p.stt(SG[:, q, :], SG[:, q, :], glc[:, q, c:c + 1], ps[:, B, q * P:(q + 1) * P],
                                     ALU.mult, ALU.add, [m, mo, gl_ok]))
            bankD.done(i, new)
            E["S"] = new
        a = p.act(A0, PO, ACT.Square, [mo, y_free])
        i, bfr = bankD.take()
        m = p.mm(DB[i], ps[:, DB[i], :], C["ones"], A0.rearrange("p a b -> p (a b)"), True, True, [a, bfr])
        c = p.act(A0, ps[:, DB[i], :].rearrange("p (a b) -> p a b", a=4), ACT.Ln, [m], bias=eps, scale=1.0 / P)
        bankD.done(i, [c])
        c = p.act(A0, A0, ACT.Exp, [c], scale=-0.5)
        d = p.stt(A0, PO, V("gdn"), A0, ALU.mult, ALU.mult, [c, mo])
        bankO.done(o, [d])
        d = p.tt(oT[:, 0:4, sl], oT[:, 0:4, sl], A0, ALU.mult, [d, heads])
        E["blk"] = [d, mo, E["S"]]
        return [d], [mo, m, qg_ok]

    def sparse_prep(chunk, rh):
        T = P * len(chunk)
        t0 = chunk[0] * P
        out_ = []
        w = Weights("win2", 7)
        i, last = project(w, 0, T, rh)
        hn_users.append(last)
        a = p.act(pT[:, 0:T], ps[:, DB[i], 0:T], ACT.Square, [last, E["pT"], gate_e])
        x, xfr = bankX.take()
        m = p.mm(XB[x], ps[:, XB[x], 0:T], C["ones"], pT[:, 0:T], True, True, [a, xfr])
        c = p.act(pT[:, 0:T], ps[:, XB[x], 0:T], ACT.Ln, [m], bias=eps, scale=1.0 / P)
        bankX.done(x, [c])
        c = p.act(pT[:, 0:T], pT[:, 0:T], ACT.Exp, [c], scale=-0.5)
        kt = p.stt(ckvT[:, t0:t0 + T], ps[:, DB[i], 0:T], V("gkv"), pT[:, 0:T], ALU.mult, ALU.mult, [c, last, a, gate_e])
        bankD.done(i, [kt])
        E["pT"] = [kt]
        out_.append(kt)
        x, xfr = bankX.take()
        for j, b in enumerate(chunk):
            m = p.tr(XB[x], ps[:, XB[x], j * P:(j + 1) * P], ckvT[:, b * P:(b + 1) * P], C["ident"], [kt, xfr])
        c = p.act(ckvR[:, chunk[0]:chunk[-1] + 1, :], ps[:, XB[x], 0:T].rearrange("p (a b) -> p a b", b=P), ACT.Identity,
                  [m, gate_e])
        bankX.done(x, [c])
        out_.append(c)
        i, last = project(w, 1, T, rh)
        hn_users.append(last)
        c = p.act(ikT[:, t0:t0 + T], ps[:, DB[i], 0:T], ACT.Identity, [last, gate_e])
        bankD.done(i, [c])
        out_.append(c)
        bws = []
        for j, b in enumerate(chunk):
            i, bfr = bankD.take()
            for kc in range(KC):
                last = p.mm(DB[i], ps[:, DB[i], 0:16], hn[:, kc, j * P:(j + 1) * P], w.at(kc, 2 * P, 16), kc == 0, kc == KC - 1,
                            [rh, w.load(kc), bfr])
                w.use(kc, last)
            hn_users.append(last)
            c1 = p.act(bawb[j][:, 0:8], ps[:, DB[i], 0:8], ACT.Identity, [last, E["baw"]])
            c2 = p.act(bawb[j][:, 8:16], ps[:, DB[i], 8:16], ACT.Identity, [last, E["baw"]], scale=8 ** -0.5 * 64 ** -0.5)
            bankD.done(i, [c1, c2])
            bws.append([c1, c2])
        w.done()
        w = Weights("win2", 6)
        for m in range(4):
            i, last = project(w, m, T, rh)
            hn_users.append(last)
            c = p.act(iqT[:, m, 0:T], ps[:, DB[i], 0:T], ACT.Identity, [last, gate_e, E["iq"]])
            bankD.done(i, [c])
            out_.append(c)
        w.done()
        w = Weights("win2", 4)
        for m in range(4):
            i, last = project(w, m, T, rh)
            hn_users.append(last)
            c = p.act(qbT[:, m, 0:T], ps[:, DB[i], 0:T], ACT.Identity, [last, gate_e, E["qb"]])
            bankD.done(i, [c])
            out_.append(c)
        w.done()
        w = Weights("win2", 5)
        for m in range(4):
            i, last = project(w, m, T, rh)
            hn_users.append(last)
            _, a = sigmoid_ps(oT[:, 4 + m, 0:T], ps[:, DB[i], 0:T], [last, free["oT"]])
            a = p.tt(oT[:, 4 + m, 0:T], oT[:, 4 + m, 0:T], ps[:, DB[i], 0:T], ALU.mult, [a])
            bankD.done(i, [a])
            out_.append(a)
        w.done()
        return out_, bws

    def sparse_block(b, j, prep, bw):
        W = (b + 1) * P
        sl = slice(j * P, (j + 1) * P)
        lgs = (lg0, lg1)
        if b == 0:
            m_ok = p.ts(Wk[:, 0:P], C["strict"], -BIG, None, ALU.mult, None, [cste_ok, E["Wk"]])
        else:
            iwv = bawb[j][:, 8:16]
            prev = E["score"]
            iqs = []
            for hh in range(8):
                x, xfr = bankX.take()
                half = slice(64 * (hh % 2), 64 * (hh % 2) + 64)
                m = p.mm(XB[x], ps[:, XB[x], 0:W], iqT[half, hh // 2, sl], ikT[half, 0:W], True, True, [prep, xfr])
                iqs.append(m)
                lb = lgs[hh % 2][:, 0:W]
                r = p.act(lb, ps[:, XB[x], 0:W], ACT.Relu, [m, E["lg"][hh % 2]])
                bankX.done(x, [r])
                if hh == 0:
                    s_ = p.ts(score[:, 0:W], lb, iwv[:, 0:1], None, ALU.mult, None, [r, bw, prev])
                else:
                    s_ = p.stt(score[:, 0:W], lb, iwv[:, hh:hh + 1], score[:, 0:W], ALU.mult, ALU.add, [r, s_])
                E["lg"][hh % 2] = [s_]
            E["iq"] = iqs
            dg = slice(b * P, W)
            a = p.stt(score[:, dg], C["strict"], -BIG, score[:, dg], ALU.mult, ALU.add, [s_, ld_c])
            src = score[:, 0:W]
            for rnd in range(16):
                a = p.vec(lambda e, s=src: e.max(m8, s), W, [a, E["Wk"] if rnd == 0 else None])
                a = p.vec(lambda e, s=src: e.match_replace(Wk[:, 0:W], m8, s, -3.3e38), W, [a, E["Wk"] if rnd == 0 else None])
                src = Wk[:, 0:W]
            E["score"] = [a]
            m_ok = p.ts(Wk[:, 0:W], Wk[:, 0:W], -3.15e38, -BIG, ALU.is_ge, ALU.mult, [a])
        near = min(W, 256)
        rd = []
        res, qbs = [], []
        for hh in range(4):
            x, xfr = bankX.take()
            m = p.mm(XB[x], ps[:, XB[x], 0:W], qbT[:, hh, sl], ckvT[:, 0:W], True, True, [prep, xfr])
            qbs.append(m)
            lgt = lgs[hh % 2]
            lb = lgt[:, 0:W]
            a = p.stt(lb, ps[:, XB[x], 0:W], float(P) ** -0.5, Wk[:, 0:W], ALU.mult, ALU.add, [m, m_ok, E["lg"][hh % 2]])
            rd.append(a)
            bankX.done(x, [a])
            a1 = p.tt(lgt[:, W - near:W], lgt[:, W - near:W], toep[:, hh, 256 - near:256], ALU.add, [a, toep_ok])
            a2 = None
            if W > near:
                a2 = p.ts(lgt[:, 0:W - near], lgt[:, 0:W - near], toep[:, hh, 0:1], None, ALU.add, None, [a, toep_ok])
            s, sfr = ringS.take()
            mx, sm_ = small[:, s, 0:1], small[:, s, 1:2]
            a = p.vec(lambda e, o=mx, i_=lb: e.tensor_reduce(o, i_, AX, ALU.max, negate=True), W, [a1, a2, sfr])
            a = p.act(lb, lb, ACT.Exp, [a], bias=mx, accum=sm_)
            c = p.vec(lambda e, o=sm_: e.reciprocal(o, o), 1, [a], 8.0)
            a = p.ts(lb, lb, sm_, None, ALU.mult, None, [a, c])
            ringS.done(s, [a])
            x, xfr = bankX.take()
            for n in range(b + 1):
                m = p.tr(XB[x], ps[:, XB[x], n * P:(n + 1) * P], lgt[:, n * P:(n + 1) * P], C["ident"], [a, xfr])
            E["lg"][hh % 2] = [m]
            c = p.act(pT[:, 0:W], ps[:, XB[x], 0:W], ACT.Identity, [m, E["pT"]])
            bankX.done(x, [c])
            x, xfr = bankX.take()
            B = XB[x]
            for n in range(b + 1):
                m = p.mm(B, ps[:, B, 0:P], ckvR[:, n, :], pT[:, n * P:(n + 1) * P], n == 0, n == b, [c, prep, xfr])
            c = p.act(ob, ps[:, B, 0:P], ACT.Identity, [m, E["ob"]])
            E["pT"] = [m]
            m = p.mm(B, ps[:, B, P:2 * P], wuv[:, hh, :], ob, True, True, [c, wuv_ok])
            E["ob"] = [m]
            c = p.tt(oT[:, 4 + hh, sl], oT[:, 4 + hh, sl], ps[:, B, P:2 * P], ALU.mult, [m, prep])
            bankX.done(x, [c])
            res.append(c)
        E["Wk"] = rd
        E["qb"] = qbs
        return res

    def finish(b, j, w2, after):
        s, sfr = ringS.take()
        c = [small[:, s, k:k + 1] for k in range(3)]
        banks, lasts, sqs = [], [], []
        for n in range(2):
            i, fr = bankD.take()
            for kc in range(KC):
                last = p.mm(DB[i], ps[:, DB[i], :], oT[:, kc, j * P:(j + 1) * P], w2[n].at(kc, 0, 512), kc == 0, kc == KC - 1,
                            [after, w2[n].load(kc), fr])
                w2[n].use(kc, last)
            banks.append(i)
            lasts.append(last)
            sqs.append(p.act(xs[:, n * 512:n * 512 + 512], ps[:, DB[i], :], ACT.Square, [last, sfr, free["xs"]], accum=c[n]))
        a = p.tt(c[2], c[0], c[1], ALU.add, sqs)
        a = p.act(c[2], c[2], ACT.Ln, [a], bias=eps, scale=1.0 / D)
        a = p.act(c[2], c[2], ACT.Exp, [a], scale=-0.5)
        new = []
        for n in range(2):
            half = slice(n * 512, n * 512 + 512)
            d = p.stt(xs[:, half], ps[:, DB[banks[n]], :], c[2], row[1][:, half], ALU.mult, ALU.mult, [a, sqs, rp])
            bankD.done(banks[n], [d])
            new.append(p.tt(h[:, b, half], h[:, b, half], xs[:, half], ALU.add, [d, hw[b], hr[b]]))
        ringS.done(s, new)
        free["xs"] = new
        hw[b], hr[b] = new, []
        return lasts

    E = {k: [] for k in ("cin", "carry", "QKV", "sgE", "blk", "S", "pT", "baw", "iq", "qb", "score", "Wk", "ob")}
    E["lg"] = [[], []]
    if upto == "E":
        gate_e = p.fill(spot[:, :], 0.0, [usersC, gate_c])
        me = [mark(f"m_e{k}") for k in range(7)]
        cste_ok = p.dma("sp", cste, t["cste"], me[0], P * cste.shape[1] * 4, [gate_e])
        wuv_ok = p.dma("sp", wuv, t["wuv"], me[1], P * 512 * 4, [gate_e])
        ab = t["ab"]
        ab_ok = p.dma("sp", abr, bass.AP(ab.tensor, ab.offset, [[0, P], [1, 8]]), me[2], P * 32, [gate_e])
        a = p.act(nea, abr[:, 0:4], ACT.Exp, [ab_ok])
        nea_ok = p.ts(nea, nea, -1.0, None, ALU.mult, None, [a])
        abr_ok = ab_ok
        E["carry"] = [p.fill(carry, 0.0, [gate_e])]
        hot_ok = p.dma("sp", Wk[0:32, 0:384], t["hot"], me[3], 32 * 384 * 4, [gate_e])
        rel_ok = p.dma("sp", score[0:32, 0:4], t["rel"], me[4], 32 * 16, [gate_e])
        x, xfr = bankX.take()
        m = p.mm(XB[x], ps[0:4, XB[x], 0:384], score[0:32, 0:4], Wk[0:32, 0:384], True, True, [hot_ok, rel_ok, xfr])
        c = p.cp(pT[0:4, 0:384], ps[0:4, XB[x], 0:384], [m, gate_e])
        bankX.done(x, [c])
        scr = nc.dram_tensor("bias_rows", (4, 384), F32).ap()
        scr_ok = p.dma("sp", scr, pT[0:4, 0:384], me[5], 4 * 384 * 4, [c])
        back = p.dma("sp", qbT.rearrange("p a b -> p (a b)").rearrange("p (a b) -> p a b", a=4),
                     bass.AP(scr.tensor, 0, [[1, P], [384, 4], [1, 256]]), me[6], P * 4096, [scr_ok, gate_e])
        flip_ok = p.dma("sp", lg0[:, 0:P], t["flip"], mark("m_e7"), P * P * 4, [gate_e])
        toep_ok, ms = [], []
        for half in range(2):
            x, xfr = bankX.take()
            mf = p.mm(XB[x], ps[:, XB[x], :], lg0[:, 0:P], qbT.rearrange("p a b -> p (a b)")[:, half * 512:half * 512 + 512],
                      True, True, [back, flip_ok, xfr])
            c2 = p.act(toep[:, 2 * half:2 * half + 2, :].rearrange("p a b -> p (a b)"), ps[:, XB[x], :], ACT.Identity, [mf])
            bankX.done(x, [c2])
            toep_ok.append(c2)
            ms.append(mf)
        E["qb"], E["lg"][0] = ms, ms
        E["pT"], E["Wk"], E["score"] = [scr_ok], [m], [m]
        g_p = gain(5, mod2[:, 8:16], V("pre"), mv[1])
        gp = p.tt(mod2[:, 16:24], mod2[:, 16:24], V("post"), ALU.mult, [mv[2]])
        rf = broadcast_row(0, V("fin"), ld_v)
        rp = broadcast_row(1, mod2[:, 16:24], gp)
        for chunk in CHUNKS_E:
            hn_again()
            rh = []
            for j, b in enumerate(chunk):
                a, c, s = rms(h[:, b, :], xs[:, :], D, [hw[b], free["xs"]])
                a = p.stt(h[:, b, :], h[:, b, :], c, row[0][:, :], ALU.mult, ALU.mult, [a, rf, hw[b], hr[b]])
                ringS.done(s, [a])
                hw[b], hr[b], free["xs"] = [a], [], [a]
                a = normed(h[:, b, :], [hw[b]])
                hr[b].append(a)
                trs, evs = spread(a, j, [(hn, gT[:, 5, :], mod2[:, 0:8], [g_p, mv[0], free["hn"]])])
                free["xs"] = trs
                rh += evs[0]
            prep, bws = sparse_prep(chunk, rh)
            heads = gated_heads(chunk, rh)
            free["oT"] = None
            mixed = []
            bwu, qkvu = [], []
            for j, b in enumerate(chunk):
                mixed += sparse_block(b, j, prep, bws[j])
                bwu.append(E["score"])
            for j, b in enumerate(chunk):
                r, u = gated_block(b, j, heads, bws[j])
                mixed += r
                qkvu += u
                bwu.append(E["blk"])
            E["baw"], E["QKV"] = bwu, qkvu
            w2 = [Weights("wout2", 0), Weights("wout2", 1)]
            used = []
            for j, b in enumerate(chunk):
                used += finish(b, j, w2, mixed)
            for w in w2:
                w.done()
            free["oT"] = used

    m_o = [mark(f"m_o{b}") for b in range(NB)]
    last = []
    for b in range(NB):
        last.append(p.dma("sp", out[b * P:(b + 1) * P, :], h[:, b, :], m_o[b], P * D * 4, [hw[b]]))
    p.emit(nc, sems, last)
    ctx.close()
    return p


def tiles(w):
    k, n = w.shape
    g = -(-n // 512)
    if n % 512:
        w = np.concatenate([w, np.zeros((k, g * 512 - n), w.dtype)], axis=1)
    return np.ascontiguousarray(w.reshape(4, 2, P, g, 512).transpose(3, 0, 2, 1, 4))


def columns(v):
    return v.reshape(-1, P).T


def layout(i):
    i = {k: np.asarray(v) for k, v in i.items()}
    o = {"x": i["x"][0]}
    for l in range(2):
        o[f"ada{l}"] = i["ada_w"][l].T.reshape(-1, P, D)
        o[f"pq{l}"] = tiles(i["peer_w_q"][l])
        o[f"sub{l}"] = np.ascontiguousarray(i["peer_subkeys"][l].reshape(8, P, P).transpose(2, 0, 1).reshape(P, 2, 512))
    w = i["hgrn_w_in"][0].reshape(D, 4, NH, P)
    o["win"] = tiles(np.stack([w[:, 0], w[:, 1], w[:, 3], w[:, 2]], axis=2).reshape(D, 4 * D))
    o["wout"] = tiles(i["hgrn_w_out"][0])
    o["kvada"] = i["kv_ada_w"].T.reshape(-1, P, D)
    o["cc"] = np.concatenate([i["c"], i["c_2"]], axis=0)
    o["kvw"] = tiles(i["kv_w"])
    o["sbq"] = tiles(i["sb_w_q"][0])
    o["sbo"] = tiles(i["sb_w_out"][0])
    o["peer_u"] = i["peer_u"].reshape(-1, D)
    o["peer_v"] = i["peer_v"].reshape(-1, D)
    o["ada_2"] = i["w_ada_2"][0].T.reshape(-1, P, D)
    w = i["w_in_2"][0]
    qkv = w[:, 0:1536].reshape(D, 3, 4, P)
    z = w[:, 1536:2048].reshape(D, 1, 4, P)
    ba, qb, ckv, zb = w[:, 2048:2056], w[:, 2056:2568], w[:, 2568:2696], w[:, 2696:3208]
    iq, ik, iw = w[:, 3208:3720], w[:, 3720:3784], w[:, 3784:3792]
    heads = np.concatenate([qkv, z], axis=1).transpose(0, 2, 1, 3).reshape(D, 2048)
    o["win2"] = tiles(np.concatenate([heads, qb, zb, iq, ckv, ik, ik, ba, iw], axis=1))
    o["wout2"] = tiles(i["w_out_2"][0])
    o["wuv"] = np.ascontiguousarray(i["w_uv_2"][0].transpose(1, 0, 2))
    o["ab"] = np.stack([i["a_log_2"][0], i["dt_bias_2"][0]]).reshape(1, 8)
    o["rel"] = i["rel_bias_2"]
    v = {"ada_b0": i["ada_b"][0], "ada_b1": i["ada_b"][1],
         "mix0": i["norm_mix_g"][0], "mix1": i["norm_mix_g"][1], "ffn0": i["norm_ffn_g"][0], "ffn1": i["norm_ffn_g"][1],
         "lb0": i["hgrn_lb_logits"][0], "lb1": i["hgrn_lb_logits"][1], "onorm": i["hgrn_onorm_g"], "kv_b": i["kv_ada_b"],
         "kv_g": i["kv_norm_g"], "fin": i["final_norm_g"], "b_2": i["b_ada_2"], "pre": i["g_pre_2"], "post": i["g_post_2"],
         "conv": i["conv_w_2"], "gdn": i["g_gdn_2"], "gkv": i["g_kv_2"]}
    o["vecs"] = np.concatenate([columns(v[k]) for k in VECS], axis=1)
    o["cst"] = const_array(CONSTS)
    o["hot"] = constants()["hot"][0:32]
    o["flip"] = constants()["ident"][::-1]
    o["cste"] = const_array(CONSTS_E)
    return {k: np.ascontiguousarray(a) for k, a in o.items()}


def kernel(**inputs):
    import concourse.bacc as bacc
    from concourse.bass_utils import run_bass_kernel_spmd as run

    arrays = layout(inputs)
    nc = bacc.Bacc("TRN2", target_bir_lowering=False, num_devices=1)
    t = {k: nc.dram_tensor(f"in_{k}_dram", a.shape, mybir.dt.from_np(a.dtype), kind="ExternalInput").ap()
         for k, a in arrays.items()}
    out = nc.dram_tensor("out_0_dram", (S, D), F32, kind="ExternalOutput").ap()
    layer_stack_kernel(nc, t, out)
    r = run(nc, [{f"in_{k}_dram": a for k, a in arrays.items()}], core_ids=[0])
    return r.results[0]["out_0_dram"].reshape(1, S, D)
```

```python
from contextlib import ExitStack

import concourse.bass as bass
import numpy as np
from concourse import mybir
from concourse.alu_op_type import AluOpType as ALU

ACT = mybir.ActivationFunctionType
F32 = mybir.dt.float32
U32 = mybir.dt.uint32
AX = mybir.AxisListType.X

P = 128
D = 1024
S = 512
KC = D // P
NB = S // P
NH = 8
NE = 64
NKEY = 128
EPS = 1e-6
BIG = 3.0e38

CHUNKS_A = [(0, 1), (2, 3)]
CHUNKS_C = [(0, 1), (2, 3)]
CHUNKS_E = [(0, 1), (2,), (3,)]
TM = 256
NGATHER = 8
NWEIGHT = 8
PASSES = 4


def bucket(n):
    n = np.maximum(n, 0)
    nf = np.maximum(n, 1).astype(np.float32)
    large = 16 + (np.log(nf / np.float32(16)) / np.float32(np.log(128 / 16)) * np.float32(16)).astype(np.int32)
    return np.where(n < 16, n, np.minimum(large, 31))


CONSTS = ["ident", "ones", "cols", "strict", "nones", "mask16", "ntri", "reset", "negm", "iota"]
CONSTS_E = ["tri64", "sup64", "n1", "n1t", "m2", "m4", "m8", "m16", "m32"]


def constants():
    r = np.arange(P)
    i, j = r[:, None], r[None, :]
    same = lambda n: (i // n) == (j // n)
    c = {}
    c["ident"] = i == j
    c["ones"] = np.ones((P, P))
    c["nones"] = -np.ones((P, P))
    c["mask16"] = same(16) & (i <= j)
    c["ntri"] = -1.0 * (i >= j)
    c["strict"] = i < j
    c["negm"] = np.where(i < j, 0.0, -1e30)
    c["reset"] = (j % 16 != 0) & (i >= 0)
    c["iota"] = np.tile(np.arange(16), (P, 1))
    c["cols"] = np.tile(np.array([EPS, 1.0, -0.5 * np.log(128.0), 0.0]), (P, 1))
    c["tri64"] = same(64) & (i <= j)
    c["sup64"] = same(64) & (i > j)
    c["n1"] = ~(same(2) & (i % 2 == 1) & (j % 2 == 0))
    c["n1t"] = c["n1"].T
    for m in (2, 4, 8, 16, 32):
        c[f"m{m}"] = same(2 * m) & (i % (2 * m) >= m) & (j % (2 * m) < m)
    hot = np.zeros((P, 384))
    hot[bucket(255 - np.arange(384)), np.arange(384)] = 1.0
    c["hot"] = hot
    return {k: np.asarray(v, np.float32) for k, v in c.items()}


def const_array(names):
    c = constants()
    return np.ascontiguousarray(np.concatenate([c[k] for k in names], axis=1))


class Mark:

    def __init__(self, sem):
        self.sem, self.value = sem, 0


class Step:
    def __init__(self, unit, emit, after, us, nbytes=0, mark=None):
        self.unit, self.emit, self.after, self.us = unit, emit, after, us
        self.nbytes, self.mark, self.value = nbytes, mark, 0
        self.rank, self.place, self.lane, self.func = 0.0, 0, None, None


def latency(a, b):
    return 0.27 if b == "pe" else 0.2 if a == "pe" else 0.14


def flat(after):
    out = []
    for a in after:
        if a is None:
            continue
        if isinstance(a, (list, tuple)):
            out += flat(a)
        else:
            out.append(a)
    return out


def cols(ap):
    n = 1
    for s in ap.shape[1:]:
        n *= s
    return n


class Plan:
    UNITS = ("sp", "pool", "pe", "act", "dve")

    tag = ""

    def __init__(self):
        self.steps = []

    def add(self, unit, emit, after, us, nbytes=0, mark=None, lane=None):
        s = Step(unit, emit, flat(after), us, nbytes, mark)
        if mark is not None:
            mark.value += 16
            s.value = mark.value
        s.lane = lane
        s.tag = self.tag
        self.steps.append(s)
        return s

    def mm(self, bank, out, lhsT, rhs, start, stop, after=(), share=False, cost=None):
        us = 0.01 + 4 * max(cols(rhs), 64) / 2400 if cost is None else cost
        return self.add("pe", lambda e: e.matmul(out, lhsT, rhs, start=start, stop=stop, skip_group_check=share),
                        after, us, lane=bank)

    def tr(self, bank, out, in_, ident, after=()):
        return self.add("pe", lambda e: e.transpose(out, in_, ident), after, 0.13, lane=bank)

    def act(self, out, in_, func, after=(), bias=0.0, scale=1.0, accum=None):
        us = 0.07 + cols(in_) * 0.833e-3 + 0.093 * (not isinstance(scale, float)) + 0.093 * (not isinstance(bias, float))
        if accum is not None:
            s = self.add("act", lambda e: e.activation(out, in_, func, bias=bias, scale=scale, accum_out=accum),
                         after, us + 0.1)
        else:
            s = self.add("act", lambda e: e.activation(out, in_, func, bias=bias, scale=scale), after, us)
        s.func = func
        return s

    def vec(self, emit, n, after, rate=1.0):
        return self.add("dve", emit, after, 0.07 + n * rate * 1.04e-3)

    def tt(self, out, a, b, op, after=()):
        return self.vec(lambda e: e.tensor_tensor(out, a, b, op), cols(out), after)

    def ts(self, out, a, s1, s2, op0, op1=None, after=()):
        if op1 is None:
            return self.vec(lambda e: e.tensor_scalar(out, a, s1, None, op0), cols(out), after)
        return self.vec(lambda e: e.tensor_scalar(out, a, s1, s2, op0, op1), cols(out), after)

    def stt(self, out, a, s, b, op0, op1, after=()):
        return self.vec(lambda e: e.scalar_tensor_tensor(out, a, s, b, op0, op1), cols(out), after)

    def cp(self, out, a, after=()):
        return self.vec(lambda e: e.tensor_copy(out, a), cols(out), after)

    def fill(self, out, value, after=()):
        return self.vec(lambda e: e.memset(out, value), cols(out), after)

    def dma(self, unit, out, in_, mark, nbytes, after=(), lane=None):
        return self.add(unit, lambda e: e.dma_start(out, in_), after, 0.6, nbytes, mark, lane)

    def gather(self, out, table, idx, mark, after=()):
        return self.add("pool", lambda e: e.indirect_dma_start(out, None, table, bass.IndirectOffsetOnAxis(idx, 0)),
                        after, 1.04, P * D * 4, mark, "gather")

    def walk(self, before, follow, rank, back=False):
        steps = self.steps
        queues = {u: [] for u in self.UNITS}
        ready = {u: [] for u in self.UNITS}
        coming = {u: [] for u in self.UNITS}
        free = {u: 0.0 for u in self.UNITS}
        pending = [len(b) for b in before]
        reach = [0.0] * len(steps)
        done = [0.0] * len(steps)
        bus, now, left = 0.0, 0.0, len(steps)
        for k, s in enumerate(steps):
            if pending[k] == 0:
                ready[s.unit].append(k)
        while left:
            for u in self.UNITS:
                if free[u] > now + 1e-9:
                    continue
                if coming[u]:
                    ready[u] += [k for at, k in coming[u] if at <= now + 1e-9]
                    coming[u] = [(at, k) for at, k in coming[u] if at > now + 1e-9]
                if not ready[u]:
                    continue
                k = max(ready[u], key=lambda k: rank[k])
                ready[u].remove(k)
                queues[u].append(k)
                left -= 1
                s = steps[k]
                free[u] = end = now + s.us
                if s.mark is not None:
                    if back:
                        bus = max(bus, now + 2.0) + s.nbytes / 360e3
                        end = bus + s.us
                    else:
                        bus = max(bus, end) + s.nbytes / 360e3
                        end = bus + 2.0
                done[k] = end
                for f, data in follow[k]:
                    at = free[u] if not data else end + (latency(steps[f].unit, u) if back else latency(u, steps[f].unit))
                    reach[f] = max(reach[f], at)
                    pending[f] -= 1
                    if pending[f] == 0:
                        coming[steps[f].unit].append((reach[f], f))
            if left:
                times = [free[u] for u in self.UNITS if ready[u]]
                times += [max(free[u], min(at for at, _ in coming[u])) for u in self.UNITS if coming[u]]
                now = max(now, min(times))
        return done, queues, max(done)

    def order(self):
        steps = self.steps
        place = {id(s): k for k, s in enumerate(steps)}
        before, follow = [{} for _ in steps], [{} for _ in steps]
        lanes = {}
        for k, s in enumerate(steps):
            if s.lane is not None:
                prev = lanes.get((s.unit, s.lane))
                if prev is not None:
                    before[k][prev] = follow[prev][k] = False
                lanes[(s.unit, s.lane)] = k
            for a in s.after:
                a = place[id(a)]
                before[k][a] = follow[a][k] = True
        before, follow = [list(b.items()) for b in before], [list(f.items()) for f in follow]
        rank = [0.0] * len(steps)
        for k in range(len(steps) - 1, -1, -1):
            s = steps[k]
            us = max(s.us, s.nbytes / 360e3) * (1.1 if s.tag else 1.0)
            rank[k] = us + max([rank[f] for f, _ in follow[k]], default=0.0)
        best = None
        for it in range(PASSES):
            done, queues, end = self.walk(before, follow, [(r, -k) for k, r in enumerate(rank)])
            if best is None or end < best[0]:
                best = end, queues
            if it < PASSES - 1:
                rank, _, _ = self.walk(follow, before, [(done[k], k) for k in range(len(steps))], True)
        _, queues = best
        for u in self.UNITS:
            queues[u] = [steps[k] for k in queues[u]]
            for k, s in enumerate(queues[u]):
                s.place = k
        return queues

    def emit(self, nc, sems, last):
        queues = self.order()
        for u in self.UNITS:
            n = 0
            for s in queues[u]:
                if s.mark is None:
                    n += 1
                    s.value = n

        def run(eng, unit):
            seen = {}
            table = None
            for s in queues[unit]:
                if s.func in (ACT.Exp, ACT.Ln) and table != "exp_ln":
                    eng.preload_act_table_set("natural_log_exp_and_others")
                    table = "exp_ln"
                if s.func == ACT.Gelu:
                    table = "gelu"
                need = {}
                for a in s.after:
                    key = a.unit if a.mark is None else a.mark
                    need[key] = max(need.get(key, 0), a.value)
                for key, value in need.items():
                    if seen.get(key, 0) < value:
                        seen[key] = value
                        eng.wait_ge(sems[key] if isinstance(key, str) else key.sem, value)
                ins = s.emit(eng)
                if s.mark is None:
                    ins.then_inc(sems[unit], 1)
                else:
                    ins.then_inc(s.mark.sem, 16)
            if unit == "sp":
                for s in last:
                    eng.wait_ge(s.mark.sem, s.value)

        with nc.Block() as block:
            @block.sync
            def _(e):
                run(e, "sp")

            @block.gpsimd
            def _(e):
                run(e, "pool")

            @block.tensor
            def _(e):
                run(e, "pe")

            @block.scalar
            def _(e):
                run(e, "act")

            @block.vector
            def _(e):
                run(e, "dve")


class Ring:

    def __init__(self, n):
        self.n, self.next, self.free = n, 0, [[] for _ in range(n)]

    def take(self):
        i, fr = self.next, self.free[self.next]
        assert fr is not None, "slot still in use"
        self.next, self.free[i] = (i + 1) % self.n, None
        return i, fr

    def done(self, i, steps):
        self.free[i] = list(steps)


VECS = {}


def _vec_cols():
    at = 0
    for name, n in (("c", 8), ("ada_b0", 48), ("ada_b1", 48), ("mix0", 8), ("mix1", 8), ("ffn0", 8),
                    ("ffn1", 8), ("lb0", 8), ("lb1", 8), ("onorm", 8), ("kv_b", 16), ("kv_g", 8), ("fin", 8),
                    ("b_2", 24), ("pre", 8), ("post", 8), ("conv", 48), ("gdn", 1), ("gkv", 1)):
        VECS[name] = (at, n)
        at += n
    return at


NVEC = _vec_cols()


def layer_stack_kernel(nc: bass.Bass, t: dict, out: bass.AP, upto: str = "E", probes=None):
    ctx = ExitStack()
    sb = lambda name, shape, dt=F32: ctx.enter_context(nc.sbuf_tensor(name, shape, dt))
    sem = lambda name: ctx.enter_context(nc.semaphore(name))
    mark = lambda name: Mark(sem(name))
    sems = {u: sem("s_" + u) for u in ("pool", "pe", "act", "dve")}
    p = Plan()

    ps = ctx.enter_context(nc.psum_tensor("ps", [P, 8, 512], F32))
    cc = {k: v.shape[1] for k, v in constants().items()}
    cst = sb("cst", [P, sum(cc[k] for k in CONSTS)])
    vec = sb("vec", [P, NVEC])
    h = sb("h", [P, NB, D])
    hn = sb("hn", [P, KC, TM])
    oT = sb("oT", [P, KC, TM])
    X = [sb(f"X{i}", [P, D]) for i in range(2)]
    xs = sb("xs", [P, D])
    acc = sb("acc", [P, D])
    gat = [sb(f"gat{i}", [P, D]) for i in range(NGATHER)]
    wbuf = sb("wbuf", [P, NWEIGHT, 2, 512])
    row = [sb(f"row{i}", [P, D]) for i in range(3)]
    dgb = [sb(f"dg{i}", [P, P]) for i in range(5)]
    mod = [sb("mod0", [P, 48]), sb("mod1", [P, 48])]
    kvm = sb("kvm", [P, 16])
    mod2 = sb("mod2", [P, 24])
    gT = sb("gT", [P, 6, 8])
    spot = sb("spot", [P, 1])
    small = sb("small", [P, 16, 4])
    idxb = sb("idx", [P, NB, NE], U32)
    gate = sb("gate", [P, NB, NE])
    hid = sb("hid", [P, 2, NE])
    wgt = sb("wgt", [P, 2, NE])
    NWS = 18400
    ws = sb("ws", [P, NWS])

    def region(base):
        at = [base]

        def take(*shape):
            n = 1
            for k in shape:
                n *= k
            v = ws[:, at[0]:at[0] + n]
            at[0] += n
            assert at[0] <= NWS, at[0]
            if len(shape) == 2:
                v = v.rearrange("p (a b) -> p a b", a=shape[0])
            elif len(shape) == 3:
                v = v.rearrange("p (a b c) -> p a b c", a=shape[0], b=shape[1])
            return v

        return take, at

    C = {}
    at = 0
    for k in CONSTS:
        C[k] = cst[:, at:at + cc[k]]
        at += cc[k]
    eps, one, nhl = C["cols"][:, 0:1], C["cols"][:, 1:2], C["cols"][:, 2:3]

    def V(name, lo=0, n=None):
        a0, k = VECS[name]
        return vec[:, a0 + lo:a0 + lo + (k - lo if n is None else n)]

    m_c, m_v = mark("m_c"), mark("m_v")
    m_h = [mark(f"m_h{b}") for b in range(NB)]
    ld_v = p.dma("sp", vec[:, :], t["vecs"], m_v, P * NVEC * 4)
    ld_c = p.dma("sp", cst[:, :], t["cst"], m_c, P * cst.shape[1] * 4)
    ld_h = [p.dma("sp", h[:, b, :], t["x"][b * P:(b + 1) * P, :], m_h[b], P * D * 4) for b in range(NB)]
    hw = [[s] for s in ld_h]
    hr = [[] for _ in range(NB)]

    bankD, bankX, bankO = Ring(3), Ring(2), Ring(1)
    DB, XB, OB, VB = (0, 1, 2), (3, 4), (5,), 6
    ringW, ringG, ringV, ringR = Ring(NWEIGHT), Ring(NGATHER), Ring(3), Ring(2)
    ringS = Ring(16)
    mW = [mark(f"m_w{i}") for i in range(NWEIGHT)]
    mG = [mark(f"m_g{i}") for i in range(NGATHER)]
    mA = [mark(f"m_a{i}") for i in range(NGATHER)]
    free = {"hn": [], "oT": [], "xs": [], "acc": [], "X0": [], "X1": [], "V": [],
            "Vb": [[], []], "mv": [[], []]}

    row_users = {0: [], 1: [], 2: []}
    hn_users = []

    def hn_again():
        free["hn"] = list(hn_users)
        hn_users.clear()

    class Weights:

        def __init__(self, name, g):
            self.slots, self.loads = [], []
            for q in range(4):
                i, fr = ringW.take()
                self.slots.append(i)
                self.loads.append(p.dma("sp", wbuf[:, i, :, :], t[name][g, q], mW[i], P * D * 4, fr, "w"))
            self.used = [[] for _ in range(4)]

        def at(self, kc, lo, n):
            return wbuf[:, self.slots[kc // 2], kc % 2, lo:lo + n]

        def load(self, kc):
            return self.loads[kc // 2]

        def use(self, kc, step):
            self.used[kc // 2].append(step)

        def done(self):
            for i, u in zip(self.slots, self.used):
                ringW.done(i, u)

    def silu_of(outp, z, tmp, after):
        a = p.act(tmp, z, ACT.Exp, after, scale=-1.0)
        a = p.act(tmp, tmp, ACT.Ln, [a, ld_c], bias=one)
        a = p.act(tmp, tmp, ACT.Exp, [a], scale=-1.0)
        return p.tt(outp, z, tmp, ALU.mult, [a])

    crow = [acc, row[2]]
    c_ready = []
    for k in range(2):
        cr = t["cc"]
        ld = p.dma("sp", crow[k][:, :], bass.AP(cr.tensor, k * D, [[0, P], [1, D]]), mark(f"m_r{k}"), P * D * 4)
        c_ready.append(silu_of(crow[k][:, :], crow[k][:, :], xs[:, :], [ld, free["xs"]]))
        free["xs"] = [c_ready[k]]
    crow_users = [[], []]

    def dot_tile(name, g, k, dst, after=()):
        s_, fr = ringG.take()
        ld = p.dma("sp", gat[s_][:, :], t[name][g], mA[s_], P * D * 4, fr, "ada")
        d = p.vec(lambda e, g_=gat[s_], c_=crow[k], o=dst:
                  e.tensor_tensor_reduce(g_[:, :], g_[:, :], c_[:, :], 1.0, 0.0, ALU.mult, ALU.add, o),
                  D, [ld, c_ready[k]])
        ringG.done(s_, [d])
        crow_users[k].append(d)
        return d

    def matvec(name, g, k, dst, bias, late=None):
        n = dst.shape[1]
        out_, dots = [], []

        def one(m):
            dots.append(dot_tile(name, g + m, k, dst[:, m:m + 1]))
            if m == n - 1:
                out_.append(p.tt(dst, dst, bias, ALU.add, [dots, ld_v]))

        for m in range(n):
            if late is None:
                one(m)
            else:
                late.append(lambda m=m: one(m))
        return out_

    def matvec_pe(name, G, cT, dst, bias, after):
        B = VB + G % 2
        slots = {}
        for pair in range(4):
            for q in range(4):
                s_, fr = ringG.take()
                slots[q] = (s_, p.dma("sp", gat[s_][:, :], t[name][4 * G + q, pair], mA[s_], P * D * 4, fr, "ada"))
            ms = {q: [] for q in range(4)}
            for k in range(2):
                kc = 2 * pair + k
                for q in range(4):
                    m = p.mm(B, ps[32 * q:32 * q + 32, B, :], cT[:, kc, :], gat[slots[q][0]][:, 512 * k:512 * k + 512],
                             kc == 0, kc == KC - 1, [slots[q][1], after, free["Vb"][B - VB]], cost=0.25)
                    ms[q].append(m)
            for q in range(4):
                ringG.done(slots[q][0], ms[q])
        rows = X[0][:, 512 * (G % 2):512 * (G % 2) + 512]
        e = p.act(rows, ps[:, B, :], ACT.Identity, [ms[0], ms[1], ms[2], ms[3], free["mv"][G % 2]])
        for k in range(4):
            m = p.tr(B, ps[:, B, k * P:(k + 1) * P], rows[:, k * P:(k + 1) * P], C["ident"], [e, ld_c])
        free["mv"][G % 2] = [m]
        free["X0"] = free["X0"] + [m]
        r = p.tt(dst.rearrange("p (q k) -> p q k", q=4), ps[:, B, :].rearrange("p (k q i) -> p q k i", k=4, q=4)[:, :, :, 0],
                 bias.rearrange("p (q k) -> p q k", q=4), ALU.add, [m, ld_v])
        free["Vb"][B - VB] = [r]
        free["V"] = free["V"] + [r]
        return [r]

    def modvec(l, part, late=None):
        return matvec(f"ada{l}", 8 * part, 0, mod[l][:, 8 * part:8 * part + 8], V(f"ada_b{l}", 8 * part, 8))

    def gain(k, scale, g, after):
        return p.stt(gT[:, k, :], scale, 1.0, g, ALU.add, ALU.mult, [after, ld_v])

    def broadcast_row(k, col8, after):
        out_steps, fr_row = [], list(row_users[k])
        row_users[k].clear()
        for half in range(2):
            i, fr = bankD.take()
            for q in range(4):
                d, dfr = ringR.take()
                d += 3
                a = p.act(dgb[d][:, :], C["ident"], ACT.Identity, [after, dfr, ld_c], scale=col8[:, 4 * half + q:4 * half + q + 1])
                mmv = p.mm(DB[i], ps[:, DB[i], q * P:(q + 1) * P], C["ones"], dgb[d][:, :], True, True, [a, fr])
                ringR.done(d - 3, [mmv])
            e = p.act(row[k][:, half * 512:half * 512 + 512], ps[:, DB[i], :], ACT.Identity, [mmv, fr_row])
            bankD.done(i, [e])
            out_steps.append(e)
        return out_steps

    def rms(src, dst, n, after):
        s, sfr = ringS.take()
        c = small[:, s, 0:1]
        a = p.act(dst, src, ACT.Square, [after, sfr], accum=c)
        a = p.act(c, c, ACT.Ln, [a], bias=eps, scale=1.0 / n)
        return p.act(c, c, ACT.Exp, [a], scale=-0.5), c, s

    def normed(src, after):
        a, c, s = rms(src, xs[:, :], D, [after, free["xs"]])
        a = p.act(xs[:, :], src, ACT.Identity, [a], scale=c)
        ringS.done(s, [a])
        return a

    def spread(a, j, targets):
        trs, evs = [], [[] for _ in targets]
        for half in range(2):
            i, fr = bankD.take()
            for q in range(4):
                kc = 4 * half + q
                trs.append(p.tr(DB[i], ps[:, DB[i], q * P:(q + 1) * P], xs[:, kc * P:(kc + 1) * P], C["ident"], [a, fr, ld_c]))
            last = []
            for q in range(4):
                kc = 4 * half + q
                for n, (dst, g, sh, after) in enumerate(targets):
                    d_, s_ = dst[:, kc, j * P:(j + 1) * P], ps[:, DB[i], q * P:(q + 1) * P]
                    if half:
                        e = p.act(d_, s_, ACT.Identity, [trs[-1], after], scale=g[:, kc:kc + 1], bias=sh[:, kc:kc + 1])
                    else:
                        e = p.ts(d_, s_, g[:, kc:kc + 1], sh[:, kc:kc + 1], ALU.mult, ALU.add, [trs[-1], after])
                        e.us += 0.08
                    last.append(e)
                    evs[n].append(e)
            bankD.done(i, last)
        return trs, evs

    def project(w, m, T, after, src=hn):
        i, fr = bankD.take()
        for kc in range(KC):
            last = p.mm(DB[i], ps[:, DB[i], 0:T], w.at(kc, m * P, P), src[:, kc, 0:T], kc == 0, kc == KC - 1,
                        [after, w.load(kc), fr])
            w.use(kc, last)
        return i, last

    def add_mix(w2, b, j, src, after, grow, gready):
        used = []
        new = []
        for n in range(2):
            i, fr = bankD.take()
            for kc in range(KC):
                last = p.mm(DB[i], ps[:, DB[i], :], src[:, kc, j * P:(j + 1) * P], w2[n].at(kc, 0, 512), kc == 0, kc == KC - 1,
                            [after, w2[n].load(kc), fr])
                w2[n].use(kc, last)
            used.append(last)
            k, tfr = ringT.take()
            e = p.tt(tmpb[k], ps[:, DB[i], :], row[grow][:, n * 512:n * 512 + 512], ALU.mult, [last, gready, tfr])
            bankD.done(i, [e])
            row_users[grow].append(e)
            f = p.tt(h[:, b, n * 512:n * 512 + 512], h[:, b, n * 512:n * 512 + 512], tmpb[k], ALU.add, [e, hw[b], hr[b]])
            ringT.done(k, [f])
            new.append(f)
        hw[b], hr[b] = new, []
        return used

    tw, at_ = region(0)
    tmpb = [tw(512) for _ in range(2)]
    ringT = Ring(2)
    scs = tw(2, 2, P)
    cand = tw(4, 256)
    s16 = tw(8, 16)
    i16 = tw(8, 16).bitcast(U32)
    i16f = tw(8, 16)
    b16 = tw(4, 16)
    f16 = tw(4, 16).bitcast(U32)
    fa = tw(4, 16).bitcast(U32)
    fb = tw(4, 16).bitcast(U32)
    faf = tw(4, 16)
    fbf = tw(4, 16)
    e1 = tw(4, 16)
    e2 = tw(4, 16)
    gm = tw(4, 1)
    selfree = {"scs": [[], []], "head": [[] for _ in range(4)], "gate": []}
    COMMON = at_[0]

    ready = {}

    def bc(ap, *shape):
        return ap.broadcast_to([P, *shape])

    def select(l, chunk, hn_ready):
        T = P * len(chunk)
        qw = []
        for g in range(2):
            w = Weights(f"pq{l}", g)
            for m in range(4):
                i, last = project(w, m, T, hn_ready)
                hn_users.append(last)
                e = p.act(oT[:, 4 * g + m, 0:T], ps[:, DB[i], 0:T], ACT.Identity, [last, free["oT"]])
                bankD.done(i, [e])
                qw.append(e)
            w.done()
            if g == 0:
                si, sfr = ringW.take()
                sk = wbuf[:, si, :, :].rearrange("p a (b n) -> p (a b) n", b=4)
                ld = p.dma("sp", wbuf[:, si, :, :], t[f"sub{l}"], mW[si], P * D * 4, sfr, "w")
        free["oT"] = None
        scm = []
        for j, b in enumerate(chunk):
            old = free.get(("idx", b), [])
            ready[b] = {"idx": [], "gate": None}
            t2 = []
            for hh in range(4):
                i, fr = bankX.take()
                for q in range(2):
                    hp = 2 * hh + q
                    last = p.mm(XB[i], ps[:, XB[i], q * P:(q + 1) * P], oT[:, hp, j * P:(j + 1) * P], sk[:, hp, :], True, True,
                                [qw[hp], ld, fr])
                scm.append(last)
                e = p.act(scs[:, hh % 2].rearrange("p a b -> p (a b)"), ps[:, XB[i], 0:2 * P], ACT.Identity,
                          [last, selfree["scs"][hh % 2]])
                bankX.done(i, [e])
                fr = selfree["head"][hh]
                tops = []
                for q in range(2):
                    s_, v8, u8 = scs[:, hh % 2, q, :], s16[:, 2 * hh + q, :], i16[:, 2 * hh + q, :]
                    a = p.vec(lambda e, o=v8[:, 0:8], i_=s_: e.max(o, i_), P, [e, fr])
                    a = p.vec(lambda e, o=u8[:, 0:8], m=v8[:, 0:8], i_=s_: e.max_index(o, m, i_), P, [a])
                    a = p.vec(lambda e, m=v8[:, 0:8], i_=s_: e.match_replace(i_, m, i_, -BIG), P, [a])
                    a = p.vec(lambda e, o=v8[:, 8:16], i_=s_: e.max(o, i_), P, [a])
                    a = p.vec(lambda e, o=u8[:, 8:16], m=v8[:, 8:16], i_=s_: e.max_index(o, m, i_), P, [a])
                    tops.append(a)
                selfree["scs"][hh % 2] = tops
                hs = slice(2 * hh, 2 * hh + 2)
                ic = p.cp(i16f[:, hs, :], i16[:, hs, :], [tops])
                c3 = cand[:, hh, :].rearrange("p (a b) -> p a b", a=16)
                a = p.tt(c3, bc(s16[:, 2 * hh, :].rearrange("p (a b) -> p a b", b=1), 16, 16),
                         bc(s16[:, 2 * hh + 1, :].rearrange("p (a b) -> p a b", a=1), 16, 16), ALU.add, [tops, fr])
                s_, v8, u8 = cand[:, hh, :], b16[:, hh, :], f16[:, hh, :]
                a = p.vec(lambda e, o=v8[:, 0:8], i_=s_: e.max(o, i_), 256, [a, selfree["gate"]])
                a = p.vec(lambda e, o=u8[:, 0:8], m=v8[:, 0:8], i_=s_: e.max_index(o, m, i_), 256, [a])
                a = p.vec(lambda e, m=v8[:, 0:8], i_=s_: e.match_replace(i_, m, i_, -BIG), 256, [a])
                a = p.vec(lambda e, o=v8[:, 8:16], i_=s_: e.max(o, i_), 256, [a])
                a = p.vec(lambda e, o=u8[:, 8:16], m=v8[:, 8:16], i_=s_: e.max_index(o, m, i_), 256, [a])
                t2.append(a)
                a1 = p.ts(fa[:, hh], f16[:, hh], 4, None, ALU.logical_shift_right, None, [a])
                b1 = p.ts(fb[:, hh], f16[:, hh], 15, None, ALU.bitwise_and, None, [a])
                a2 = p.cp(faf[:, hh], fa[:, hh], [a1])
                b2 = p.cp(fbf[:, hh], fb[:, hh], [b1])
                prev = a
                es = []
                for half, src, dst, rd in ((0, faf, e1, a2), (1, fbf, e2, b2)):
                    x1 = p.tt(c3, bc(src[:, hh].rearrange("p (k n) -> p k n", n=1), 16, 16),
                              bc(C["iota"].rearrange("p (k n) -> p k n", k=1), 16, 16), ALU.is_equal, [rd, prev, ic])
                    x2 = p.tt(c3, c3, bc(i16f[:, 2 * hh + half, :].rearrange("p (k n) -> p k n", k=1), 16, 16), ALU.mult, [x1])
                    x3 = p.vec(lambda e, o=dst[:, hh], i_=c3: e.tensor_reduce(o, i_, AX, ALU.add), 256, [x2])
                    prev = [x3]
                    es.append(x3)
                x4 = p.stt(e2[:, hh], e1[:, hh], float(NKEY), e2[:, hh], ALU.mult, ALU.add, [es])
                x5 = p.ts(idxb[:, b, 16 * hh:16 * hh + 16], e2[:, hh], float(l * NKEY * NKEY), None, ALU.add, None, [x4, old])
                selfree["head"][hh] = [x5]
                ready[b]["idx"].append(x5)
            gb = gate[:, b, :].rearrange("p (a b) -> p a b", a=4)
            g1_ = p.tt(gb, b16, bc(b16[:, :, 0:1], 4, 16), ALU.subtract, [t2, free.get(("gate", b), [])])
            g2_ = p.act(gb, gb, ACT.Exp, [g1_])
            g3_ = p.vec(lambda e, o=gm, i_=gb: e.tensor_reduce(o, i_, AX, ALU.add), 64, [g2_, selfree["gate"]])
            g4_ = p.vec(lambda e, o=gm: e.reciprocal(o, o), 4, [g3_], 8.0)
            g5_ = p.tt(gb, gb, bc(gm, 4, 16), ALU.mult, [g4_])
            selfree["gate"] = [g5_]
            ready[b]["gate"] = g5_
        ringW.done(si, scm)
        free["oT"] = scm

    def keep_rows(chunk, hn_ready):
        for j, b in enumerate(chunk):
            evs = []
            for half in range(2):
                i, fr = bankD.take()
                for q in range(4):
                    kc = 4 * half + q
                    last = p.tr(DB[i], ps[:, DB[i], q * P:(q + 1) * P], hn[:, kc, j * P:(j + 1) * P], C["ident"], [hn_ready, fr])
                hn_users.append(last)
                e = p.act(X[b % 2][:, half * 512:half * 512 + 512], ps[:, DB[i], :], ACT.Identity, [last, free[f"X{b % 2}"]])
                bankD.done(i, [e])
                evs.append(e)
            free[f"X{b % 2}"] = None
            ready[b]["X"] = evs

    def experts(l, blocks, grow, gready, late=()):
        us = [("u", b, e) for b in blocks for e in range(NE)]
        vs = [("v", b, e) for b in blocks for e in range(NE)]
        seq = us[:16]
        for k in range(16, len(us)):
            seq += [us[k], vs[k - 16]]
        seq += vs[-16:]
        dots = {}
        accs = {b: [] for b in blocks}
        wsteps = {}
        late = list(late)
        every = len(seq) // (len(late) + 1)
        for n_, (kind, b, e) in enumerate(seq):
            if late and n_ % every == every - 1:
                late.pop(0)()
            s, fr = ringG.take()
            rd = ready[b]
            g = p.gather(gat[s][:, :], t["peer_" + kind], idxb[:, b, e:e + 1], mG[s], [fr, rd["idx"][e // 16]])
            if kind == "u":
                first = [] if e else free.get(("hid", b % 2), [])
                d = p.vec(lambda en, g_=gat[s], x_=X[b % 2], o=hid[:, b % 2, e:e + 1]:
                          en.tensor_tensor_reduce(g_[:, :], g_[:, :], x_[:, :], 1.0, 0.0, ALU.mult, ALU.add, o),
                          D, [g, rd["X"], free.get(("hid", b % 2), [])])
                ringG.done(s, [d])
                dots.setdefault(b, []).append(d)
                if e % 16 == 15:
                    lo = e - 15
                    hsl, wsl = hid[:, b % 2, lo:e + 1], wgt[:, b % 2, lo:e + 1]
                    a = p.act(hsl, hsl, ACT.Gelu, [dots[b][lo:]])
                    a = p.tt(wsl, hsl, gate[:, b, lo:e + 1], ALU.mult, [a, rd["gate"], free.get(("wgt", b % 2), [])])
                    for k in range(lo, e + 1):
                        wsteps[(b, k)] = a
                if e == NE - 1:
                    free[f"X{b % 2}"] = dots[b]
                    free[("hid", b % 2)] = [a]
                    free[("gate", b)] = [a]
            else:
                wc = wgt[:, b % 2, e:e + 1]
                wst = wsteps[(b, e)]
                if e == 0 or (e % 2 == 1 and 1 < e < NE - 1):
                    if e == 0:
                        a = p.ts(acc[:, :], gat[s][:, :], wc, None, ALU.mult, None, [g, wst, free["acc"]])
                    else:
                        a = p.stt(acc[:, :], gat[s][:, :], wc, acc[:, :], ALU.mult, ALU.add, [g, wst, prev_acc])
                    prev_acc = a
                    ringG.done(s, [a])
                else:
                    k, dfr = ringV.take()
                    a = p.act(dgb[k][:, :], C["ident"], ACT.Identity, [wst, dfr], scale=wc)
                    m = []
                    for half in range(2):
                        m.append(p.mm(VB + half, ps[:, VB + half, :], dgb[k][:, :], gat[s][:, half * 512:half * 512 + 512], e == 1, e == NE - 1,
                                      [a, g, free["V"]], cost=0.95))
                    ringV.done(k, m)
                    ringG.done(s, m)
                    lastd = a
                    lastm = m
                if e == NE - 1:
                    free[("idx", b)] = [g]
                    free[("wgt", b % 2)] = [prev_acc, lastd]
                    pv = ps[:, VB:VB + 2, :].rearrange("p a b -> p (a b)")
                    x1 = p.tt(acc[:, :], pv, acc[:, :], ALU.add, [prev_acc, lastm])
                    x2 = p.tt(acc[:, :], acc[:, :], row[grow][:, :], ALU.mult, [x1, gready])
                    x3 = p.tt(h[:, b, :], h[:, b, :], acc[:, :], ALU.add, [x2, hw[b], hr[b]])
                    hw[b], hr[b] = [x3], []
                    free["acc"], free["V"] = [x3], [x1]
                    row_users[grow].append(x2)

    tA, atA = region(COMMON)
    lbv, oml, noml, lt0, lt1 = (tA(8) for _ in range(5))
    SA = tA(8, P)
    hset = [{k: tA(3, TM) if k == "sg" else tA(2, P) if k == "v" else tA(TM)
             for k in ("sg", "kk", "cum", "ecum", "kd", "dl", "qd", "v", "sq", "o1")} for _ in range(2)]
    kset = [{"KM": tA(8 * 144), "qP": tA(P), "sc": tA(P), "KT": tA(P), "pre": tA(16)} for _ in range(2)]
    ringH, ringK = Ring(2), Ring(2)
    stateA = {}

    def hgrn_setup():
        m = p.tt(lt0, V("lb0"), V("lb1"), ALU.max, [ld_v])
        a = p.tt(lbv, V("lb0"), lt0, ALU.subtract, [m])
        b = p.tt(lt1, V("lb1"), lt0, ALU.subtract, [m])
        a = p.act(lbv, lbv, ACT.Exp, [a])
        b = p.act(lt1, lt1, ACT.Exp, [b])
        s = p.tt(lt0, lbv, lt1, ALU.add, [a, b])
        s = p.vec(lambda e: e.reciprocal(lt0, lt0), 8, [s], 8.0)
        a = p.tt(lbv, lbv, lt0, ALU.mult, [s])
        b = p.tt(oml, lt1, lt0, ALU.mult, [s])
        c = p.ts(noml, oml, -1.0, None, ALU.mult, None, [b])
        lb_ready = [a, b, c]
        for k in kset:
            ringK.done(kset.index(k), [p.fill(k["KM"], 0.0), p.fill(k["sc"], 0.0), p.fill(k["pre"], 1.0)])
        return lb_ready

    def sigmoid_ps(dst, src, after):
        a = p.act(dst, src, ACT.Exp, after, scale=-1.0)
        b = p.act(dst, dst, ACT.Ln, [a], bias=one)
        return a, p.act(dst, dst, ACT.Exp, [b], scale=-1.0)

    def hgrn(chunk, hn_ready, lb_ready):
        T = P * len(chunk)
        nb = len(chunk)
        done = []
        for hh in range(NH):
            k, fr = ringH.take()
            q = hset[k]
            sg = q["sg"][:, :, 0:T]
            w = Weights("win", hh)
            i, last = project(w, 1, T, hn_ready)
            hn_users.append(last)
            a, sf = sigmoid_ps(sg[:, 1, :], ps[:, DB[i], 0:T], [last, fr, ld_c])
            bankD.done(i, [a])
            kk, cum, ecum, kd, dl, qd = (q[n][:, 0:T] for n in ("kk", "cum", "ecum", "kd", "dl", "qd"))
            k1 = p.ts(kk, sg[:, 1, :], noml[:, hh:hh + 1], oml[:, hh:hh + 1], ALU.mult, ALU.add, [sf, lb_ready, fr])
            lf = p.act(cum, sg[:, 1, :], ACT.Ln, [sf, lb_ready, fr], bias=lbv[:, hh:hh + 1], scale=oml[:, hh:hh + 1])
            cu = [p.vec(lambda e, o=cum[:, j * P:(j + 1) * P]:
                        e.tensor_tensor_scan(o, C["reset"], o, 0.0, ALU.mult, ALU.add), P, [lf, ld_c], 2.0)
                  for j in range(nb)]
            c16 = cum.rearrange("p (n c) -> p n c", c=16)
            d0 = p.tt(dl.rearrange("p (n c) -> p n c", c=16), bc(c16[:, :, 15:16], T // 16, 16), c16, ALU.subtract, [cu, fr])
            ec = p.act(ecum, cum, ACT.Exp, [cu, fr])
            en = p.act(kd, cum, ACT.Exp, [cu, fr], scale=-1.0)
            d1 = p.act(dl, dl, ACT.Exp, [d0])
            kd1 = p.tt(kd, kd, kk, ALU.mult, [en, k1])
            i, last = project(w, 0, T, hn_ready)
            hn_users.append(last)
            a, sq_ = sigmoid_ps(sg[:, 0, :], ps[:, DB[i], 0:T], [last, fr])
            a = p.tt(sg[:, 0, :], sg[:, 0, :], ps[:, DB[i], 0:T], ALU.mult, [sq_])
            bankD.done(i, [a])
            qd1 = p.tt(qd, sg[:, 0, :], ecum, ALU.mult, [a, ec, fr])
            i, bfr = bankD.take()
            for j in range(nb):
                for kc in range(KC):
                    last = p.mm(DB[i], ps[:, DB[i], j * P:(j + 1) * P], hn[:, kc, j * P:(j + 1) * P], w.at(kc, 3 * P, P),
                                kc == 0, kc == KC - 1, [hn_ready, w.load(kc), bfr])
                    w.use(kc, last)
            hn_users.append(last)
            vv = p.act(q["v"][:, 0:nb, :].rearrange("p a b -> p (a b)"), ps[:, DB[i], 0:T], ACT.Identity, [last, fr])
            bankD.done(i, [vv])
            i, last = project(w, 2, T, hn_ready)
            hn_users.append(last)
            a, sg_ = sigmoid_ps(sg[:, 2, :], ps[:, DB[i], 0:T], [last, fr])
            gs = p.tt(sg[:, 2, :], sg[:, 2, :], ps[:, DB[i], 0:T], ALU.mult, [sg_])
            bankD.done(i, [gs])
            w.done()
            o, ofr = bankO.take()
            po = ps[:, OB[o], 0:T]
            users = []
            for j, b in enumerate(chunk):
                x, kfr = ringK.take()
                z = kset[x]
                KM, qP, sc, KT, pre = z["KM"], z["qP"], z["sc"], z["KT"], z["pre"]
                sl = slice(j * P, (j + 1) * P)
                ed = ecum[:, sl].rearrange("p (n c) -> p n c", c=16)[:, :, 15]
                km = [p.tt(KM.rearrange("p (r c) -> p r c", c=144)[:, :, 0:16], dl[:, sl].rearrange("p (r c) -> p r c", c=16),
                           kk[:, sl].rearrange("p (r c) -> p r c", c=16), ALU.mult, [d1, k1, kfr])]
                for r in range(1, 8):
                    km.append(p.ts(KM[:, r * P:r * P + 16 * r], KM[:, (r - 1) * P:(r - 1) * P + 16 * r], ed[:, r:r + 1], None,
                                   ALU.mult, None, [km[-1], ec]))
                pr = p.vec(lambda e, o=pre[:, 1:9], d=ed: e.tensor_tensor_scan(o, d, C["ones"][:, 0:8], 1.0, ALU.mult, ALU.mult),
                           8, [ec, kfr], 2.0)
                qp = p.tt(qP.rearrange("p (n c) -> p n c", c=16), qd[:, sl].rearrange("p (n c) -> p n c", c=16),
                          bc(pre[:, 0:8].rearrange("p (n c) -> p n c", c=1), 8, 16), ALU.mult, [pr, qd1])
                i, xfr = bankX.take()
                B = XB[i]
                for r in range(1, 8):
                    m1 = p.mm(B, ps[:, B, 16 * r:16 * r + 16], KM[:, (r - 1) * P:r * P], qd[:, j * P + 16 * r:j * P + 16 * r + 16],
                              True, True, [km[r - 1], qd1, xfr])
                m2 = p.mm(B, ps[:, B, P:2 * P], kd[:, sl], qd[:, sl], True, True, [kd1, qd1, xfr])
                m3 = p.tr(B, ps[:, B, 2 * P:3 * P], KM[:, 7 * P:8 * P], C["ident"], [km[7], ld_c, xfr])
                s1 = p.act(sc[:, 16:P], ps[:, B, 16:P], ACT.Identity, [m1, m2, m3, kfr])
                s2 = p.act(KT, ps[:, B, 2 * P:3 * P], ACT.Identity, [m3, m2, m1, kfr])
                s3 = p.vec(lambda e, o=sc, m=C["mask16"].bitcast(U32), d=ps[:, B, P:2 * P]: e.copy_predicated(o, m, d),
                           P, [s1, s2, ld_c])
                o1 = p.mm(OB[o], po[:, sl], q["v"][:, j, :], sc, True, b == 0, [vv, s3, ofr])
                if b > 0:
                    o1 = p.mm(OB[o], po[:, sl], SA[:, hh, :], qP, False, True, [stateA[hh], qp])
                users += [o1, km[-1], qp]
                if b < NB - 1:
                    m4 = p.mm(B, ps[:, B, 3 * P:4 * P], KT, q["v"][:, j, :], True, True, [s2, s3, vv])
                    if b == 0:
                        st = p.cp(SA[:, hh, :], ps[:, B, 3 * P:4 * P], [m4])
                    else:
                        st = p.stt(SA[:, hh, :], SA[:, hh, :], pre[:, 8:9], ps[:, B, 3 * P:4 * P], ALU.mult, ALU.add, [m4, o1])
                    stateA[hh] = st
                    users.append(st)
                    bankX.done(i, [st])
                    ringK.done(x, [st, o1, m2, m3, qp])
                else:
                    bankX.done(i, [s3])
                    ringK.done(x, [o1, m2, m3, qp])
            sqv, o1v = q["sq"][:, 0:T], q["o1"][:, 0:T]
            a = p.act(sqv, po, ACT.Square, [o1, fr])
            i, xfr = bankX.take()
            m = p.mm(XB[i], ps[:, XB[i], 0:T], C["ones"], sqv, True, True, [a, xfr])
            b1 = p.act(sqv, ps[:, XB[i], 0:T], ACT.Ln, [m], bias=eps, scale=1.0 / P)
            bankX.done(i, [b1])
            b2 = p.act(sqv, sqv, ACT.Exp, [b1], scale=-0.5)
            b3 = p.stt(o1v, po, V("onorm", hh, 1), sg[:, 2, :], ALU.mult, ALU.mult, [gs, o1, a, fr])
            bankO.done(o, [b3])
            b4 = p.tt(oT[:, hh, 0:T], o1v, sqv, ALU.mult, [b2, b3, free["oT"]])
            ringH.done(k, [b4, users])
            done.append(b4)
        free["oT"] = None
        return done

    c32 = X[1][:, 0:256].rearrange("p (a b) -> p a b", a=8)
    a = silu_of(X[1][:, 256:264], V("c"), X[1][:, 264:272], [ld_v])
    c32_ok = p.cp(c32, bc(X[1][:, 256:264].rearrange("p (a b) -> p a b", b=1), 8, 32), [a])
    mod0 = []
    for G in range(3):
        r = matvec_pe("ada0", G, c32, mod[0][:, 16 * G:16 * G + 16], V("ada_b0", 16 * G, 16), c32_ok)
        mod0 += [r, r]
    free["X1"] = free["V"]
    late = []
    kvm_s = matvec("kvada", 0, 0, kvm[:, :], V("kv_b"))
    mod1 = [modvec(1, k) for k in range(6)]
    mv = [matvec("ada_2", 8 * k, 1, mod2[:, 8 * k:8 * k + 8], V("b_2", 8 * k, 8)) for k in range(3)]
    free["acc"] = list(crow_users[0])
    usersA, usersC, usersE = [], [], []
    at0 = len(p.steps)
    lb_ready = hgrn_setup()
    usersA += p.steps[at0:]
    for n, chunk in enumerate(CHUNKS_A):
        if n == 0:
            (sh, scl, g1, sh2, sc2, g2) = mod0
            g_a = gain(0, mod[0][:, 8:16], V("mix0"), scl)
        hn_again()
        hr1 = []
        for j, b in enumerate(chunk):
            a = normed(h[:, b, :], [hw[b]])
            hr[b].append(a)
            trs, evs = spread(a, j, [(hn, gT[:, 0, :], mod[0][:, 0:8], [g_a, sh, free["hn"]])])
            free["xs"] = trs
            hr1 += evs[0]
        at0 = len(p.steps)
        done = hgrn(chunk, hr1, lb_ready)
        usersA += p.steps[at0:]
        if n == 0:
            r1 = broadcast_row(0, mod[0][:, 16:24], g1)
        w2 = [Weights("wout", 0), Weights("wout", 1)]
        used = []
        for j, b in enumerate(chunk):
            used += add_mix(w2, b, j, oT, done, 0, r1)
        for w in w2:
            w.done()
        free["oT"] = used
        if n == 0:
            g_f = gain(1, mod[0][:, 32:40], V("ffn0"), sc2)
        hn_again()
        hr2 = []
        for j, b in enumerate(chunk):
            a = normed(h[:, b, :], [hw[b]])
            hr[b].append(a)
            trs, evs = spread(a, j, [(hn, gT[:, 1, :], mod[0][:, 24:32], [g_f, sh2, free["hn"]])])
            free["xs"] = trs
            hr2 += evs[0]
        select(0, chunk, hr2)
        keep_rows(chunk, hr2)
        if n == 0:
            r2 = broadcast_row(1, mod[0][:, 40:48], g2)
        if upto == "A":
            continue
        experts(0, chunk, 1, r2)
        if n == 0:
            row_users[2] += crow_users[1]
        late = []

    tC, atC = region(COMMON)
    kT, vS, qT = tC(NH, S), tC(NB, D), tC(NH, TM)
    cset = [{k: tC(S) for k in ("e", "lk", "a")} for _ in range(2)]
    ringC = Ring(2)

    def attend(chunk, kv_done, q_done):
        done, used = [], []
        for j, b in enumerate(chunk):
            W = (b + 1) * P
            for hh in range(NH):
                c, fr = ringC.take()
                e, lk, a = (cset[c][k][:, 0:W] for k in ("e", "lk", "a"))
                i, bfr = bankD.take()
                B = DB[i]
                z = ps[:, B, 0:W]
                qh = qT[:, hh, j * P:(j + 1) * P]
                for n in range(b + 1):
                    m1 = p.mm(B, z[:, n * P:(n + 1) * P], kT[:, hh, n * P:(n + 1) * P], qh, n == 0, True,
                              [kv_done, q_done, bfr], True)
                a1 = p.act(e, z, ACT.Abs, [m1, fr])
                a2 = p.act(e, e, ACT.Exp, [a1], scale=-1.0)
                a3 = p.act(e, e, ACT.Ln, [a2], bias=one)
                d1 = p.stt(lk, z, 0.0, e, ALU.max, ALU.add, [a3, fr])
                d2 = p.tt(lk[:, b * P:W], lk[:, b * P:W], C["strict"], ALU.mult, [d1])
                for n in range(b + 1):
                    m2 = p.mm(B, z[:, n * P:(n + 1) * P], C["ntri"], lk[:, n * P:(n + 1) * P], False, True, [d2, d1], True)
                for n in range(1, b + 1):
                    m2 = p.mm(B, z[:, 0:n * P].rearrange("p (a b) -> p a b", b=P), C["nones"],
                              bc(lk[:, n * P:(n + 1) * P].rearrange("p (a b) -> p a b", a=1), n, P), False, True, [d2, d1], True)
                m2 = p.mm(B, z[:, b * P:W], C["ident"], C["negm"], False, True, [d1], True)
                a4 = p.act(a, z, ACT.Exp, [m2, fr])
                bankD.done(i, [a4])
                x, xfr = bankX.take()
                po = ps[:, XB[x], 0:P]
                for n in range(b + 1):
                    m3 = p.mm(XB[x], po, vS[:, n, hh * P:(hh + 1) * P], a[:, n * P:(n + 1) * P], n == 0, n == b, [a4, xfr])
                o = p.act(oT[:, hh, j * P:(j + 1) * P], po, ACT.Identity, [m3, free["oT"]])
                bankX.done(x, [o])
                ringC.done(c, [m3, m2])
                done.append(o)
                used.append(m1)
        return done, used

    gate_c = None
    if upto in "CDE":
        gate_c = p.fill(spot[:, :], 0.0, [usersA])
        g_kv = gain(2, kvm[:, 8:16], V("kv_g"), kvm_s)
        (sh, scl, g1, sh2, sc2, g2) = mod1
        g_a = gain(3, mod[1][:, 8:16], V("mix1"), scl)
    kv_done, qused = [], []
    for n, chunk in enumerate(CHUNKS_C if upto in "CDE" else []):
        T = P * len(chunk)
        t0 = chunk[0] * P
        at0 = len(p.steps)
        hn_again()
        rk, rq = [], []
        for j, b in enumerate(chunk):
            a = normed(h[:, b, :], [hw[b]])
            hr[b].append(a)
            trs, evs = spread(a, j, [(hn, gT[:, 2, :], kvm[:, 0:8], [g_kv, kvm_s, free["hn"]]),
                                     (oT, gT[:, 3, :], mod[1][:, 0:8], [g_a, sh, free["oT"]])])
            free["xs"] = trs
            rk += evs[0]
            rq += evs[1]
        for g in range(2):
            w = Weights("kvw", g)
            for m in range(4):
                i, last = project(w, m, T, rk)
                hn_users.append(last)
                e = p.act(kT[:, 4 * g + m, t0:t0 + T], ps[:, DB[i], 0:T], ACT.Identity, [last, gate_c])
                bankD.done(i, [e])
                kv_done.append(e)
            w.done()
        for g in range(2):
            w = Weights("kvw", 2 + g)
            for j, b in enumerate(chunk):
                i, fr = bankD.take()
                for kc in range(KC):
                    last = p.mm(DB[i], ps[:, DB[i], :], hn[:, kc, j * P:(j + 1) * P], w.at(kc, 0, 512), kc == 0, kc == KC - 1,
                                [rk, w.load(kc), fr])
                    w.use(kc, last)
                hn_users.append(last)
                e = p.act(vS[:, b, g * 512:g * 512 + 512], ps[:, DB[i], :], ACT.Identity, [last, gate_c])
                bankD.done(i, [e])
                kv_done.append(e)
            w.done()
        q_done, qin = [], []
        for g in range(2):
            w = Weights("sbq", g)
            for m in range(4):
                i, last = project(w, m, T, rq, oT)
                qin.append(last)
                e = p.act(qT[:, 4 * g + m, 0:T], ps[:, DB[i], 0:T], ACT.Identity, [last, gate_c, qused], scale=float(P) ** -0.5)
                bankD.done(i, [e])
                q_done.append(e)
            w.done()
        free["oT"] = qin
        done, qused = attend(chunk, kv_done, q_done)
        free["oT"] = None
        if n == 0:
            r1 = broadcast_row(0, mod[1][:, 16:24], g1)
        w2 = [Weights("sbo", 0), Weights("sbo", 1)]
        used = []
        for j, b in enumerate(chunk):
            used += add_mix(w2, b, j, oT, done, 0, r1)
        for w in w2:
            w.done()
        free["oT"] = used
        if n == 0:
            g_f = gain(4, mod[1][:, 32:40], V("ffn1"), sc2)
        hn_again()
        hr2 = []
        for j, b in enumerate(chunk):
            a = normed(h[:, b, :], [hw[b]])
            hr[b].append(a)
            trs, evs = spread(a, j, [(hn, gT[:, 4, :], mod[1][:, 24:32], [g_f, sh2, free["hn"]])])
            free["xs"] = trs
            hr2 += evs[0]
        select(1, chunk, hr2)
        keep_rows(chunk, hr2)
        if n == 0:
            r2 = broadcast_row(2, mod[1][:, 40:48], g2)
        usersC += p.steps[at0:]
        if upto == "C":
            continue
        experts(1, chunk, 2, r2)

    tE, atE = region(0)
    cste = tE(cc["tri64"] * len(CONSTS_E))
    CE = {k: cste[:, n * P:(n + 1) * P] for n, k in enumerate(CONSTS_E)}
    SG = tE(4, P)
    carry = tE(12, 3)
    ckvT, ckvR, ikT, toep = tE(S), tE(NB, P), tE(S), tE(4, 256)
    cin, sgE = tE(3, TM + 3), tE(3, TM)
    Q2, K2, V2 = tE(4, TM), tE(4, TM), tE(4, TM)
    MA = [tE(4, P) for _ in range(9)]
    XN = [m.rearrange("p (a b) c -> p a b c", a=2) for m in MA[3:5]]
    iqT, qbT = tE(4, TM), tE(4, TM)
    score, Wk, lg0, pT = tE(S), tE(S), tE(S), tE(S)
    lg1 = tE(S)
    sm = tE(96)
    ob = cst[:, cc["ident"] + cc["ones"] + cc["cols"] + cc["strict"] + 512:][:, 0:P]
    abr, nea = sm[:, 0:8], sm[:, 8:12]
    bawb = [sm[:, 80:96], sm[:, 16:32]]
    sc4 = [sm[:, 32 + 4 * k:36 + 4 * k] for k in range(8)]
    glc = sm[:, 64:72].rearrange("p (a b) -> p a b", a=4)
    m8 = sm[:, 72:80]
    at = cc["ident"] + cc["ones"] + cc["cols"] + cc["strict"]
    wuv = cst[:, at:at + 512].rearrange("p (a b) -> p a b", a=4)

    def b4(ap):
        return bc(ap.rearrange("p (a b) -> p a b", a=1), 4, P)

    def b2(ap):
        return bc(ap.rearrange("p (a b) -> p a b", a=1), 2, P)

    def b4c(ap):
        return bc(ap.rearrange("p (a b) -> p a b", b=1), 4, P)

    def gated_heads(chunk, rh):
        T = P * len(chunk)
        out_ = []
        for hh in range(4):
            w = Weights("win2", hh)
            ins, rd = [], []
            for ty in range(3):
                i, last = project(w, ty, T, rh)
                hn_users.append(last)
                ins.append(p.act(cin[:, ty, 3:3 + T], ps[:, DB[i], 0:T], ACT.Identity, [last, E["cin"], gate_e]))
                bankD.done(i, [ins[-1]])
            cr = p.cp(cin[:, :, 0:3], carry[:, 3 * hh:3 * hh + 3, :], [E["carry"], E["cin"]])
            rel = []
            cw = [V("conv", 12 * tap, 12) for tap in range(4)]
            for ty, dst in enumerate((Q2, K2, V2)):
                tile_ = 4 * ty + hh
                d = dst[:, hh, 0:T]
                a = p.act(d, cin[:, ty, 0:T], ACT.Identity, [ins[ty], cr, E["QKV"]], scale=cw[0][:, tile_:tile_ + 1])
                for tap in range(1, 4):
                    a = p.stt(d, cin[:, ty, tap:tap + T], cw[tap][:, tile_:tile_ + 1], d, ALU.mult, ALU.add, [a])
                rel.append(a)
            ca = p.cp(carry[:, 3 * hh:3 * hh + 3, :], cin[:, :, T:T + 3], [ins, cr])
            E["cin"], E["carry"] = rel + [ca], [ca]
            sgs = []
            for ty, dst in enumerate((Q2, K2, V2)):
                s_ = sgE[:, ty, 0:T]
                _, a = sigmoid_ps(s_, dst[:, hh, 0:T], [rel[ty], E["sgE"]])
                sgs.append(p.tt(dst[:, hh, 0:T], dst[:, hh, 0:T], s_, ALU.mult, [a]))
            sq = [p.act(sgE[:, ty, 0:T], dst[:, hh, 0:T], ACT.Square, [sgs[ty]]) for ty, dst in enumerate((Q2, K2))]
            i, fr = bankD.take()
            B = DB[i]
            mq = p.mm(B, ps[:, B, 0:T], C["ones"], sgE[:, 0, 0:T], True, True, [sq[0], fr])
            mk = p.mm(B, ps[:, B, TM:TM + T], C["ones"], sgE[:, 1, 0:T], True, True, [sq[1], fr])
            lq = p.act(sgE[:, 0, 0:T], ps[:, B, 0:T], ACT.Ln, [mq, mk], bias=eps)
            lk = p.act(sgE[:, 1, 0:T], ps[:, B, TM:TM + T], ACT.Ln, [mk], bias=eps)
            bankD.done(i, [lq, lk])
            lq = p.act(sgE[:, 0, 0:T], sgE[:, 0, 0:T], ACT.Exp, [lq], bias=nhl, scale=-0.5)
            lk = p.act(sgE[:, 1, 0:T], sgE[:, 1, 0:T], ACT.Exp, [lk], scale=-0.5)
            aq = p.tt(Q2[:, hh, 0:T], Q2[:, hh, 0:T], sgE[:, 0, 0:T], ALU.mult, [lq])
            ak = p.tt(K2[:, hh, 0:T], K2[:, hh, 0:T], sgE[:, 1, 0:T], ALU.mult, [lk])
            E["sgE"] = [aq, ak, sgs[2]]
            out_ += [aq, ak, sgs[2]]
            i, last = project(w, 3, T, rh)
            hn_users.append(last)
            _, a = sigmoid_ps(oT[:, hh, 0:T], ps[:, DB[i], 0:T], [last, free["oT"]])
            a = p.tt(oT[:, hh, 0:T], oT[:, hh, 0:T], ps[:, DB[i], 0:T], ALU.mult, [a])
            bankD.done(i, [a])
            out_.append(a)
            w.done()
        return out_

    def gated_block(b, j, heads, bw):
        sl = slice(j * P, (j + 1) * P)
        A0, A1, A2, _, _, A5, A6, A7, A8 = MA
        beta, gg, eg, el, be, x0, x1, gcl = sc4
        fr = E["blk"]
        baw = bawb[j]

        def four(mms, after):
            i, bfr = bankD.take()
            for q in range(4):
                o_, l_, r_ = mms(q, ps[:, DB[i], q * P:(q + 1) * P])
                last = p.mm(DB[i], o_, l_, r_, True, True, [after, bfr])
            return i, ps[:, DB[i], :].rearrange("p (a b) -> p a b", a=4), last

        a = p.act(beta, baw[:, 0:4], ACT.Exp, [bw, fr], scale=-1.0)
        a = p.ts(beta, beta, 1.0, None, ALU.add, None, [a])
        beta_ok = p.vec(lambda e: e.reciprocal(beta, beta), 4, [a], 8.0)
        a = p.tt(x0, baw[:, 4:8], abr[:, 4:8], ALU.add, [bw, abr_ok, fr])
        c = p.act(x1, x0, ACT.Abs, [a])
        c = p.act(x1, x1, ACT.Exp, [c], scale=-1.0)
        c = p.act(x1, x1, ACT.Ln, [c], bias=one)
        c = p.stt(x1, x0, 0.0, x1, ALU.max, ALU.add, [c])
        g_ok = p.tt(gg, x1, nea, ALU.mult, [c, nea_ok])
        i, bfr = bankD.take()
        B = DB[i]
        m = p.mm(B, ps[:, B, 0:4], CE["tri64"], gg, True, True, [g_ok, cste_ok, bfr])
        m = p.mm(B, ps[:, B, 4:8], CE["sup64"], gg, True, True, [g_ok])
        e1_ = p.act(eg, ps[:, B, 0:4], ACT.Exp, [m])
        e2_ = p.act(el, ps[:, B, 4:8], ACT.Exp, [m])
        bankD.done(i, [e1_, e2_])
        be_ok = p.tt(be, beta, eg, ALU.mult, [e1_, beta_ok])
        a2_ = [p.act(A2[:, q, :], CE["tri64"], ACT.Identity, [g_ok, cste_ok, fr], scale=gg[:, q:q + 1]) for q in range(4)]
        i, bfr = bankD.take()
        PR = ps[:, DB[i], :].rearrange("p (a b) -> p a b", a=4)
        m = p.mm(DB[i], ps[:, DB[i], :], C["ones"], A2.rearrange("p a b -> p (a b)"), True, True, [a2_, bfr])
        eg_ok = p.act(A6, PR, ACT.Exp, [m, fr])
        bankD.done(i, [eg_ok])
        i, bfr = bankD.take()
        md = p.mm(DB[i], ps[:, DB[i], :], CE["sup64"], A2.rearrange("p a b -> p (a b)"), True, True, [a2_, bfr])
        a = p.act(A0, ps[:, DB[i], :].rearrange("p (a b) -> p a b", a=4), ACT.Exp, [md, fr])
        bankD.done(i, [a])
        a1_ = [p.act(A1[:, q, :], C["ident"], ACT.Identity, [beta_ok, fr, ld_c], scale=beta[:, q:q + 1]) for q in range(4)]
        i, bfr = bankD.take()
        PBt = ps[:, DB[i], :].rearrange("p (a b) -> p a b", a=4)
        mb = p.mm(DB[i], ps[:, DB[i], :], CE["sup64"], A1.rearrange("p a b -> p (a b)"), True, True, [a1_, cste_ok, bfr])
        ib = i
        i, pk, m = four(lambda q, o: (o, K2[:, q, sl], K2[:, q, sl]), [heads])
        c = p.tt(A1, pk, A0, ALU.mult, [m, a, mb])
        bankD.done(i, [c])
        lt = p.tt(A1, A1, PBt, ALU.mult, [c, mb])
        bankD.done(ib, [lt])
        dec = p.tt(A0, A0, b4(CE["tri64"]), ALU.mult, [c])
        i, bfr = bankD.take()
        for q in range(4):
            m = p.tr(DB[i], ps[:, DB[i], q * P:(q + 1) * P], A1[:, q, :], C["ident"], [lt, bfr])
        xn, y, ng = [None] * 2, [None] * 2, []
        for pr in range(2):
            hs = slice(2 * pr, 2 * pr + 2)
            a = p.act(XN[pr][:, 0, :, :], ps[:, DB[i], 256 * pr:256 * pr + 256].rearrange("p (a b) -> p a b", a=2),
                      ACT.Identity, [m, fr], scale=-1.0)
            ng.append(a)
            c = p.act(XN[pr][:, 1, :, :], A1[:, hs, :], ACT.Identity, [lt, fr], scale=-1.0)
            xn[pr] = [p.vec(lambda e, o=XN[pr][:, k, :, :], m_=b2(CE[n]).bitcast(U32), d_=b2(C["ident"]): e.copy_predicated(o, m_, d_),
                            256, [a, c, cste_ok]) for k, n in enumerate(("n1", "n1t"))]
        bankD.done(i, ng)
        i, pq, m = four(lambda q, o: (o, K2[:, q, sl], Q2[:, q, sl]), [heads])
        at_ok = p.tt(A5, pq, A0, ALU.mult, [m, dec, fr])
        bankD.done(i, [at_ok])
        qg_ok = p.tt(Q2[:, :, sl], Q2[:, :, sl], A6, ALU.mult, [m, eg_ok])
        gl_ok = p.cp(glc, A6.rearrange("p a (c t) -> p a c t", t=64)[:, :, :, 63], [eg_ok, fr])
        y_free = [[at_ok], [at_ok]]
        for lev in (2, 4, 8, 16, 32):
            for pr in range(2):
                i, bfr = bankD.take()
                B = DB[i]
                for q in range(2):
                    m = p.mm(B, ps[:, B, q * P:(q + 1) * P], A1[:, 2 * pr + q, :], XN[pr][:, 0, q, :], True, True, [xn[pr], bfr])
                y[pr] = p.tt(A0[:, 2 * pr:2 * pr + 2, :], ps[:, B, 0:256].rearrange("p (a b) -> p a b", a=2),
                             b2(CE[f"m{lev}"]), ALU.mult, [m, y_free[pr]])
                bankD.done(i, [y[pr]])
            for pr in range(2):
                i, bfr = bankD.take()
                B = DB[i]
                lo = 0 if lev < 32 else 1
                for q in range(2):
                    Y = A0[:, 2 * pr + q, :]
                    if lev < 32:
                        m = p.mm(B, ps[:, B, q * P:(q + 1) * P], XN[pr][:, 1, q, :], Y, True, True, [y[pr], bfr])
                    m = p.mm(B, ps[:, B, 256 + q * P:256 + (q + 1) * P], Y, XN[pr][:, 1, q, :], True, True, [y[pr], bfr])
                xn[pr] = [p.tt(XN[pr][:, lo:2, :, :].rearrange("p a b c -> p (a b c)"),
                               XN[pr][:, lo:2, :, :].rearrange("p a b c -> p (a b c)"), ps[:, B, 256 * lo:512], ALU.subtract, [m])]
                bankD.done(i, xn[pr])
                y_free[pr] = [m]
        n_ok = xn
        i, bfr = bankD.take()
        for q in range(4):
            m = p.tr(DB[i], ps[:, DB[i], q * P:(q + 1) * P], K2[:, q, sl], C["ident"], [heads, bfr])
        pk = ps[:, DB[i], :].rearrange("p (a b) -> p a b", a=4)
        kb_ok = [p.act(A6[:, q, :], pk[:, q, :], ACT.Identity, [m, be_ok, gl_ok, qg_ok], scale=be[:, q:q + 1]) for q in range(4)]
        kg_ok = [p.act(A7[:, q, :], pk[:, q, :], ACT.Identity, [m, e2_, fr], scale=el[:, q:q + 1]) for q in range(4)]
        bankD.done(i, kb_ok + kg_ok)
        i, bfr = bankD.take()
        for q in range(4):
            m = p.tr(DB[i], ps[:, DB[i], q * P:(q + 1) * P], V2[:, q, sl], C["ident"], [heads, bfr])
        vb_ok = [p.act(A8[:, q, :], ps[:, DB[i], q * P:(q + 1) * P], ACT.Identity, [m, beta_ok, fr], scale=beta[:, q:q + 1])
                 for q in range(4)]
        bankD.done(i, vb_ok)
        N = lambda q: XN[q // 2][:, 1, q % 2, :]
        i, pw, m = four(lambda q, o: (o, A6[:, q, :], N(q)), [kb_ok, n_ok])
        w_ok = p.act(A2, pw, ACT.Identity, [m, xn, md], scale=-1.0)
        bankD.done(i, [w_ok])
        o, ofr = bankO.take()
        PO = ps[:, OB[o], :].rearrange("p (a b) -> p a b", a=4)
        mo = None
        for c in range(2):
            r = slice(64 * c, 64 * c + 64)
            qsl = slice(j * P + 64 * c, j * P + 64 * c + 64)
            first = b == 0 and c == 0
            i, bfr = bankD.take()
            B = DB[i]
            for q in range(4):
                m = p.mm(B, ps[r, B, q * P:(q + 1) * P], N(q)[:, r], A8[:, q, :], True, first, [vb_ok, n_ok, bfr])
                if not first:
                    m = p.mm(B, ps[r, B, q * P:(q + 1) * P], A2[:, q, r], SG[:, q, :], False, True, [w_ok, E["S"]])
            vn = p.act(A0[r, :, :], ps[r, B, :].rearrange("p (a b) -> p a b", a=4), ACT.Identity, [m, y_free])
            bankD.done(i, [vn])
            for q in range(4):
                m = p.mm(OB[o], PO[:, q, r], A0[r, q, :], A5[r, q, r], True, first, [vn, at_ok, ofr, mo])
                if not first:
                    m = p.mm(OB[o], PO[:, q, r], SG[:, q, :], Q2[:, q, qsl], False, True, [qg_ok, E["S"]])
            mo = m
            if b == NB - 1 and c == 1:
                break
            i, bfr = bankD.take()
            B = DB[i]
            new = []
            for q in range(4):
                m = p.mm(B, ps[:, B, q * P:(q + 1) * P], A7[r, q, :], A0[r, q, :], True, True, [kg_ok, vn, bfr])
            for q in range(4):
                if first:
                    new.append(p.cp(SG[:, q, :], ps[:, B, q * P:(q + 1) * P], [m, gate_e]))
                else:
                    new.append(p.stt(SG[:, q, :], SG[:, q, :], glc[:, q, c:c + 1], ps[:, B, q * P:(q + 1) * P],
                                     ALU.mult, ALU.add, [m, mo, gl_ok]))
            bankD.done(i, new)
            E["S"] = new
        a = p.act(A0, PO, ACT.Square, [mo, E["S"], y_free])
        i, bfr = bankD.take()
        m = p.mm(DB[i], ps[:, DB[i], :], C["ones"], A0.rearrange("p a b -> p (a b)"), True, True, [a, bfr])
        c = p.act(A0, ps[:, DB[i], :].rearrange("p (a b) -> p a b", a=4), ACT.Ln, [m], bias=eps, scale=1.0 / P)
        bankD.done(i, [c])
        c = p.act(A0, A0, ACT.Exp, [c], scale=-0.5)
        d = p.stt(A0, PO, V("gdn"), A0, ALU.mult, ALU.mult, [c, mo])
        bankO.done(o, [d])
        d = p.tt(oT[:, 0:4, sl], oT[:, 0:4, sl], A0, ALU.mult, [d, heads])
        E["blk"] = [d, mo, E["S"]]
        return [d], [mo, m, qg_ok]

    def sparse_prep(chunk, rh):
        T = P * len(chunk)
        t0 = chunk[0] * P
        out_ = []
        w = Weights("win2", 7)
        i, last = project(w, 0, T, rh)
        hn_users.append(last)
        a = p.act(pT[:, 0:T], ps[:, DB[i], 0:T], ACT.Square, [last, E["pT"], gate_e])
        x, xfr = bankX.take()
        m = p.mm(XB[x], ps[:, XB[x], 0:T], C["ones"], pT[:, 0:T], True, True, [a, xfr])
        c = p.act(pT[:, 0:T], ps[:, XB[x], 0:T], ACT.Ln, [m], bias=eps, scale=1.0 / P)
        bankX.done(x, [c])
        c = p.act(pT[:, 0:T], pT[:, 0:T], ACT.Exp, [c], scale=-0.5)
        kt = p.stt(ckvT[:, t0:t0 + T], ps[:, DB[i], 0:T], V("gkv"), pT[:, 0:T], ALU.mult, ALU.mult, [c, last, a, gate_e])
        bankD.done(i, [kt])
        E["pT"] = [kt]
        out_.append(kt)
        x, xfr = bankX.take()
        for j, b in enumerate(chunk):
            m = p.tr(XB[x], ps[:, XB[x], j * P:(j + 1) * P], ckvT[:, b * P:(b + 1) * P], C["ident"], [kt, xfr])
        c = p.act(ckvR[:, chunk[0]:chunk[-1] + 1, :], ps[:, XB[x], 0:T].rearrange("p (a b) -> p a b", b=P), ACT.Identity,
                  [m, gate_e])
        bankX.done(x, [c])
        out_.append(c)
        i, last = project(w, 1, T, rh)
        hn_users.append(last)
        c = p.act(ikT[:, t0:t0 + T], ps[:, DB[i], 0:T], ACT.Identity, [last, gate_e])
        bankD.done(i, [c])
        out_.append(c)
        bws = []
        for j, b in enumerate(chunk):
            i, bfr = bankD.take()
            for kc in range(KC):
                last = p.mm(DB[i], ps[:, DB[i], 0:16], hn[:, kc, j * P:(j + 1) * P], w.at(kc, 2 * P, 16), kc == 0, kc == KC - 1,
                            [rh, w.load(kc), bfr])
                w.use(kc, last)
            hn_users.append(last)
            c1 = p.act(bawb[j][:, 0:8], ps[:, DB[i], 0:8], ACT.Identity, [last, E["baw"]])
            c2 = p.act(bawb[j][:, 8:16], ps[:, DB[i], 8:16], ACT.Identity, [last, E["baw"]], scale=8 ** -0.5 * 64 ** -0.5)
            bankD.done(i, [c1, c2])
            bws.append([c1, c2])
        w.done()
        w = Weights("win2", 6)
        for m in range(4):
            i, last = project(w, m, T, rh)
            hn_users.append(last)
            c = p.act(iqT[:, m, 0:T], ps[:, DB[i], 0:T], ACT.Identity, [last, gate_e, E["iq"]])
            bankD.done(i, [c])
            out_.append(c)
        w.done()
        return out_, bws

    def sparse_rest(chunk, rh):
        T = P * len(chunk)
        out_ = []
        w = Weights("win2", 4)
        for m in range(4):
            i, last = project(w, m, T, rh)
            hn_users.append(last)
            c = p.act(qbT[:, m, 0:T], ps[:, DB[i], 0:T], ACT.Identity, [last, gate_e, E["qb"]])
            bankD.done(i, [c])
            out_.append(c)
        w.done()
        w = Weights("win2", 5)
        for m in range(4):
            i, last = project(w, m, T, rh)
            hn_users.append(last)
            _, a = sigmoid_ps(oT[:, 4 + m, 0:T], ps[:, DB[i], 0:T], [last, free["oT"]])
            a = p.tt(oT[:, 4 + m, 0:T], oT[:, 4 + m, 0:T], ps[:, DB[i], 0:T], ALU.mult, [a])
            bankD.done(i, [a])
            out_.append(a)
        w.done()
        return out_

    def sparse_block(b, j, prep, prep2, bw):
        W = (b + 1) * P
        sl = slice(j * P, (j + 1) * P)
        lgs = (lg0, lg1)
        if b == 0:
            m_ok = p.ts(Wk[:, 0:P], C["strict"], -BIG, None, ALU.mult, None, [cste_ok, E["Wk"]])
        else:
            iwv = bawb[j][:, 8:16]
            prev = E["score"]
            iqs = []
            for hh in range(8):
                x, xfr = bankX.take()
                half = slice(64 * (hh % 2), 64 * (hh % 2) + 64)
                m = p.mm(XB[x], ps[:, XB[x], 0:W], iqT[half, hh // 2, sl], ikT[half, 0:W], True, True, [prep, xfr])
                iqs.append(m)
                lb = lgs[hh % 2][:, 0:W]
                r = p.act(lb, ps[:, XB[x], 0:W], ACT.Relu, [m, E["lg"][hh % 2]])
                bankX.done(x, [r])
                if hh == 0:
                    s_ = p.ts(score[:, 0:W], lb, iwv[:, 0:1], None, ALU.mult, None, [r, bw, prev])
                else:
                    s_ = p.stt(score[:, 0:W], lb, iwv[:, hh:hh + 1], score[:, 0:W], ALU.mult, ALU.add, [r, s_])
                E["lg"][hh % 2] = [s_]
            E["iq"] = iqs
            dg = slice(b * P, W)
            a = p.stt(score[:, dg], C["strict"], -BIG, score[:, dg], ALU.mult, ALU.add, [s_, ld_c])
            src = score[:, 0:W]
            for rnd in range(16):
                a = p.vec(lambda e, s=src: e.max(m8, s), W, [a, E["Wk"] if rnd == 0 else None])
                a = p.vec(lambda e, s=src: e.match_replace(Wk[:, 0:W], m8, s, -3.3e38), W, [a, E["Wk"] if rnd == 0 else None])
                src = Wk[:, 0:W]
            E["score"] = [a]
            m_ok = p.ts(Wk[:, 0:W], Wk[:, 0:W], -3.15e38, -BIG, ALU.is_ge, ALU.mult, [a])
        near = min(W, 256)
        rd = []
        res, qbs = [], []
        for hh in range(4):
            x, xfr = bankX.take()
            m = p.mm(XB[x], ps[:, XB[x], 0:W], qbT[:, hh, sl], ckvT[:, 0:W], True, True, [prep, prep2, xfr])
            qbs.append(m)
            lgt = lgs[hh % 2]
            lb = lgt[:, 0:W]
            s, sfr = ringS.take()
            mx, mx2, sm_ = (small[:, s, k:k + 1] for k in range(3))
            nl, tl = lgt[:, W - near:W], toep[:, hh, 256 - near:256]
            a = p.stt(lb, ps[:, XB[x], 0:W], float(P) ** -0.5, Wk[:, 0:W], ALU.mult, ALU.add, [m, m_ok, E["lg"][hh % 2]])
            rd.append(a)
            bankX.done(x, [a])
            a1 = p.vec(lambda e, n=nl, t_=tl, o=mx: e.tensor_tensor_reduce(n, n, t_, 1.0, -BIG, ALU.add, ALU.max, o),
                       near, [a, toep_ok, sfr])
            if W > near:
                fl = lgt[:, 0:W - near]
                a2 = p.vec(lambda e, f=fl, t_=toep[:, hh, 0:1], o=mx2: e.tensor_scalar(f, f, t_, None, ALU.add, ALU.max, accum_out=o),
                           W - near, [a, toep_ok, sfr])
                a1 = p.tt(mx, mx, mx2, ALU.max, [a1, a2])
            a = p.ts(mx, mx, -1.0, None, ALU.mult, None, [a1])
            a = p.act(lb, lb, ACT.Exp, [a], bias=mx, accum=sm_)
            c = p.vec(lambda e, o=sm_: e.reciprocal(o, o), 1, [a], 8.0)
            a = p.act(lb, lb, ACT.Identity, [a, c], scale=sm_)
            ringS.done(s, [a])
            x, xfr = bankX.take()
            for n in range(b + 1):
                m = p.tr(XB[x], ps[:, XB[x], n * P:(n + 1) * P], lgt[:, n * P:(n + 1) * P], C["ident"], [a, xfr])
            E["lg"][hh % 2] = [m]
            c = p.act(pT[:, 0:W], ps[:, XB[x], 0:W], ACT.Identity, [m, E["pT"]])
            bankX.done(x, [c])
            x, xfr = bankX.take()
            B = XB[x]
            for n in range(b + 1):
                m = p.mm(B, ps[:, B, 0:P], ckvR[:, n, :], pT[:, n * P:(n + 1) * P], n == 0, n == b, [c, prep, xfr])
            c = p.act(ob, ps[:, B, 0:P], ACT.Identity, [m, E["ob"]])
            E["pT"] = [m]
            m = p.mm(B, ps[:, B, P:2 * P], wuv[:, hh, :], ob, True, True, [c, wuv_ok])
            E["ob"] = [m]
            c = p.tt(oT[:, 4 + hh, sl], oT[:, 4 + hh, sl], ps[:, B, P:2 * P], ALU.mult, [m, prep2])
            bankX.done(x, [c])
            res.append(c)
        E["Wk"] = rd
        E["qb"] = qbs
        return res

    def finish(b, j, w2, after):
        s, sfr = ringS.take()
        c = [small[:, s, k:k + 1] for k in range(3)]
        banks, lasts, sqs = [], [], []
        for n in range(2):
            i, fr = bankD.take()
            for kc in range(KC):
                last = p.mm(DB[i], ps[:, DB[i], :], oT[:, kc, j * P:(j + 1) * P], w2[n].at(kc, 0, 512), kc == 0, kc == KC - 1,
                            [after, w2[n].load(kc), fr])
                w2[n].use(kc, last)
            banks.append(i)
            lasts.append(last)
            sqs.append(p.act(X[0][:, n * 512:n * 512 + 512], ps[:, DB[i], :], ACT.Square, [last, sfr, free["X0"]], accum=c[n]))
        a = p.tt(c[2], c[0], c[1], ALU.add, sqs)
        a = p.act(c[2], c[2], ACT.Ln, [a], bias=eps, scale=1.0 / D)
        a = p.act(c[2], c[2], ACT.Exp, [a], scale=-0.5)
        new = []
        for n in range(2):
            half = slice(n * 512, n * 512 + 512)
            d = p.stt(X[0][:, half], ps[:, DB[banks[n]], :], c[2], row[1][:, half], ALU.mult, ALU.mult, [a, sqs, rp])
            bankD.done(banks[n], [d])
            new.append(p.tt(h[:, b, half], h[:, b, half], X[0][:, half], ALU.add, [d, hw[b], hr[b]]))
        ringS.done(s, new)
        free["X0"] = new
        hw[b], hr[b] = new, []
        return lasts

    E = {k: [] for k in ("cin", "carry", "QKV", "sgE", "blk", "S", "pT", "baw", "iq", "qb", "score", "Wk", "ob")}
    E["lg"] = [[], []]
    if upto == "E":
        gate_e = p.fill(spot[:, :], 0.0, [usersC, gate_c])
        me = [mark(f"m_e{k}") for k in range(7)]
        cste_ok = p.dma("sp", cste, t["cste"], me[0], P * cste.shape[1] * 4, [gate_e])
        wuv_ok = p.dma("sp", wuv, t["wuv"], me[1], P * 512 * 4, [gate_e])
        ab = t["ab"]
        ab_ok = p.dma("sp", abr, bass.AP(ab.tensor, ab.offset, [[0, P], [1, 8]]), me[2], P * 32, [gate_e])
        a = p.act(nea, abr[:, 0:4], ACT.Exp, [ab_ok])
        nea_ok = p.ts(nea, nea, -1.0, None, ALU.mult, None, [a])
        abr_ok = ab_ok
        E["carry"] = [p.fill(carry, 0.0, [gate_e])]
        hot_ok = p.dma("sp", Wk[0:32, 0:384], t["hot"], me[3], 32 * 384 * 4, [gate_e])
        rel_ok = p.dma("sp", score[0:32, 0:4], t["rel"], me[4], 32 * 16, [gate_e])
        x, xfr = bankX.take()
        m = p.mm(XB[x], ps[0:4, XB[x], 0:384], score[0:32, 0:4], Wk[0:32, 0:384], True, True, [hot_ok, rel_ok, xfr])
        c = p.cp(pT[0:4, 0:384], ps[0:4, XB[x], 0:384], [m, gate_e])
        bankX.done(x, [c])
        scr = nc.dram_tensor("bias_rows", (4, 384), F32).ap()
        scr_ok = p.dma("sp", scr, pT[0:4, 0:384], me[5], 4 * 384 * 4, [c])
        back = p.dma("sp", qbT.rearrange("p a b -> p (a b)").rearrange("p (a b) -> p a b", a=4),
                     bass.AP(scr.tensor, 0, [[1, P], [384, 4], [1, 256]]), me[6], P * 4096, [scr_ok, gate_e])
        flip_ok = p.dma("sp", lg0[:, 0:P], t["flip"], mark("m_e7"), P * P * 4, [gate_e])
        toep_ok, ms = [], []
        for half in range(2):
            x, xfr = bankX.take()
            mf = p.mm(XB[x], ps[:, XB[x], :], lg0[:, 0:P], qbT.rearrange("p a b -> p (a b)")[:, half * 512:half * 512 + 512],
                      True, True, [back, flip_ok, xfr])
            c2 = p.act(toep[:, 2 * half:2 * half + 2, :].rearrange("p a b -> p (a b)"), ps[:, XB[x], :], ACT.Identity, [mf])
            bankX.done(x, [c2])
            toep_ok.append(c2)
            ms.append(mf)
        E["qb"], E["lg"][0] = ms, ms
        E["pT"], E["Wk"], E["score"] = [scr_ok], [m], [m]
        g_p = gain(5, mod2[:, 8:16], V("pre"), mv[1])
        gp = p.tt(mod2[:, 16:24], mod2[:, 16:24], V("post"), ALU.mult, [mv[2]])
        rf = broadcast_row(0, V("fin"), ld_v)
        rp = broadcast_row(1, mod2[:, 16:24], gp)
        out_proj = None
        for chunk in CHUNKS_E:
            p.tag = f"E{chunk[0]} norm"
            hn_again()
            rh = []
            for j, b in enumerate(chunk):
                a, c, s = rms(h[:, b, :], xs[:, :], D, [hw[b], free["xs"]])
                a = p.stt(h[:, b, :], h[:, b, :], c, row[0][:, :], ALU.mult, ALU.mult, [a, rf, hw[b], hr[b]])
                ringS.done(s, [a])
                hw[b], hr[b], free["xs"] = [a], [], [a]
                a = normed(h[:, b, :], [hw[b]])
                hr[b].append(a)
                trs, evs = spread(a, j, [(hn, gT[:, 5, :], mod2[:, 0:8], [g_p, mv[0], free["hn"]])])
                free["xs"] = trs
                rh += evs[0]
            p.tag = f"E{chunk[0]} prep"
            prep, bws = sparse_prep(chunk, rh)
            if out_proj is not None:
                out_proj()
            p.tag = f"E{chunk[0]} heads"
            heads = gated_heads(chunk, rh)
            p.tag = f"E{chunk[0]} rest"
            prep2 = sparse_rest(chunk, rh)
            free["oT"] = None
            mixed = []
            bwu, qkvu = [], []
            for j, b in enumerate(chunk):
                p.tag = f"E{b} sparse"
                mixed += sparse_block(b, j, prep, prep2, bws[j])
                bwu.append(E["score"])
            for j, b in enumerate(chunk):
                p.tag = f"E{b} gated"
                r, u = gated_block(b, j, heads, bws[j])
                mixed += r
                qkvu += u
                bwu.append(E["blk"])
            E["baw"], E["QKV"] = bwu, qkvu
            def out_proj(chunk=chunk, mixed=mixed):
                p.tag = f"E{chunk[0]} out"
                w2 = [Weights("wout2", 0), Weights("wout2", 1)]
                used = []
                for j, b in enumerate(chunk):
                    used += finish(b, j, w2, mixed)
                for w in w2:
                    w.done()
                free["oT"] = used
        out_proj()

    m_o = [mark(f"m_o{b}") for b in range(NB)]
    last = []
    for b in range(NB):
        last.append(p.dma("sp", out[b * P:(b + 1) * P, :], h[:, b, :], m_o[b], P * D * 4, [hw[b]]))
    p.emit(nc, sems, last)
    ctx.close()
    return p


def tiles(w):
    k, n = w.shape
    g = -(-n // 512)
    if n % 512:
        w = np.concatenate([w, np.zeros((k, g * 512 - n), w.dtype)], axis=1)
    return np.ascontiguousarray(w.reshape(4, 2, P, g, 512).transpose(3, 0, 2, 1, 4))


def columns(v):
    return v.reshape(-1, P).T


def layout(i):
    i = {k: np.asarray(v) for k, v in i.items()}
    o = {"x": i["x"][0]}
    for l in range(2):
        o[f"pq{l}"] = tiles(i["peer_w_q"][l])
        o[f"sub{l}"] = np.ascontiguousarray(i["peer_subkeys"][l].reshape(8, P, P).transpose(2, 0, 1).reshape(P, 2, 512))
    w = i["hgrn_w_in"][0].reshape(D, 4, NH, P)
    o["win"] = tiles(np.stack([w[:, 0], w[:, 1], w[:, 3], w[:, 2]], axis=2).reshape(D, 4 * D))
    o["wout"] = tiles(i["hgrn_w_out"][0])
    o["ada0"] = tiles(i["ada_w"][0])
    o["ada1"] = i["ada_w"][1].T.reshape(-1, P, D)
    o["kvada"] = i["kv_ada_w"].T.reshape(-1, P, D)
    o["cc"] = np.concatenate([i["c"], i["c_2"]], axis=0)
    o["kvw"] = tiles(i["kv_w"])
    o["sbq"] = tiles(i["sb_w_q"][0])
    o["sbo"] = tiles(i["sb_w_out"][0])
    o["peer_u"] = i["peer_u"].reshape(-1, D)
    o["peer_v"] = i["peer_v"].reshape(-1, D)
    o["ada_2"] = i["w_ada_2"][0].T.reshape(-1, P, D)
    w = i["w_in_2"][0]
    qkv = w[:, 0:1536].reshape(D, 3, 4, P)
    z = w[:, 1536:2048].reshape(D, 1, 4, P)
    ba, qb, ckv, zb = w[:, 2048:2056], w[:, 2056:2568], w[:, 2568:2696], w[:, 2696:3208]
    iq, ik, iw = w[:, 3208:3720], w[:, 3720:3784], w[:, 3784:3792]
    heads = np.concatenate([qkv, z], axis=1).transpose(0, 2, 1, 3).reshape(D, 2048)
    o["win2"] = tiles(np.concatenate([heads, qb, zb, iq, ckv, ik, ik, ba, iw], axis=1))
    o["wout2"] = tiles(i["w_out_2"][0])
    o["wuv"] = np.ascontiguousarray(i["w_uv_2"][0].transpose(1, 0, 2))
    o["ab"] = np.stack([i["a_log_2"][0], i["dt_bias_2"][0]]).reshape(1, 8)
    o["rel"] = i["rel_bias_2"]
    v = {"c": i["c"], "ada_b0": i["ada_b"][0], "ada_b1": i["ada_b"][1],
         "mix0": i["norm_mix_g"][0], "mix1": i["norm_mix_g"][1], "ffn0": i["norm_ffn_g"][0], "ffn1": i["norm_ffn_g"][1],
         "lb0": i["hgrn_lb_logits"][0], "lb1": i["hgrn_lb_logits"][1], "onorm": i["hgrn_onorm_g"], "kv_b": i["kv_ada_b"],
         "kv_g": i["kv_norm_g"], "fin": i["final_norm_g"], "b_2": i["b_ada_2"], "pre": i["g_pre_2"], "post": i["g_post_2"],
         "conv": i["conv_w_2"], "gdn": i["g_gdn_2"], "gkv": i["g_kv_2"]}
    o["vecs"] = np.concatenate([columns(v[k]) for k in VECS], axis=1)
    o["cst"] = const_array(CONSTS)
    o["hot"] = constants()["hot"][0:32]
    o["flip"] = constants()["ident"][::-1]
    o["cste"] = const_array(CONSTS_E)
    return {k: np.ascontiguousarray(a) for k, a in o.items()}


def kernel(**inputs):
    import concourse.bacc as bacc
    from concourse.bass_utils import run_bass_kernel_spmd as run

    arrays = layout(inputs)
    nc = bacc.Bacc("TRN2", target_bir_lowering=False, num_devices=1)
    t = {k: nc.dram_tensor(f"in_{k}_dram", a.shape, mybir.dt.from_np(a.dtype), kind="ExternalInput").ap()
         for k, a in arrays.items()}
    out = nc.dram_tensor("out_0_dram", (S, D), F32, kind="ExternalOutput").ap()
    layer_stack_kernel(nc, t, out)
    r = run(nc, [{f"in_{k}_dram": a for k, a in arrays.items()}], core_ids=[0])
    return r.results[0]["out_0_dram"].reshape(1, S, D)
```

```python
from contextlib import ExitStack

import concourse.bass as bass
import numpy as np
from concourse import mybir
from concourse.alu_op_type import AluOpType as ALU

ACT = mybir.ActivationFunctionType
F32 = mybir.dt.float32
U32 = mybir.dt.uint32
AX = mybir.AxisListType.X

P = 128
D = 1024
S = 512
KC = D // P
NB = S // P
NH = 8
NE = 64
NKEY = 128
EPS = 1e-6
BIG = 3.0e38

CHUNKS_A = [(0, 1), (2, 3)]
CHUNKS_C = [(0, 1), (2, 3)]
CHUNKS_E = [(0, 1), (2,), (3,)]
TM = 256
NGATHER = 8
NWEIGHT = 8
PASSES = 4


def bucket(n):
    n = np.maximum(n, 0)
    nf = np.maximum(n, 1).astype(np.float32)
    large = 16 + (np.log(nf / np.float32(16)) / np.float32(np.log(128 / 16)) * np.float32(16)).astype(np.int32)
    return np.where(n < 16, n, np.minimum(large, 31))


CONSTS = ["ident", "ones", "cols", "strict", "nones", "mask16", "ntri", "reset", "negm", "iota"]
CONSTS_E = ["tri64", "sup64", "n1", "n1t", "m2", "m4", "m8", "m16", "m32"]


def constants():
    r = np.arange(P)
    i, j = r[:, None], r[None, :]
    same = lambda n: (i // n) == (j // n)
    c = {}
    c["ident"] = i == j
    c["ones"] = np.ones((P, P))
    c["nones"] = -np.ones((P, P))
    c["mask16"] = same(16) & (i <= j)
    c["ntri"] = -1.0 * (i >= j)
    c["strict"] = i < j
    c["negm"] = np.where(i < j, 0.0, -1e30)
    c["reset"] = (j % 16 != 0) & (i >= 0)
    c["iota"] = np.tile(np.arange(16), (P, 1))
    c["cols"] = np.tile(np.array([EPS, 1.0, -0.5 * np.log(128.0), 0.0]), (P, 1))
    c["tri64"] = same(64) & (i <= j)
    c["sup64"] = same(64) & (i > j)
    c["n1"] = ~(same(2) & (i % 2 == 1) & (j % 2 == 0))
    c["n1t"] = c["n1"].T
    for m in (2, 4, 8, 16, 32):
        c[f"m{m}"] = same(2 * m) & (i % (2 * m) >= m) & (j % (2 * m) < m)
    hot = np.zeros((P, 384))
    hot[bucket(255 - np.arange(384)), np.arange(384)] = 1.0
    c["hot"] = hot
    return {k: np.asarray(v, np.float32) for k, v in c.items()}


def const_array(names):
    c = constants()
    return np.ascontiguousarray(np.concatenate([c[k] for k in names], axis=1))


class Mark:

    def __init__(self, sem):
        self.sem, self.value = sem, 0


class Step:
    def __init__(self, unit, emit, after, us, nbytes=0, mark=None):
        self.unit, self.emit, self.after, self.us = unit, emit, after, us
        self.nbytes, self.mark, self.value = nbytes, mark, 0
        self.rank, self.place, self.lane, self.func = 0.0, 0, None, None


def latency(a, b):
    return 0.27 if b == "pe" else 0.2 if a == "pe" else 0.14


def flat(after):
    out = []
    for a in after:
        if a is None:
            continue
        if isinstance(a, (list, tuple)):
            out += flat(a)
        else:
            out.append(a)
    return out


def cols(ap):
    n = 1
    for s in ap.shape[1:]:
        n *= s
    return n


class Plan:
    UNITS = ("sp", "pool", "pe", "act", "dve")

    def __init__(self):
        self.steps = []

    def add(self, unit, emit, after, us, nbytes=0, mark=None, lane=None):
        s = Step(unit, emit, flat(after), us, nbytes, mark)
        if mark is not None:
            mark.value += 16
            s.value = mark.value
        s.lane = lane
        self.steps.append(s)
        return s

    def mm(self, bank, out, lhsT, rhs, start, stop, after=(), share=False, cost=None):
        us = 0.01 + 4 * max(cols(rhs), 64) / 2400 if cost is None else cost
        return self.add("pe", lambda e: e.matmul(out, lhsT, rhs, start=start, stop=stop, skip_group_check=share),
                        after, us, lane=bank)

    def tr(self, bank, out, in_, ident, after=()):
        return self.add("pe", lambda e: e.transpose(out, in_, ident), after, 0.13, lane=bank)

    def act(self, out, in_, func, after=(), bias=0.0, scale=1.0, accum=None):
        us = 0.08 + cols(in_) * 0.833e-3 + 0.093 * (not isinstance(scale, float)) + 0.093 * (not isinstance(bias, float))
        if accum is not None:
            s = self.add("act", lambda e: e.activation(out, in_, func, bias=bias, scale=scale, accum_out=accum),
                         after, us + 0.1)
        else:
            s = self.add("act", lambda e: e.activation(out, in_, func, bias=bias, scale=scale), after, us)
        s.func = func
        return s

    def vec(self, emit, n, after, rate=1.0, column=None):
        more = 0.0 if column is None or isinstance(column, (int, float)) else 0.04
        return self.add("dve", emit, after, 0.07 + n * rate * 1.04e-3 + more)

    def tt(self, out, a, b, op, after=()):
        return self.vec(lambda e: e.tensor_tensor(out, a, b, op), cols(out), after)

    def ts(self, out, a, s1, s2, op0, op1=None, after=()):
        if op1 is None:
            return self.vec(lambda e: e.tensor_scalar(out, a, s1, None, op0), cols(out), after, column=s1)
        return self.vec(lambda e: e.tensor_scalar(out, a, s1, s2, op0, op1), cols(out), after, column=s1)

    def stt(self, out, a, s, b, op0, op1, after=()):
        return self.vec(lambda e: e.scalar_tensor_tensor(out, a, s, b, op0, op1), cols(out), after, column=s)

    def cp(self, out, a, after=()):
        return self.vec(lambda e: e.tensor_copy(out, a), cols(out), after)

    def fill(self, out, value, after=()):
        return self.vec(lambda e: e.memset(out, value), cols(out), after)

    def dma(self, unit, out, in_, mark, nbytes, after=(), lane=None):
        return self.add(unit, lambda e: e.dma_start(out, in_), after, 0.6, nbytes, mark, lane)

    def gather(self, out, table, idx, mark, after=()):
        return self.add("pool", lambda e: e.indirect_dma_start(out, None, table, bass.IndirectOffsetOnAxis(idx, 0)),
                        after, 1.04, P * D * 4, mark, "gather")

    def walk(self, before, follow, rank, back=False):
        steps = self.steps
        queues = {u: [] for u in self.UNITS}
        ready = {u: [] for u in self.UNITS}
        coming = {u: [] for u in self.UNITS}
        free = {u: 0.0 for u in self.UNITS}
        pending = [len(b) for b in before]
        reach = [0.0] * len(steps)
        done = [0.0] * len(steps)
        bus, now, left = 0.0, 0.0, len(steps)
        for k, s in enumerate(steps):
            if pending[k] == 0:
                ready[s.unit].append(k)
        while left:
            for u in self.UNITS:
                if free[u] > now + 1e-9:
                    continue
                if coming[u]:
                    ready[u] += [k for at, k in coming[u] if at <= now + 1e-9]
                    coming[u] = [(at, k) for at, k in coming[u] if at > now + 1e-9]
                if not ready[u]:
                    continue
                k = max(ready[u], key=lambda k: rank[k])
                ready[u].remove(k)
                queues[u].append(k)
                left -= 1
                s = steps[k]
                free[u] = end = now + s.us
                if s.mark is not None:
                    if back:
                        bus = max(bus, now + 2.0) + s.nbytes / 360e3
                        end = bus + s.us
                    else:
                        bus = max(bus, end) + s.nbytes / 360e3
                        end = bus + 2.0
                done[k] = end
                for f, data in follow[k]:
                    at = free[u] if not data else end + (latency(steps[f].unit, u) if back else latency(u, steps[f].unit))
                    reach[f] = max(reach[f], at)
                    pending[f] -= 1
                    if pending[f] == 0:
                        coming[steps[f].unit].append((reach[f], f))
            if left:
                times = [free[u] for u in self.UNITS if ready[u]]
                times += [max(free[u], min(at for at, _ in coming[u])) for u in self.UNITS if coming[u]]
                now = max(now, min(times))
        return done, queues, max(done)

    def order(self):
        steps = self.steps
        place = {id(s): k for k, s in enumerate(steps)}
        before, follow = [{} for _ in steps], [{} for _ in steps]
        lanes = {}
        for k, s in enumerate(steps):
            if s.lane is not None:
                prev = lanes.get((s.unit, s.lane))
                if prev is not None:
                    before[k][prev] = follow[prev][k] = False
                lanes[(s.unit, s.lane)] = k
            for a in s.after:
                a = place[id(a)]
                before[k][a] = follow[a][k] = True
        before, follow = [list(b.items()) for b in before], [list(f.items()) for f in follow]
        rank = [0.0] * len(steps)
        for k in range(len(steps) - 1, -1, -1):
            s = steps[k]
            us = max(s.us, s.nbytes / 360e3)
            rank[k] = us + max([rank[f] for f, _ in follow[k]], default=0.0)
        best = None
        for it in range(PASSES):
            done, queues, end = self.walk(before, follow, [(r, -k) for k, r in enumerate(rank)])
            if best is None or end < best[0]:
                best = end, queues
            if it < PASSES - 1:
                rank, _, _ = self.walk(follow, before, [(done[k], k) for k in range(len(steps))], True)
        _, queues = best
        for u in self.UNITS:
            queues[u] = [steps[k] for k in queues[u]]
            for k, s in enumerate(queues[u]):
                s.place = k
        return queues

    def emit(self, nc, sems, last):
        queues = self.order()
        for u in self.UNITS:
            n = 0
            for s in queues[u]:
                if s.mark is None:
                    n += 1
                    s.value = n

        def run(eng, unit):
            seen = {}
            table = None
            for s in queues[unit]:
                if s.func in (ACT.Exp, ACT.Ln) and table != "exp_ln":
                    eng.preload_act_table_set("natural_log_exp_and_others")
                    table = "exp_ln"
                if s.func == ACT.Gelu:
                    table = "gelu"
                need = {}
                for a in s.after:
                    key = a.unit if a.mark is None else a.mark
                    need[key] = max(need.get(key, 0), a.value)
                for key, value in need.items():
                    if seen.get(key, 0) < value:
                        seen[key] = value
                        eng.wait_ge(sems[key] if isinstance(key, str) else key.sem, value)
                ins = s.emit(eng)
                if s.mark is None:
                    ins.then_inc(sems[unit], 1)
                else:
                    ins.then_inc(s.mark.sem, 16)
            if unit == "sp":
                for s in last:
                    eng.wait_ge(s.mark.sem, s.value)

        with nc.Block() as block:
            @block.sync
            def _(e):
                run(e, "sp")

            @block.gpsimd
            def _(e):
                run(e, "pool")

            @block.tensor
            def _(e):
                run(e, "pe")

            @block.scalar
            def _(e):
                run(e, "act")

            @block.vector
            def _(e):
                run(e, "dve")


class Ring:

    def __init__(self, n):
        self.n, self.next, self.free = n, 0, [[] for _ in range(n)]

    def take(self):
        i, fr = self.next, self.free[self.next]
        assert fr is not None, "slot still in use"
        self.next, self.free[i] = (i + 1) % self.n, None
        return i, fr

    def done(self, i, steps):
        self.free[i] = list(steps)


class Projections:

    def __init__(self, ring, banks):
        self.ring, self.banks = ring, banks


VECS = {}


def _vec_cols():
    at = 0
    for name, n in (("c", 8), ("ada_b0", 48), ("ada_b1", 48), ("mix0", 8), ("mix1", 8), ("ffn0", 8),
                    ("ffn1", 8), ("lb0", 8), ("lb1", 8), ("onorm", 8), ("kv_b", 16), ("kv_g", 8), ("fin", 8),
                    ("b_2", 24), ("pre", 8), ("post", 8), ("conv", 48), ("gdn", 1), ("gkv", 1)):
        VECS[name] = (at, n)
        at += n
    return at


NVEC = _vec_cols()


def layer_stack_kernel(nc: bass.Bass, t: dict, out: bass.AP, upto: str = "E", probes=None):
    ctx = ExitStack()
    sb = lambda name, shape, dt=F32: ctx.enter_context(nc.sbuf_tensor(name, shape, dt))
    sem = lambda name: ctx.enter_context(nc.semaphore(name))
    mark = lambda name: Mark(sem(name))
    sems = {u: sem("s_" + u) for u in ("pool", "pe", "act", "dve")}
    p = Plan()

    ps = ctx.enter_context(nc.psum_tensor("ps", [P, 8, 512], F32))
    cc = {k: v.shape[1] for k, v in constants().items()}
    cst = sb("cst", [P, sum(cc[k] for k in CONSTS)])
    vec = sb("vec", [P, NVEC])
    h = sb("h", [P, NB, D])
    hn = sb("hn", [P, KC, TM])
    oT = sb("oT", [P, KC, TM])
    X = [sb(f"X{i}", [P, D]) for i in range(2)]
    xs = sb("xs", [P, D])
    acc = sb("acc", [P, D])
    gat = [sb(f"gat{i}", [P, D]) for i in range(NGATHER)]
    wbuf = sb("wbuf", [P, NWEIGHT, 2, 512])
    row = [sb(f"row{i}", [P, D]) for i in range(3)]
    dgb = [sb(f"dg{i}", [P, P]) for i in range(5)]
    mod = [sb("mod0", [P, 48]), sb("mod1", [P, 48])]
    kvm = sb("kvm", [P, 16])
    mod2 = sb("mod2", [P, 24])
    gT = sb("gT", [P, 6, 8])
    spot = sb("spot", [P, 1])
    small = sb("small", [P, 16, 4])
    idxb = sb("idx", [P, NB, NE], U32)
    gate = sb("gate", [P, NB, NE])
    hid = sb("hid", [P, 2, NE])
    wgt = sb("wgt", [P, 2, NE])
    NWS = 18400
    ws = sb("ws", [P, NWS])

    def region(base):
        at = [base]

        def take(*shape):
            n = 1
            for k in shape:
                n *= k
            v = ws[:, at[0]:at[0] + n]
            at[0] += n
            assert at[0] <= NWS, at[0]
            if len(shape) == 2:
                v = v.rearrange("p (a b) -> p a b", a=shape[0])
            elif len(shape) == 3:
                v = v.rearrange("p (a b c) -> p a b c", a=shape[0], b=shape[1])
            return v

        return take, at

    C = {}
    at = 0
    for k in CONSTS:
        C[k] = cst[:, at:at + cc[k]]
        at += cc[k]
    eps, one, nhl = C["cols"][:, 0:1], C["cols"][:, 1:2], C["cols"][:, 2:3]

    def V(name, lo=0, n=None):
        a0, k = VECS[name]
        return vec[:, a0 + lo:a0 + lo + (k - lo if n is None else n)]

    m_c, m_v = mark("m_c"), mark("m_v")
    m_h = [mark(f"m_h{b}") for b in range(NB)]
    ld_v = p.dma("sp", vec[:, :], t["vecs"], m_v, P * NVEC * 4)
    ld_c = p.dma("sp", cst[:, :], t["cst"], m_c, P * cst.shape[1] * 4)
    ld_h = [p.dma("sp", h[:, b, :], t["x"][b * P:(b + 1) * P, :], m_h[b], P * D * 4) for b in range(NB)]
    hw = [[s] for s in ld_h]
    hr = [[] for _ in range(NB)]

    bankD, bankX, bankO = Ring(3), Ring(2), Ring(1)
    DB, XB, OB, VB = (0, 1, 2), (3, 4), (5,), 6
    proj = Projections(bankD, DB)
    ringW, ringG, ringV, ringR = Ring(NWEIGHT), Ring(NGATHER), Ring(3), Ring(2)
    ringS = Ring(16)
    mW = [mark(f"m_w{i}") for i in range(NWEIGHT)]
    mG = [mark(f"m_g{i}") for i in range(NGATHER)]
    mA = [mark(f"m_a{i}") for i in range(NGATHER)]
    free = {"hn": [], "oT": [], "xs": [], "acc": [], "X0": [], "X1": [], "V": [],
            "Vb": [[], []], "mv": [[], []]}

    row_users = {0: [], 1: [], 2: []}
    hn_users = []

    def hn_again():
        free["hn"] = list(hn_users)
        hn_users.clear()

    kept = {}

    def keep(name, g, q, view, after=()):
        kept[(name, g, q)] = {"view": view, "after": after, "load": None, "users": []}

    class Weights:

        def __init__(self, name, g):
            self.views, self.slots, self.loads = [], [], []
            self.used = []
            for q in range(4):
                k = kept.get((name, g, q))
                if k is None:
                    i, fr = ringW.take()
                    self.views.append(wbuf[:, i, :, :])
                    self.loads.append(p.dma("sp", wbuf[:, i, :, :], t[name][g, q], mW[i], P * D * 4, fr, "w"))
                    self.slots.append(i)
                    self.used.append([])
                else:
                    if k["load"] is None:
                        k["load"] = p.dma("sp", k["view"], t[name][g, q], mark(f"m_{name}{g}{q}"), P * D * 4, k["after"], "w")
                    self.views.append(k["view"])
                    self.loads.append(k["load"])
                    self.slots.append(None)
                    self.used.append(k["users"])

        def at(self, kc, lo, n):
            return self.views[kc // 2][:, kc % 2, lo:lo + n]

        def load(self, kc):
            return self.loads[kc // 2]

        def use(self, kc, step):
            self.used[kc // 2].append(step)

        def done(self):
            for i, u in zip(self.slots, self.used):
                if i is not None:
                    ringW.done(i, u)

    def silu_of(outp, z, tmp, after):
        a = p.act(tmp, z, ACT.Exp, after, scale=-1.0)
        a = p.act(tmp, tmp, ACT.Ln, [a, ld_c], bias=one)
        a = p.act(tmp, tmp, ACT.Exp, [a], scale=-1.0)
        return p.tt(outp, z, tmp, ALU.mult, [a])

    crow = [acc, row[2]]
    c_ready = []
    for k in range(2):
        cr = t["cc"]
        ld = p.dma("sp", crow[k][:, :], bass.AP(cr.tensor, k * D, [[0, P], [1, D]]), mark(f"m_r{k}"), P * D * 4)
        c_ready.append(silu_of(crow[k][:, :], crow[k][:, :], xs[:, :], [ld, free["xs"]]))
        free["xs"] = [c_ready[k]]
    crow_users = [[], []]

    def dot_tile(name, g, k, dst, after=()):
        s_, fr = ringG.take()
        ld = p.dma("sp", gat[s_][:, :], t[name][g], mA[s_], P * D * 4, fr, "ada")
        d = p.vec(lambda e, g_=gat[s_], c_=crow[k], o=dst:
                  e.tensor_tensor_reduce(g_[:, :], g_[:, :], c_[:, :], 1.0, 0.0, ALU.mult, ALU.add, o),
                  D, [ld, c_ready[k]])
        ringG.done(s_, [d])
        crow_users[k].append(d)
        return d

    def matvec(name, g, k, dst, bias, late=None):
        n = dst.shape[1]
        out_, dots = [], []

        def one(m):
            dots.append(dot_tile(name, g + m, k, dst[:, m:m + 1]))
            if m == n - 1:
                out_.append(p.tt(dst, dst, bias, ALU.add, [dots, ld_v]))

        for m in range(n):
            if late is None:
                one(m)
            else:
                late.append(lambda m=m: one(m))
        return out_

    def matvec_pe(name, G, cT, dst, bias, after):
        B = VB + G % 2
        slots = {}
        for pair in range(4):
            for q in range(4):
                s_, fr = ringG.take()
                slots[q] = (s_, p.dma("sp", gat[s_][:, :], t[name][4 * G + q, pair], mA[s_], P * D * 4, fr, "ada"))
            ms = {q: [] for q in range(4)}
            for k in range(2):
                kc = 2 * pair + k
                for q in range(4):
                    m = p.mm(B, ps[32 * q:32 * q + 32, B, :], cT[:, kc, :], gat[slots[q][0]][:, 512 * k:512 * k + 512],
                             kc == 0, kc == KC - 1, [slots[q][1], after, free["Vb"][B - VB]], cost=0.31)
                    ms[q].append(m)
            for q in range(4):
                ringG.done(slots[q][0], ms[q])
        rows = X[0][:, 512 * (G % 2):512 * (G % 2) + 512]
        e = p.act(rows, ps[:, B, :], ACT.Identity, [ms[0], ms[1], ms[2], ms[3], free["mv"][G % 2]])
        for k in range(4):
            m = p.tr(B, ps[:, B, k * P:(k + 1) * P], rows[:, k * P:(k + 1) * P], C["ident"], [e, ld_c])
        free["mv"][G % 2] = [m]
        free["X0"] = free["X0"] + [m]
        r = p.tt(dst.rearrange("p (q k) -> p q k", q=4), ps[:, B, :].rearrange("p (k q i) -> p q k i", k=4, q=4)[:, :, :, 0],
                 bias.rearrange("p (q k) -> p q k", q=4), ALU.add, [m, ld_v])
        free["Vb"][B - VB] = [r]
        free["V"] = free["V"] + [r]
        return [r]

    def modvec(l, part, late=None):
        return matvec(f"ada{l}", 8 * part, 0, mod[l][:, 8 * part:8 * part + 8], V(f"ada_b{l}", 8 * part, 8))

    def gain(k, scale, g, after):
        return p.stt(gT[:, k, :], scale, 1.0, g, ALU.add, ALU.mult, [after, ld_v])

    def broadcast_row(k, col8, after):
        out_steps, fr_row = [], list(row_users[k])
        row_users[k].clear()
        for half in range(2):
            i, fr = bankD.take()
            for q in range(4):
                d, dfr = ringR.take()
                d += 3
                a = p.act(dgb[d][:, :], C["ident"], ACT.Identity, [after, dfr, ld_c], scale=col8[:, 4 * half + q:4 * half + q + 1])
                mmv = p.mm(DB[i], ps[:, DB[i], q * P:(q + 1) * P], C["ones"], dgb[d][:, :], True, True, [a, fr])
                ringR.done(d - 3, [mmv])
            e = p.act(row[k][:, half * 512:half * 512 + 512], ps[:, DB[i], :], ACT.Identity, [mmv, fr_row])
            bankD.done(i, [e])
            out_steps.append(e)
        return out_steps

    def rms(src, dst, n, after):
        s, sfr = ringS.take()
        c = small[:, s, 0:1]
        a = p.act(dst, src, ACT.Square, [after, sfr], accum=c)
        a = p.act(c, c, ACT.Ln, [a], bias=eps, scale=1.0 / n)
        return p.act(c, c, ACT.Exp, [a], scale=-0.5), c, s

    def normed(src, after):
        a, c, s = rms(src, xs[:, :], D, [after, free["xs"]])
        a = p.act(xs[:, :], src, ACT.Identity, [a], scale=c)
        ringS.done(s, [a])
        return a

    def spread(a, j, targets):
        trs, evs = [], [[] for _ in targets]
        for half in range(2):
            i, fr = proj.ring.take()
            for q in range(4):
                kc = 4 * half + q
                trs.append(p.tr(proj.banks[i], ps[:, proj.banks[i], q * P:(q + 1) * P], xs[:, kc * P:(kc + 1) * P], C["ident"], [a, fr, ld_c]))
            last = []
            for q in range(4):
                kc = 4 * half + q
                for n, (dst, g, sh, after) in enumerate(targets):
                    d_, s_ = dst[:, kc, j * P:(j + 1) * P], ps[:, proj.banks[i], q * P:(q + 1) * P]
                    if half:
                        e = p.act(d_, s_, ACT.Identity, [trs[-1], after], scale=g[:, kc:kc + 1], bias=sh[:, kc:kc + 1])
                    else:
                        e = p.ts(d_, s_, g[:, kc:kc + 1], sh[:, kc:kc + 1], ALU.mult, ALU.add, [trs[-1], after])
                        e.us += 0.08
                    last.append(e)
                    evs[n].append(e)
            proj.ring.done(i, last)
        return trs, evs

    def project(w, m, T, after, src=hn):
        i, fr = proj.ring.take()
        for kc in range(KC):
            last = p.mm(proj.banks[i], ps[:, proj.banks[i], 0:T], w.at(kc, m * P, P), src[:, kc, 0:T], kc == 0, kc == KC - 1,
                        [after, w.load(kc), fr])
            w.use(kc, last)
        return i, last

    def add_mix(w2, b, j, src, after, grow, gready):
        used = []
        new = []
        for n in range(2):
            i, fr = bankD.take()
            for kc in range(KC):
                last = p.mm(DB[i], ps[:, DB[i], :], src[:, kc, j * P:(j + 1) * P], w2[n].at(kc, 0, 512), kc == 0, kc == KC - 1,
                            [after, w2[n].load(kc), fr])
                w2[n].use(kc, last)
            used.append(last)
            k, tfr = ringT.take()
            e = p.tt(tmpb[k], ps[:, DB[i], :], row[grow][:, n * 512:n * 512 + 512], ALU.mult, [last, gready, tfr])
            bankD.done(i, [e])
            row_users[grow].append(e)
            f = p.tt(h[:, b, n * 512:n * 512 + 512], h[:, b, n * 512:n * 512 + 512], tmpb[k], ALU.add, [e, hw[b], hr[b]])
            ringT.done(k, [f])
            new.append(f)
        hw[b], hr[b] = new, []
        return used

    tw, at_ = region(0)
    tmpb = [tw(512) for _ in range(2)]
    ringT = Ring(2)
    scs = tw(2, 2, P)
    cand = tw(4, 256)
    s16 = tw(8, 16)
    i16 = tw(8, 16).bitcast(U32)
    i16f = tw(8, 16)
    b16 = tw(4, 16)
    f16 = tw(4, 16).bitcast(U32)
    fa = tw(4, 16).bitcast(U32)
    fb = tw(4, 16).bitcast(U32)
    faf = tw(4, 16)
    fbf = tw(4, 16)
    e1 = tw(4, 16)
    e2 = tw(4, 16)
    gm = tw(4, 1)
    selfree = {"scs": [[], []], "head": [[] for _ in range(4)], "gate": []}
    COMMON = at_[0]

    ready = {}

    def bc(ap, *shape):
        return ap.broadcast_to([P, *shape])

    def select(l, chunk, hn_ready):
        T = P * len(chunk)
        qw = []
        for g in range(2):
            w = Weights(f"pq{l}", g)
            for m in range(4):
                i, last = project(w, m, T, hn_ready)
                hn_users.append(last)
                e = p.act(oT[:, 4 * g + m, 0:T], ps[:, DB[i], 0:T], ACT.Identity, [last, free["oT"]])
                bankD.done(i, [e])
                qw.append(e)
            w.done()
            if g == 0:
                si, sfr = ringW.take()
                sk = wbuf[:, si, :, :].rearrange("p a (b n) -> p (a b) n", b=4)
                ld = p.dma("sp", wbuf[:, si, :, :], t[f"sub{l}"], mW[si], P * D * 4, sfr, "w")
        free["oT"] = None
        scm = []
        for j, b in enumerate(chunk):
            old = free.get(("idx", b), [])
            ready[b] = {"idx": [], "gate": None}
            t2 = []
            for hh in range(4):
                i, fr = bankX.take()
                for q in range(2):
                    hp = 2 * hh + q
                    last = p.mm(XB[i], ps[:, XB[i], q * P:(q + 1) * P], oT[:, hp, j * P:(j + 1) * P], sk[:, hp, :], True, True,
                                [qw[hp], ld, fr])
                scm.append(last)
                e = p.act(scs[:, hh % 2].rearrange("p a b -> p (a b)"), ps[:, XB[i], 0:2 * P], ACT.Identity,
                          [last, selfree["scs"][hh % 2]])
                bankX.done(i, [e])
                fr = selfree["head"][hh]
                tops = []
                for q in range(2):
                    s_, v8, u8 = scs[:, hh % 2, q, :], s16[:, 2 * hh + q, :], i16[:, 2 * hh + q, :]
                    a = p.vec(lambda e, o=v8[:, 0:8], i_=s_: e.max(o, i_), P, [e, fr])
                    a = p.vec(lambda e, o=u8[:, 0:8], m=v8[:, 0:8], i_=s_: e.max_index(o, m, i_), P, [a])
                    a = p.vec(lambda e, m=v8[:, 0:8], i_=s_: e.match_replace(i_, m, i_, -BIG), P, [a])
                    a = p.vec(lambda e, o=v8[:, 8:16], i_=s_: e.max(o, i_), P, [a])
                    a = p.vec(lambda e, o=u8[:, 8:16], m=v8[:, 8:16], i_=s_: e.max_index(o, m, i_), P, [a])
                    tops.append(a)
                selfree["scs"][hh % 2] = tops
                hs = slice(2 * hh, 2 * hh + 2)
                ic = p.cp(i16f[:, hs, :], i16[:, hs, :], [tops])
                c3 = cand[:, hh, :].rearrange("p (a b) -> p a b", a=16)
                a = p.tt(c3, bc(s16[:, 2 * hh, :].rearrange("p (a b) -> p a b", b=1), 16, 16),
                         bc(s16[:, 2 * hh + 1, :].rearrange("p (a b) -> p a b", a=1), 16, 16), ALU.add, [tops, fr])
                s_, v8, u8 = cand[:, hh, :], b16[:, hh, :], f16[:, hh, :]
                a = p.vec(lambda e, o=v8[:, 0:8], i_=s_: e.max(o, i_), 256, [a, selfree["gate"]])
                a = p.vec(lambda e, o=u8[:, 0:8], m=v8[:, 0:8], i_=s_: e.max_index(o, m, i_), 256, [a])
                a = p.vec(lambda e, m=v8[:, 0:8], i_=s_: e.match_replace(i_, m, i_, -BIG), 256, [a])
                a = p.vec(lambda e, o=v8[:, 8:16], i_=s_: e.max(o, i_), 256, [a])
                a = p.vec(lambda e, o=u8[:, 8:16], m=v8[:, 8:16], i_=s_: e.max_index(o, m, i_), 256, [a])
                t2.append(a)
                a1 = p.ts(fa[:, hh], f16[:, hh], 4, None, ALU.logical_shift_right, None, [a])
                b1 = p.ts(fb[:, hh], f16[:, hh], 15, None, ALU.bitwise_and, None, [a])
                a2 = p.cp(faf[:, hh], fa[:, hh], [a1])
                b2 = p.cp(fbf[:, hh], fb[:, hh], [b1])
                prev = a
                es = []
                for half, src, dst, rd in ((0, faf, e1, a2), (1, fbf, e2, b2)):
                    x1 = p.tt(c3, bc(src[:, hh].rearrange("p (k n) -> p k n", n=1), 16, 16),
                              bc(C["iota"].rearrange("p (k n) -> p k n", k=1), 16, 16), ALU.is_equal, [rd, prev, ic])
                    x2 = p.tt(c3, c3, bc(i16f[:, 2 * hh + half, :].rearrange("p (k n) -> p k n", k=1), 16, 16), ALU.mult, [x1])
                    x3 = p.vec(lambda e, o=dst[:, hh], i_=c3: e.tensor_reduce(o, i_, AX, ALU.add), 256, [x2])
                    prev = [x3]
                    es.append(x3)
                x4 = p.stt(e2[:, hh], e1[:, hh], float(NKEY), e2[:, hh], ALU.mult, ALU.add, [es])
                x5 = p.ts(idxb[:, b, 16 * hh:16 * hh + 16], e2[:, hh], float(l * NKEY * NKEY), None, ALU.add, None, [x4, old])
                selfree["head"][hh] = [x5]
                ready[b]["idx"].append(x5)
            gb = gate[:, b, :].rearrange("p (a b) -> p a b", a=4)
            g1_ = p.tt(gb, b16, bc(b16[:, :, 0:1], 4, 16), ALU.subtract, [t2, free.get(("gate", b), [])])
            g2_ = p.act(gb, gb, ACT.Exp, [g1_])
            g3_ = p.vec(lambda e, o=gm, i_=gb: e.tensor_reduce(o, i_, AX, ALU.add), 64, [g2_, selfree["gate"]])
            g4_ = p.vec(lambda e, o=gm: e.reciprocal(o, o), 4, [g3_], 8.0)
            g5_ = p.tt(gb, gb, bc(gm, 4, 16), ALU.mult, [g4_])
            selfree["gate"] = [g5_]
            ready[b]["gate"] = g5_
        ringW.done(si, scm)
        free["oT"] = scm

    def keep_rows(chunk, hn_ready):
        for j, b in enumerate(chunk):
            evs = []
            for half in range(2):
                i, fr = bankD.take()
                for q in range(4):
                    kc = 4 * half + q
                    last = p.tr(DB[i], ps[:, DB[i], q * P:(q + 1) * P], hn[:, kc, j * P:(j + 1) * P], C["ident"], [hn_ready, fr])
                hn_users.append(last)
                e = p.act(X[b % 2][:, half * 512:half * 512 + 512], ps[:, DB[i], :], ACT.Identity, [last, free[f"X{b % 2}"]])
                bankD.done(i, [e])
                evs.append(e)
            free[f"X{b % 2}"] = None
            ready[b]["X"] = evs

    def experts(l, blocks, grow, gready, late=()):
        us = [("u", b, e) for b in blocks for e in range(NE)]
        vs = [("v", b, e) for b in blocks for e in range(NE)]
        seq = us[:16]
        for k in range(16, len(us)):
            seq += [us[k], vs[k - 16]]
        seq += vs[-16:]
        dots = {}
        accs = {b: [] for b in blocks}
        wsteps = {}
        late = list(late)
        every = len(seq) // (len(late) + 1)
        for n_, (kind, b, e) in enumerate(seq):
            if late and n_ % every == every - 1:
                late.pop(0)()
            s, fr = ringG.take()
            rd = ready[b]
            g = p.gather(gat[s][:, :], t["peer_" + kind], idxb[:, b, e:e + 1], mG[s], [fr, rd["idx"][e // 16]])
            if kind == "u":
                first = [] if e else free.get(("hid", b % 2), [])
                d = p.vec(lambda en, g_=gat[s], x_=X[b % 2], o=hid[:, b % 2, e:e + 1]:
                          en.tensor_tensor_reduce(g_[:, :], g_[:, :], x_[:, :], 1.0, 0.0, ALU.mult, ALU.add, o),
                          D, [g, rd["X"], free.get(("hid", b % 2), [])])
                ringG.done(s, [d])
                dots.setdefault(b, []).append(d)
                if e % 16 == 15:
                    lo = e - 15
                    hsl, wsl = hid[:, b % 2, lo:e + 1], wgt[:, b % 2, lo:e + 1]
                    a = p.act(hsl, hsl, ACT.Gelu, [dots[b][lo:]])
                    a = p.tt(wsl, hsl, gate[:, b, lo:e + 1], ALU.mult, [a, rd["gate"], free.get(("wgt", b % 2), [])])
                    for k in range(lo, e + 1):
                        wsteps[(b, k)] = a
                if e == NE - 1:
                    free[f"X{b % 2}"] = dots[b]
                    free[("hid", b % 2)] = [a]
                    free[("gate", b)] = [a]
            else:
                wc = wgt[:, b % 2, e:e + 1]
                wst = wsteps[(b, e)]
                if e == 0 or (e % 2 == 1 and 1 < e < NE - 1):
                    if e == 0:
                        a = p.ts(acc[:, :], gat[s][:, :], wc, None, ALU.mult, None, [g, wst, free["acc"]])
                    else:
                        a = p.stt(acc[:, :], gat[s][:, :], wc, acc[:, :], ALU.mult, ALU.add, [g, wst, prev_acc])
                    prev_acc = a
                    ringG.done(s, [a])
                else:
                    k, dfr = ringV.take()
                    a = p.act(dgb[k][:, :], C["ident"], ACT.Identity, [wst, dfr], scale=wc)
                    m = []
                    for half in range(2):
                        m.append(p.mm(VB + half, ps[:, VB + half, :], dgb[k][:, :], gat[s][:, half * 512:half * 512 + 512], e == 1, e == NE - 1,
                                      [a, g, free["V"]], cost=0.95))
                    ringV.done(k, m)
                    ringG.done(s, m)
                    lastd = a
                    lastm = m
                if e == NE - 1:
                    free[("idx", b)] = [g]
                    free[("wgt", b % 2)] = [prev_acc, lastd]
                    pv = ps[:, VB:VB + 2, :].rearrange("p a b -> p (a b)")
                    x1 = p.tt(acc[:, :], pv, acc[:, :], ALU.add, [prev_acc, lastm])
                    x2 = p.tt(acc[:, :], acc[:, :], row[grow][:, :], ALU.mult, [x1, gready])
                    x3 = p.tt(h[:, b, :], h[:, b, :], acc[:, :], ALU.add, [x2, hw[b], hr[b]])
                    hw[b], hr[b] = [x3], []
                    free["acc"], free["V"] = [x3], [x1]
                    row_users[grow].append(x2)

    tA, atA = region(COMMON)
    lbv, oml, noml, lt0, lt1 = (tA(8) for _ in range(5))
    SA = tA(8, P)
    hset = [{k: tA(3, TM) if k == "sg" else tA(2, P) if k == "v" else tA(TM)
             for k in ("sg", "kk", "cum", "ecum", "kd", "dl", "qd", "v", "sq", "o1")} for _ in range(2)]
    kset = [{"KM": tA(8 * 144), "qP": tA(P), "sc": tA(P), "KT": tA(P), "pre": tA(16)} for _ in range(2)]
    ringH, ringK = Ring(2), Ring(2)
    stateA = {}
    for q in range(4):
        keep("wout", 1, q, tA(2, 512))

    def hgrn_setup():
        m = p.tt(lt0, V("lb0"), V("lb1"), ALU.max, [ld_v])
        a = p.tt(lbv, V("lb0"), lt0, ALU.subtract, [m])
        b = p.tt(lt1, V("lb1"), lt0, ALU.subtract, [m])
        a = p.act(lbv, lbv, ACT.Exp, [a])
        b = p.act(lt1, lt1, ACT.Exp, [b])
        s = p.tt(lt0, lbv, lt1, ALU.add, [a, b])
        s = p.vec(lambda e: e.reciprocal(lt0, lt0), 8, [s], 8.0)
        a = p.tt(lbv, lbv, lt0, ALU.mult, [s])
        b = p.tt(oml, lt1, lt0, ALU.mult, [s])
        c = p.ts(noml, oml, -1.0, None, ALU.mult, None, [b])
        lb_ready = [a, b, c]
        for k in kset:
            ringK.done(kset.index(k), [p.fill(k["KM"], 0.0), p.fill(k["sc"], 0.0), p.fill(k["pre"], 1.0)])
        return lb_ready

    def sigmoid_ps(dst, src, after):
        a = p.act(dst, src, ACT.Exp, after, scale=-1.0)
        b = p.act(dst, dst, ACT.Ln, [a], bias=one)
        return a, p.act(dst, dst, ACT.Exp, [b], scale=-1.0)

    def hgrn(chunk, hn_ready, lb_ready):
        T = P * len(chunk)
        nb = len(chunk)
        done = []
        for hh in range(NH):
            k, fr = ringH.take()
            q = hset[k]
            sg = q["sg"][:, :, 0:T]
            w = Weights("win", hh)
            i, last = project(w, 1, T, hn_ready)
            hn_users.append(last)
            a, sf = sigmoid_ps(sg[:, 1, :], ps[:, DB[i], 0:T], [last, fr, ld_c])
            bankD.done(i, [a])
            kk, cum, ecum, kd, dl, qd = (q[n][:, 0:T] for n in ("kk", "cum", "ecum", "kd", "dl", "qd"))
            k1 = p.ts(kk, sg[:, 1, :], noml[:, hh:hh + 1], oml[:, hh:hh + 1], ALU.mult, ALU.add, [sf, lb_ready, fr])
            lf = p.act(cum, sg[:, 1, :], ACT.Ln, [sf, lb_ready, fr], bias=lbv[:, hh:hh + 1], scale=oml[:, hh:hh + 1])
            cu = [p.vec(lambda e, o=cum[:, j * P:(j + 1) * P]:
                        e.tensor_tensor_scan(o, C["reset"], o, 0.0, ALU.mult, ALU.add), P, [lf, ld_c], 2.0)
                  for j in range(nb)]
            c16 = cum.rearrange("p (n c) -> p n c", c=16)
            d0 = p.tt(dl.rearrange("p (n c) -> p n c", c=16), bc(c16[:, :, 15:16], T // 16, 16), c16, ALU.subtract, [cu, fr])
            ec = p.act(ecum, cum, ACT.Exp, [cu, fr])
            en = p.act(kd, cum, ACT.Exp, [cu, fr], scale=-1.0)
            d1 = p.act(dl, dl, ACT.Exp, [d0])
            kd1 = p.tt(kd, kd, kk, ALU.mult, [en, k1])
            i, last = project(w, 0, T, hn_ready)
            hn_users.append(last)
            a, sq_ = sigmoid_ps(sg[:, 0, :], ps[:, DB[i], 0:T], [last, fr])
            a = p.tt(sg[:, 0, :], sg[:, 0, :], ps[:, DB[i], 0:T], ALU.mult, [sq_])
            bankD.done(i, [a])
            qd1 = p.tt(qd, sg[:, 0, :], ecum, ALU.mult, [a, ec, fr])
            i, bfr = bankD.take()
            for j in range(nb):
                for kc in range(KC):
                    last = p.mm(DB[i], ps[:, DB[i], j * P:(j + 1) * P], hn[:, kc, j * P:(j + 1) * P], w.at(kc, 3 * P, P),
                                kc == 0, kc == KC - 1, [hn_ready, w.load(kc), bfr])
                    w.use(kc, last)
            hn_users.append(last)
            vv = p.act(q["v"][:, 0:nb, :].rearrange("p a b -> p (a b)"), ps[:, DB[i], 0:T], ACT.Identity, [last, fr])
            bankD.done(i, [vv])
            i, last = project(w, 2, T, hn_ready)
            hn_users.append(last)
            a, sg_ = sigmoid_ps(sg[:, 2, :], ps[:, DB[i], 0:T], [last, fr])
            gs = p.tt(sg[:, 2, :], sg[:, 2, :], ps[:, DB[i], 0:T], ALU.mult, [sg_])
            bankD.done(i, [gs])
            w.done()
            o, ofr = bankO.take()
            po = ps[:, OB[o], 0:T]
            users = []
            for j, b in enumerate(chunk):
                x, kfr = ringK.take()
                z = kset[x]
                KM, qP, sc, KT, pre = z["KM"], z["qP"], z["sc"], z["KT"], z["pre"]
                sl = slice(j * P, (j + 1) * P)
                ed = ecum[:, sl].rearrange("p (n c) -> p n c", c=16)[:, :, 15]
                km = [p.tt(KM.rearrange("p (r c) -> p r c", c=144)[:, :, 0:16], dl[:, sl].rearrange("p (r c) -> p r c", c=16),
                           kk[:, sl].rearrange("p (r c) -> p r c", c=16), ALU.mult, [d1, k1, kfr])]
                for r in range(1, 8):
                    km.append(p.ts(KM[:, r * P:r * P + 16 * r], KM[:, (r - 1) * P:(r - 1) * P + 16 * r], ed[:, r:r + 1], None,
                                   ALU.mult, None, [km[-1], ec]))
                pr = p.vec(lambda e, o=pre[:, 1:9], d=ed: e.tensor_tensor_scan(o, d, C["ones"][:, 0:8], 1.0, ALU.mult, ALU.mult),
                           8, [ec, kfr], 2.0)
                qp = p.tt(qP.rearrange("p (n c) -> p n c", c=16), qd[:, sl].rearrange("p (n c) -> p n c", c=16),
                          bc(pre[:, 0:8].rearrange("p (n c) -> p n c", c=1), 8, 16), ALU.mult, [pr, qd1])
                i, xfr = bankX.take()
                B = XB[i]
                for r in range(1, 8):
                    m1 = p.mm(B, ps[:, B, 16 * r:16 * r + 16], KM[:, (r - 1) * P:r * P], qd[:, j * P + 16 * r:j * P + 16 * r + 16],
                              True, True, [km[r - 1], qd1, xfr])
                m2 = p.mm(B, ps[:, B, P:2 * P], kd[:, sl], qd[:, sl], True, True, [kd1, qd1, xfr])
                m3 = p.tr(B, ps[:, B, 2 * P:3 * P], KM[:, 7 * P:8 * P], C["ident"], [km[7], ld_c, xfr])
                s1 = p.act(sc[:, 16:P], ps[:, B, 16:P], ACT.Identity, [m1, m2, m3, kfr])
                s2 = p.act(KT, ps[:, B, 2 * P:3 * P], ACT.Identity, [m3, m2, m1, kfr])
                s3 = p.vec(lambda e, o=sc, m=C["mask16"].bitcast(U32), d=ps[:, B, P:2 * P]: e.copy_predicated(o, m, d),
                           P, [s1, s2, ld_c])
                o1 = p.mm(OB[o], po[:, sl], q["v"][:, j, :], sc, True, b == 0, [vv, s3, ofr])
                if b > 0:
                    o1 = p.mm(OB[o], po[:, sl], SA[:, hh, :], qP, False, True, [stateA[hh], qp])
                users += [o1, km[-1], qp]
                if b < NB - 1:
                    m4 = p.mm(B, ps[:, B, 3 * P:4 * P], KT, q["v"][:, j, :], True, True, [s2, s3, vv])
                    if b == 0:
                        st = p.cp(SA[:, hh, :], ps[:, B, 3 * P:4 * P], [m4])
                    else:
                        st = p.stt(SA[:, hh, :], SA[:, hh, :], pre[:, 8:9], ps[:, B, 3 * P:4 * P], ALU.mult, ALU.add, [m4, o1])
                    stateA[hh] = st
                    users.append(st)
                    bankX.done(i, [st])
                    ringK.done(x, [st, o1, m2, m3, qp])
                else:
                    bankX.done(i, [s3])
                    ringK.done(x, [o1, m2, m3, qp])
            sqv, o1v = q["sq"][:, 0:T], q["o1"][:, 0:T]
            a = p.act(sqv, po, ACT.Square, [o1, fr])
            i, xfr = bankX.take()
            m = p.mm(XB[i], ps[:, XB[i], 0:T], C["ones"], sqv, True, True, [a, xfr])
            b1 = p.act(sqv, ps[:, XB[i], 0:T], ACT.Ln, [m], bias=eps, scale=1.0 / P)
            bankX.done(i, [b1])
            b2 = p.act(sqv, sqv, ACT.Exp, [b1], scale=-0.5)
            b3 = p.stt(o1v, po, V("onorm", hh, 1), sg[:, 2, :], ALU.mult, ALU.mult, [gs, o1, a, fr])
            bankO.done(o, [b3])
            b4 = p.tt(oT[:, hh, 0:T], o1v, sqv, ALU.mult, [b2, b3, free["oT"]])
            ringH.done(k, [b4, users])
            done.append(b4)
        free["oT"] = None
        return done

    c32 = X[1][:, 0:256].rearrange("p (a b) -> p a b", a=8)
    a = silu_of(X[1][:, 256:264], V("c"), X[1][:, 264:272], [ld_v])
    c32_ok = p.cp(c32, bc(X[1][:, 256:264].rearrange("p (a b) -> p a b", b=1), 8, 32), [a])
    mod0 = []
    for G in range(3):
        r = matvec_pe("ada0", G, c32, mod[0][:, 16 * G:16 * G + 16], V("ada_b0", 16 * G, 16), c32_ok)
        mod0 += [r, r]
    free["X1"] = free["V"]
    late = []
    kvm_s = matvec("kvada", 0, 0, kvm[:, :], V("kv_b"))
    mod1 = [modvec(1, k) for k in range(6)]
    mv = [matvec("ada_2", 8 * k, 1, mod2[:, 8 * k:8 * k + 8], V("b_2", 8 * k, 8)) for k in range(3)]
    free["acc"] = list(crow_users[0])
    usersA, usersC, usersE = [], [], []
    at0 = len(p.steps)
    lb_ready = hgrn_setup()
    usersA += p.steps[at0:]
    for n, chunk in enumerate(CHUNKS_A):
        if n == 0:
            (sh, scl, g1, sh2, sc2, g2) = mod0
            g_a = gain(0, mod[0][:, 8:16], V("mix0"), scl)
        hn_again()
        hr1 = []
        for j, b in enumerate(chunk):
            a = normed(h[:, b, :], [hw[b]])
            hr[b].append(a)
            trs, evs = spread(a, j, [(hn, gT[:, 0, :], mod[0][:, 0:8], [g_a, sh, free["hn"]])])
            free["xs"] = trs
            hr1 += evs[0]
        at0 = len(p.steps)
        done = hgrn(chunk, hr1, lb_ready)
        usersA += p.steps[at0:]
        if n == 0:
            r1 = broadcast_row(0, mod[0][:, 16:24], g1)
        w2 = [Weights("wout", 0), Weights("wout", 1)]
        used = []
        for j, b in enumerate(chunk):
            used += add_mix(w2, b, j, oT, done, 0, r1)
        for w in w2:
            w.done()
        free["oT"] = used
        if n == 0:
            g_f = gain(1, mod[0][:, 32:40], V("ffn0"), sc2)
        hn_again()
        hr2 = []
        for j, b in enumerate(chunk):
            a = normed(h[:, b, :], [hw[b]])
            hr[b].append(a)
            trs, evs = spread(a, j, [(hn, gT[:, 1, :], mod[0][:, 24:32], [g_f, sh2, free["hn"]])])
            free["xs"] = trs
            hr2 += evs[0]
        select(0, chunk, hr2)
        keep_rows(chunk, hr2)
        if n == 0:
            r2 = broadcast_row(1, mod[0][:, 40:48], g2)
        if upto == "A":
            continue
        experts(0, chunk, 1, r2)
        if n == 0:
            row_users[2] += crow_users[1]
        late = []

    tC, atC = region(COMMON)
    kT, vS, qT = tC(NH, S), tC(NB, D), tC(NH, TM)
    cset = [{k: tC(S) for k in ("e", "lk", "a")} for _ in range(2)]
    ringC = Ring(2)
    sbo_kept = tC(2, 512)

    def attend(chunk, kv_done, q_done):
        done, used = [], []
        for j, b in enumerate(chunk):
            W = (b + 1) * P
            for hh in range(NH):
                c, fr = ringC.take()
                e, lk, a = (cset[c][k][:, 0:W] for k in ("e", "lk", "a"))
                i, bfr = bankD.take()
                B = DB[i]
                z = ps[:, B, 0:W]
                qh = qT[:, hh, j * P:(j + 1) * P]
                for n in range(b + 1):
                    m1 = p.mm(B, z[:, n * P:(n + 1) * P], kT[:, hh, n * P:(n + 1) * P], qh, n == 0, True,
                              [kv_done, q_done, bfr], True)
                a1 = p.act(e, z, ACT.Abs, [m1, fr])
                a2 = p.act(e, e, ACT.Exp, [a1], scale=-1.0)
                a3 = p.act(e, e, ACT.Ln, [a2], bias=one)
                d1 = p.stt(lk, z, 0.0, e, ALU.max, ALU.add, [a3, fr])
                d2 = p.tt(lk[:, b * P:W], lk[:, b * P:W], C["strict"], ALU.mult, [d1])
                for n in range(b + 1):
                    m2 = p.mm(B, z[:, n * P:(n + 1) * P], C["ntri"], lk[:, n * P:(n + 1) * P], False, True, [d2, d1], True)
                for n in range(1, b + 1):
                    m2 = p.mm(B, z[:, 0:n * P].rearrange("p (a b) -> p a b", b=P), C["nones"],
                              bc(lk[:, n * P:(n + 1) * P].rearrange("p (a b) -> p a b", a=1), n, P), False, True, [d2, d1], True)
                m2 = p.mm(B, z[:, b * P:W], C["ident"], C["negm"], False, True, [d1], True)
                a4 = p.act(a, z, ACT.Exp, [m2, fr])
                bankD.done(i, [a4])
                x, xfr = bankX.take()
                po = ps[:, XB[x], 0:P]
                for n in range(b + 1):
                    m3 = p.mm(XB[x], po, vS[:, n, hh * P:(hh + 1) * P], a[:, n * P:(n + 1) * P], n == 0, n == b, [a4, xfr])
                o = p.act(oT[:, hh, j * P:(j + 1) * P], po, ACT.Identity, [m3, free["oT"]])
                bankX.done(x, [o])
                ringC.done(c, [m3, m2])
                done.append(o)
                used.append(m1)
        return done, used

    gate_c = None
    if upto in "CDE":
        gate_c = p.fill(spot[:, :], 0.0, [usersA, [k["users"] for k in kept.values()]])
        keep("sbo", 1, 3, sbo_kept, [gate_c])
        g_kv = gain(2, kvm[:, 8:16], V("kv_g"), kvm_s)
        (sh, scl, g1, sh2, sc2, g2) = mod1
        g_a = gain(3, mod[1][:, 8:16], V("mix1"), scl)
    kv_done, qused = [], []
    for n, chunk in enumerate(CHUNKS_C if upto in "CDE" else []):
        T = P * len(chunk)
        t0 = chunk[0] * P
        at0 = len(p.steps)
        hn_again()
        rk, rq = [], []
        for j, b in enumerate(chunk):
            a = normed(h[:, b, :], [hw[b]])
            hr[b].append(a)
            trs, evs = spread(a, j, [(hn, gT[:, 2, :], kvm[:, 0:8], [g_kv, kvm_s, free["hn"]]),
                                     (oT, gT[:, 3, :], mod[1][:, 0:8], [g_a, sh, free["oT"]])])
            free["xs"] = trs
            rk += evs[0]
            rq += evs[1]
        for g in range(2):
            w = Weights("kvw", g)
            for m in range(4):
                i, last = project(w, m, T, rk)
                hn_users.append(last)
                e = p.act(kT[:, 4 * g + m, t0:t0 + T], ps[:, DB[i], 0:T], ACT.Identity, [last, gate_c])
                bankD.done(i, [e])
                kv_done.append(e)
            w.done()
        for g in range(2):
            w = Weights("kvw", 2 + g)
            for j, b in enumerate(chunk):
                i, fr = bankD.take()
                for kc in range(KC):
                    last = p.mm(DB[i], ps[:, DB[i], :], hn[:, kc, j * P:(j + 1) * P], w.at(kc, 0, 512), kc == 0, kc == KC - 1,
                                [rk, w.load(kc), fr])
                    w.use(kc, last)
                hn_users.append(last)
                e = p.act(vS[:, b, g * 512:g * 512 + 512], ps[:, DB[i], :], ACT.Identity, [last, gate_c])
                bankD.done(i, [e])
                kv_done.append(e)
            w.done()
        q_done, qin = [], []
        for g in range(2):
            w = Weights("sbq", g)
            for m in range(4):
                i, last = project(w, m, T, rq, oT)
                qin.append(last)
                e = p.act(qT[:, 4 * g + m, 0:T], ps[:, DB[i], 0:T], ACT.Identity, [last, gate_c, qused], scale=float(P) ** -0.5)
                bankD.done(i, [e])
                q_done.append(e)
            w.done()
        free["oT"] = qin
        done, qused = attend(chunk, kv_done, q_done)
        free["oT"] = None
        if n == 0:
            r1 = broadcast_row(0, mod[1][:, 16:24], g1)
        w2 = [Weights("sbo", 0), Weights("sbo", 1)]
        used = []
        for j, b in enumerate(chunk):
            used += add_mix(w2, b, j, oT, done, 0, r1)
        for w in w2:
            w.done()
        free["oT"] = used
        if n == 0:
            g_f = gain(4, mod[1][:, 32:40], V("ffn1"), sc2)
        hn_again()
        hr2 = []
        for j, b in enumerate(chunk):
            a = normed(h[:, b, :], [hw[b]])
            hr[b].append(a)
            trs, evs = spread(a, j, [(hn, gT[:, 4, :], mod[1][:, 24:32], [g_f, sh2, free["hn"]])])
            free["xs"] = trs
            hr2 += evs[0]
        select(1, chunk, hr2)
        keep_rows(chunk, hr2)
        if n == 0:
            r2 = broadcast_row(2, mod[1][:, 40:48], g2)
        usersC += p.steps[at0:]
        if upto == "C":
            continue
        experts(1, chunk, 2, r2)

    tE, atE = region(0)
    cste = tE(cc["tri64"] * len(CONSTS_E))
    CE = {k: cste[:, n * P:(n + 1) * P] for n, k in enumerate(CONSTS_E)}
    SG = tE(4, P)
    carry = tE(12, 3)
    ckvT, ckvR, ikT, toep = tE(S), tE(NB, P), tE(S), tE(4, 256)
    cin, sgE = tE(3, TM + 3), tE(3, TM)
    Q2, K2, V2 = tE(4, TM), tE(4, TM), tE(4, TM)
    MA = [tE(4, P) for _ in range(9)]
    XN = [m.rearrange("p (a b) c -> p a b c", a=2) for m in MA[3:5]]
    iqT, qbT = tE(4, TM), tE(4, TM)
    score, Wk, lg0, pT = tE(S), tE(S), tE(S), tE(S)
    lg1 = tE(S)
    sm = tE(96)
    ob = cst[:, cc["ident"] + cc["ones"] + cc["cols"] + cc["strict"] + 512:][:, 0:P]
    abr, nea = sm[:, 0:8], sm[:, 8:12]
    bawb = [sm[:, 80:96], sm[:, 16:32]]
    sc4 = [sm[:, 32 + 4 * k:36 + 4 * k] for k in range(8)]
    glc = sm[:, 64:72].rearrange("p (a b) -> p a b", a=4)
    m8 = sm[:, 72:80]
    at = cc["ident"] + cc["ones"] + cc["cols"] + cc["strict"]
    wuv = cst[:, at:at + 512].rearrange("p (a b) -> p a b", a=4)

    def b4(ap):
        return bc(ap.rearrange("p (a b) -> p a b", a=1), 4, P)

    def b2(ap):
        return bc(ap.rearrange("p (a b) -> p a b", a=1), 2, P)

    def b4c(ap):
        return bc(ap.rearrange("p (a b) -> p a b", b=1), 4, P)

    def placed(chunk):
        return [(b % 2, b) for b in chunk]

    def chunk_cols(chunk):
        return slice(chunk[0] % 2 * P, chunk[0] % 2 * P + len(chunk) * P)

    def gated_heads(chunk, rh):
        T = P * len(chunk)
        at = chunk_cols(chunk)
        out_, zs = [], []
        for hh in range(4):
            w = Weights("win2", hh)
            ins, rd = [], []
            for ty in range(3):
                i, last = project(w, ty, T, rh, hn[:, :, at])
                hn_users.append(last)
                ins.append(p.act(cin[:, ty, 3:3 + T], ps[:, proj.banks[i], 0:T], ACT.Identity, [last, E["cin"], gate_e]))
                proj.ring.done(i, [ins[-1]])
            cr = p.cp(cin[:, :, 0:3], carry[:, 3 * hh:3 * hh + 3, :], [E["carry"], E["cin"]])
            rel = []
            cw = [V("conv", 12 * tap, 12) for tap in range(4)]
            for ty, dst in enumerate((Q2, K2, V2)):
                tile_ = 4 * ty + hh
                d = dst[:, hh, at]
                a = p.act(d, cin[:, ty, 0:T], ACT.Identity, [ins[ty], cr, E["QKV"]], scale=cw[0][:, tile_:tile_ + 1])
                for tap in range(1, 4):
                    a = p.stt(d, cin[:, ty, tap:tap + T], cw[tap][:, tile_:tile_ + 1], d, ALU.mult, ALU.add, [a])
                rel.append(a)
            ca = p.cp(carry[:, 3 * hh:3 * hh + 3, :], cin[:, :, T:T + 3], [ins, cr])
            E["cin"], E["carry"] = rel + [ca], [ca]
            sgs = []
            for ty, dst in enumerate((Q2, K2, V2)):
                s_ = sgE[:, ty, 0:T]
                _, a = sigmoid_ps(s_, dst[:, hh, at], [rel[ty], E["sgE"]])
                sgs.append(p.tt(dst[:, hh, at], dst[:, hh, at], s_, ALU.mult, [a]))
            sq = [p.act(sgE[:, ty, 0:T], dst[:, hh, at], ACT.Square, [sgs[ty]]) for ty, dst in enumerate((Q2, K2))]
            i, fr = proj.ring.take()
            B = proj.banks[i]
            mq = p.mm(B, ps[:, B, 0:T], C["ones"], sgE[:, 0, 0:T], True, True, [sq[0], fr])
            mk = p.mm(B, ps[:, B, TM:TM + T], C["ones"], sgE[:, 1, 0:T], True, True, [sq[1], fr])
            lq = p.act(sgE[:, 0, 0:T], ps[:, B, 0:T], ACT.Ln, [mq, mk], bias=eps)
            lk = p.act(sgE[:, 1, 0:T], ps[:, B, TM:TM + T], ACT.Ln, [mk], bias=eps)
            proj.ring.done(i, [lq, lk])
            lq = p.act(sgE[:, 0, 0:T], sgE[:, 0, 0:T], ACT.Exp, [lq], bias=nhl, scale=-0.5)
            lk = p.act(sgE[:, 1, 0:T], sgE[:, 1, 0:T], ACT.Exp, [lk], scale=-0.5)
            aq = p.tt(Q2[:, hh, at], Q2[:, hh, at], sgE[:, 0, 0:T], ALU.mult, [lq])
            ak = p.tt(K2[:, hh, at], K2[:, hh, at], sgE[:, 1, 0:T], ALU.mult, [lk])
            E["sgE"] = [aq, ak, sgs[2]]
            out_.append([aq, ak, sgs[2]])
            i, last = project(w, 3, T, rh, hn[:, :, at])
            hn_users.append(last)
            _, a = sigmoid_ps(oT[:, hh, at], ps[:, proj.banks[i], 0:T], [last, free["oT"]])
            a = p.tt(oT[:, hh, at], oT[:, hh, at], ps[:, proj.banks[i], 0:T], ALU.mult, [a])
            proj.ring.done(i, [a])
            zs.append(a)
            w.done()
        return out_, zs

    def gated_block(b, j, heads, zs, bw):
        sl = slice(j * P, (j + 1) * P)
        A0, A1, A2, _, _, A5, A6, A7, A8 = MA
        beta, gg, eg, el, be, x0, x1, gcl = sc4
        fr = E["blk"]
        bank, GB = bankX, XB
        baw = bawb[j]

        def four(mms, after):
            i, bfr = bank.take()
            for q in range(4):
                o_, l_, r_ = mms(q, ps[:, GB[i], q * P:(q + 1) * P])
                last = p.mm(GB[i], o_, l_, r_, True, True, [after, bfr])
            return i, ps[:, GB[i], :].rearrange("p (a b) -> p a b", a=4), last

        a = p.act(beta, baw[:, 0:4], ACT.Exp, [bw, fr], scale=-1.0)
        a = p.ts(beta, beta, 1.0, None, ALU.add, None, [a])
        beta_ok = p.vec(lambda e: e.reciprocal(beta, beta), 4, [a], 8.0)
        a = p.tt(x0, baw[:, 4:8], abr[:, 4:8], ALU.add, [bw, abr_ok, fr])
        c = p.act(x1, x0, ACT.Abs, [a])
        c = p.act(x1, x1, ACT.Exp, [c], scale=-1.0)
        c = p.act(x1, x1, ACT.Ln, [c], bias=one)
        c = p.stt(x1, x0, 0.0, x1, ALU.max, ALU.add, [c])
        g_ok = p.tt(gg, x1, nea, ALU.mult, [c, nea_ok])
        i, bfr = bank.take()
        B = GB[i]
        m = p.mm(B, ps[:, B, 0:4], CE["tri64"], gg, True, True, [g_ok, cste_ok, bfr])
        m = p.mm(B, ps[:, B, 4:8], CE["sup64"], gg, True, True, [g_ok])
        e1_ = p.act(eg, ps[:, B, 0:4], ACT.Exp, [m])
        e2_ = p.act(el, ps[:, B, 4:8], ACT.Exp, [m])
        bank.done(i, [e1_, e2_])
        be_ok = p.tt(be, beta, eg, ALU.mult, [e1_, beta_ok])
        a2_ = [p.act(A2[:, q, :], CE["tri64"], ACT.Identity, [g_ok, cste_ok, fr], scale=gg[:, q:q + 1]) for q in range(4)]
        i, bfr = bank.take()
        PR = ps[:, GB[i], :].rearrange("p (a b) -> p a b", a=4)
        m = p.mm(GB[i], ps[:, GB[i], :], C["ones"], A2.rearrange("p a b -> p (a b)"), True, True, [a2_, bfr])
        eg_ok = p.act(A6, PR, ACT.Exp, [m, fr])
        bank.done(i, [eg_ok])
        i, bfr = bank.take()
        md = p.mm(GB[i], ps[:, GB[i], :], CE["sup64"], A2.rearrange("p a b -> p (a b)"), True, True, [a2_, bfr])
        a = p.act(A0, ps[:, GB[i], :].rearrange("p (a b) -> p a b", a=4), ACT.Exp, [md, fr])
        bank.done(i, [a])
        a1_ = [p.act(A1[:, q, :], C["ident"], ACT.Identity, [beta_ok, fr, ld_c], scale=beta[:, q:q + 1]) for q in range(4)]
        i, bfr = bank.take()
        mb = p.mm(GB[i], ps[:, GB[i], :], CE["sup64"], A1.rearrange("p a b -> p (a b)"), True, True, [a1_, cste_ok, bfr])
        pb = p.act(A7, ps[:, GB[i], :].rearrange("p (a b) -> p a b", a=4), ACT.Identity, [mb, fr])
        bank.done(i, [pb])
        xn, y, at_ok, pqs, lts = [None] * 2, [None] * 2, [None] * 2, [], []
        for pr in range(2):
            hs = slice(2 * pr, 2 * pr + 2)
            pair = lambda i: ps[:, GB[i], 0:256].rearrange("p (a b) -> p a b", a=2)
            i, bfr = bank.take()
            for k in range(2):
                q = 2 * pr + k
                m = p.mm(GB[i], pair(i)[:, k, :], K2[:, q, sl], K2[:, q, sl], True, True, [heads[q], bfr])
            c = p.tt(A1[:, hs, :], pair(i), A0[:, hs, :], ALU.mult, [m, a, mb])
            bank.done(i, [c])
            lt = p.tt(A1[:, hs, :], A1[:, hs, :], A7[:, hs, :], ALU.mult, [c, pb])
            lts.append(lt)
            dec = p.tt(A0[:, hs, :], A0[:, hs, :], b2(CE["tri64"]), ALU.mult, [c])
            i, bfr = bank.take()
            for k in range(2):
                m = p.tr(GB[i], pair(i)[:, k, :], A1[:, 2 * pr + k, :], C["ident"], [lt, bfr])
            n0 = p.act(XN[pr][:, 0, :, :], pair(i), ACT.Identity, [m, fr], scale=-1.0)
            bank.done(i, [n0])
            n1 = p.act(XN[pr][:, 1, :, :], A1[:, hs, :], ACT.Identity, [lt, fr], scale=-1.0)
            xn[pr] = [p.vec(lambda e, o=XN[pr][:, k, :, :], m_=b2(CE[n]).bitcast(U32), d_=b2(C["ident"]): e.copy_predicated(o, m_, d_),
                            256, [n0, n1, cste_ok]) for k, n in enumerate(("n1", "n1t"))]
            i, bfr = bank.take()
            for k in range(2):
                q = 2 * pr + k
                m = p.mm(GB[i], pair(i)[:, k, :], K2[:, q, sl], Q2[:, q, sl], True, True, [heads[q], bfr])
            at_ok[pr] = p.tt(A5[:, hs, :], pair(i), A0[:, hs, :], ALU.mult, [m, dec, fr])
            bank.done(i, [at_ok[pr]])
            pqs.append(m)
        qg_ok = p.tt(Q2[:, :, sl], Q2[:, :, sl], A6, ALU.mult, [pqs, eg_ok])
        gl_ok = p.cp(glc, A6.rearrange("p a (c t) -> p a c t", t=64)[:, :, :, 63], [eg_ok, fr])
        y_free = [[at_ok[0]], [at_ok[1]]]
        for lev in (2, 4, 8, 16, 32):
            for pr in range(2):
                i, bfr = bank.take()
                B = GB[i]
                for q in range(2):
                    m = p.mm(B, ps[:, B, q * P:(q + 1) * P], A1[:, 2 * pr + q, :], XN[pr][:, 0, q, :], True, True, [xn[pr], bfr])
                y[pr] = p.tt(A0[:, 2 * pr:2 * pr + 2, :], ps[:, B, 0:256].rearrange("p (a b) -> p a b", a=2),
                             b2(CE[f"m{lev}"]), ALU.mult, [m, y_free[pr]])
                bank.done(i, [y[pr]])
            for pr in range(2):
                i, bfr = bank.take()
                B = GB[i]
                lo = 0 if lev < 32 else 1
                for q in range(2):
                    Y = A0[:, 2 * pr + q, :]
                    if lev < 32:
                        m = p.mm(B, ps[:, B, q * P:(q + 1) * P], XN[pr][:, 1, q, :], Y, True, True, [y[pr], bfr])
                    m = p.mm(B, ps[:, B, 256 + q * P:256 + (q + 1) * P], Y, XN[pr][:, 1, q, :], True, True, [y[pr], bfr])
                xn[pr] = [p.tt(XN[pr][:, lo:2, :, :].rearrange("p a b c -> p (a b c)"),
                               XN[pr][:, lo:2, :, :].rearrange("p a b c -> p (a b c)"), ps[:, B, 256 * lo:512], ALU.subtract, [m])]
                bank.done(i, xn[pr])
                y_free[pr] = [m]
        n_ok = xn
        i, bfr = bank.take()
        for q in range(4):
            m = p.tr(GB[i], ps[:, GB[i], q * P:(q + 1) * P], K2[:, q, sl], C["ident"], [heads, bfr])
        pk = ps[:, GB[i], :].rearrange("p (a b) -> p a b", a=4)
        kb_ok = [p.act(A6[:, q, :], pk[:, q, :], ACT.Identity, [m, be_ok, gl_ok, qg_ok], scale=be[:, q:q + 1]) for q in range(4)]
        kg_ok = [p.act(A7[:, q, :], pk[:, q, :], ACT.Identity, [m, e2_, fr, lts], scale=el[:, q:q + 1]) for q in range(4)]
        bank.done(i, kb_ok + kg_ok)
        i, bfr = bank.take()
        for q in range(4):
            m = p.tr(GB[i], ps[:, GB[i], q * P:(q + 1) * P], V2[:, q, sl], C["ident"], [heads, bfr])
        vb_ok = [p.act(A8[:, q, :], ps[:, GB[i], q * P:(q + 1) * P], ACT.Identity, [m, beta_ok, fr], scale=beta[:, q:q + 1])
                 for q in range(4)]
        bank.done(i, vb_ok)
        N = lambda q: XN[q // 2][:, 1, q % 2, :]
        i, pw, m = four(lambda q, o: (o, A6[:, q, :], N(q)), [kb_ok, n_ok])
        w_ok = p.act(A2, pw, ACT.Identity, [m, xn, md], scale=-1.0)
        bank.done(i, [w_ok])
        o, ofr = bankO.take()
        PO = ps[:, OB[o], :].rearrange("p (a b) -> p a b", a=4)
        mo = None
        for c in range(2):
            r = slice(64 * c, 64 * c + 64)
            qsl = slice(j * P + 64 * c, j * P + 64 * c + 64)
            first = b == 0 and c == 0
            i, bfr = bank.take()
            B = GB[i]
            for q in range(4):
                m = p.mm(B, ps[r, B, q * P:(q + 1) * P], N(q)[:, r], A8[:, q, :], True, first, [vb_ok, n_ok, bfr])
                if not first:
                    m = p.mm(B, ps[r, B, q * P:(q + 1) * P], A2[:, q, r], SG[:, q, :], False, True, [w_ok, E["S"]])
            vn = p.act(A0[r, :, :], ps[r, B, :].rearrange("p (a b) -> p a b", a=4), ACT.Identity, [m, y_free])
            bank.done(i, [vn])
            for q in range(4):
                m = p.mm(OB[o], PO[:, q, r], A0[r, q, :], A5[r, q, r], True, first, [vn, at_ok, ofr, mo])
                if not first:
                    m = p.mm(OB[o], PO[:, q, r], SG[:, q, :], Q2[:, q, qsl], False, True, [qg_ok, E["S"]])
            mo = m
            if b == NB - 1 and c == 1:
                break
            i, bfr = bank.take()
            B = GB[i]
            new = []
            for q in range(4):
                m = p.mm(B, ps[:, B, q * P:(q + 1) * P], A7[r, q, :], A0[r, q, :], True, True, [kg_ok, vn, bfr])
            for q in range(4):
                if first:
                    new.append(p.cp(SG[:, q, :], ps[:, B, q * P:(q + 1) * P], [m, gate_e]))
                else:
                    new.append(p.stt(SG[:, q, :], SG[:, q, :], glc[:, q, c:c + 1], ps[:, B, q * P:(q + 1) * P],
                                     ALU.mult, ALU.add, [m, mo, gl_ok]))
            bank.done(i, new)
            E["S"] = new
        a = p.act(A0, PO, ACT.Square, [mo, E["S"], y_free])
        i, bfr = bank.take()
        m = p.mm(GB[i], ps[:, GB[i], :], C["ones"], A0.rearrange("p a b -> p (a b)"), True, True, [a, bfr])
        c = p.act(A0, ps[:, GB[i], :].rearrange("p (a b) -> p a b", a=4), ACT.Ln, [m], bias=eps, scale=1.0 / P)
        bank.done(i, [c])
        c = p.act(A0, A0, ACT.Exp, [c], scale=-0.5)
        d = p.stt(A0, PO, V("gdn"), A0, ALU.mult, ALU.mult, [c, mo])
        bankO.done(o, [d])
        d = p.tt(oT[:, 0:4, sl], oT[:, 0:4, sl], A0, ALU.mult, [d, heads, zs])
        E["blk"] = [d, mo, E["S"]]
        return [d], [mo, m, qg_ok]

    def sparse_prep(chunk, rh):
        T = P * len(chunk)
        at = chunk_cols(chunk)
        t0 = chunk[0] * P
        out_ = []
        w = Weights("win2", 7)
        i, last = project(w, 0, T, rh, hn[:, :, at])
        hn_users.append(last)
        a = p.act(pT[:, 0:T], ps[:, proj.banks[i], 0:T], ACT.Square, [last, E["pT"], gate_e])
        x, xfr = bankX.take()
        m = p.mm(XB[x], ps[:, XB[x], 0:T], C["ones"], pT[:, 0:T], True, True, [a, xfr])
        c = p.act(pT[:, 0:T], ps[:, XB[x], 0:T], ACT.Ln, [m], bias=eps, scale=1.0 / P)
        bankX.done(x, [c])
        c = p.act(pT[:, 0:T], pT[:, 0:T], ACT.Exp, [c], scale=-0.5)
        kt = p.stt(ckvT[:, t0:t0 + T], ps[:, proj.banks[i], 0:T], V("gkv"), pT[:, 0:T], ALU.mult, ALU.mult, [c, last, a, gate_e])
        proj.ring.done(i, [kt])
        E["pT"] = [kt]
        out_.append(kt)
        x, xfr = bankX.take()
        for j, b in enumerate(chunk):
            m = p.tr(XB[x], ps[:, XB[x], j * P:(j + 1) * P], ckvT[:, b * P:(b + 1) * P], C["ident"], [kt, xfr])
        c = p.act(ckvR[:, chunk[0]:chunk[-1] + 1, :], ps[:, XB[x], 0:T].rearrange("p (a b) -> p a b", b=P), ACT.Identity,
                  [m, gate_e])
        bankX.done(x, [c])
        out_.append(c)
        i, last = project(w, 1, T, rh, hn[:, :, at])
        hn_users.append(last)
        c = p.act(ikT[:, t0:t0 + T], ps[:, proj.banks[i], 0:T], ACT.Identity, [last, gate_e])
        proj.ring.done(i, [c])
        out_.append(c)
        bws = {}
        for j, b in placed(chunk):
            i, bfr = proj.ring.take()
            for kc in range(KC):
                last = p.mm(proj.banks[i], ps[:, proj.banks[i], 0:16], hn[:, kc, j * P:(j + 1) * P], w.at(kc, 2 * P, 16), kc == 0, kc == KC - 1,
                            [rh, w.load(kc), bfr])
                w.use(kc, last)
            hn_users.append(last)
            c1 = p.act(bawb[j][:, 0:8], ps[:, proj.banks[i], 0:8], ACT.Identity, [last, E["baw"]])
            c2 = p.act(bawb[j][:, 8:16], ps[:, proj.banks[i], 8:16], ACT.Identity, [last, E["baw"]], scale=8 ** -0.5 * 64 ** -0.5)
            proj.ring.done(i, [c1, c2])
            bws[b] = [c1, c2]
        w.done()
        w = Weights("win2", 6)
        for m in range(4):
            i, last = project(w, m, T, rh, hn[:, :, at])
            hn_users.append(last)
            c = p.act(iqT[:, m, at], ps[:, proj.banks[i], 0:T], ACT.Identity, [last, gate_e, E["iq"]])
            proj.ring.done(i, [c])
            out_.append(c)
        w.done()
        return out_, bws

    def sparse_rest(chunk, rh):
        T = P * len(chunk)
        at = chunk_cols(chunk)
        out_ = []
        w = Weights("win2", 4)
        for m in range(4):
            i, last = project(w, m, T, rh, hn[:, :, at])
            hn_users.append(last)
            c = p.act(qbT[:, m, at], ps[:, proj.banks[i], 0:T], ACT.Identity, [last, gate_e, E["qb"]])
            proj.ring.done(i, [c])
            out_.append(c)
        w.done()
        w = Weights("win2", 5)
        for m in range(4):
            i, last = project(w, m, T, rh, hn[:, :, at])
            hn_users.append(last)
            _, a = sigmoid_ps(oT[:, 4 + m, at], ps[:, proj.banks[i], 0:T], [last, free["oT"]])
            a = p.tt(oT[:, 4 + m, at], oT[:, 4 + m, at], ps[:, proj.banks[i], 0:T], ALU.mult, [a])
            proj.ring.done(i, [a])
            out_.append(a)
        w.done()
        return out_

    lgs = (lg0, lg1)
    bankS, SB = bankD, DB

    def sparse_choice(b, j, prep, bw):
        W = (b + 1) * P
        sl = slice(j * P, (j + 1) * P)
        if b == 0:
            mask = score[:, S - P:S]
            return mask, p.ts(mask, C["strict"], -BIG, None, ALU.mult, None, [cste_ok, E["score"]])
        else:
            iwv = bawb[j][:, 8:16]
            prev = E["score"]
            iqs = []
            for hh in range(8):
                x, xfr = bankS.take()
                half = slice(64 * (hh % 2), 64 * (hh % 2) + 64)
                m = p.mm(SB[x], ps[:, SB[x], 0:W], iqT[half, hh // 2, sl], ikT[half, 0:W], True, True, [prep, xfr])
                iqs.append(m)
                lb = lgs[hh % 2][:, 0:W]
                r = p.act(lb, ps[:, SB[x], 0:W], ACT.Relu, [m, E["lg"][hh % 2]])
                bankS.done(x, [r])
                if hh == 0:
                    s_ = p.ts(score[:, 0:W], lb, iwv[:, 0:1], None, ALU.mult, None, [r, bw, prev, E["mask"]])
                else:
                    s_ = p.stt(score[:, 0:W], lb, iwv[:, hh:hh + 1], score[:, 0:W], ALU.mult, ALU.add, [r, s_])
                E["lg"][hh % 2] = [s_]
            E["iq"] = iqs
            dg = slice(b * P, W)
            a = p.stt(score[:, dg], C["strict"], -BIG, score[:, dg], ALU.mult, ALU.add, [s_, ld_c])
            src = score[:, 0:W]
            for rnd in range(16):
                a = p.vec(lambda e, s=src: e.max(m8, s), W, [a, E["Wk"] if rnd == 0 else None])
                a = p.vec(lambda e, s=src: e.match_replace(Wk[:, 0:W], m8, s, -3.3e38), W, [a, E["Wk"] if rnd == 0 else None])
                src = Wk[:, 0:W]
            E["score"] = [a]
            return Wk[:, 0:W], p.ts(Wk[:, 0:W], Wk[:, 0:W], -3.15e38, -BIG, ALU.is_ge, ALU.mult, [a])

    def sparse_block(b, j, prep, prep2, choice):
        W = (b + 1) * P
        sl = slice(j * P, (j + 1) * P)
        mask, m_ok = choice
        near = min(W, 256)
        rd = []
        res, qbs = [], []
        for hh in range(4):
            x, xfr = bankS.take()
            m = p.mm(SB[x], ps[:, SB[x], 0:W], qbT[:, hh, sl], ckvT[:, 0:W], True, True, [prep, prep2, xfr])
            qbs.append(m)
            lgt = lgs[hh % 2]
            lb = lgt[:, 0:W]
            s, sfr = ringS.take()
            mx, mx2, sm_ = (small[:, s, k:k + 1] for k in range(3))
            nl, tl = lgt[:, W - near:W], toep[:, hh, 256 - near:256]
            a = p.stt(lb, ps[:, SB[x], 0:W], float(P) ** -0.5, mask, ALU.mult, ALU.add, [m, m_ok, E["lg"][hh % 2]])
            rd.append(a)
            bankS.done(x, [a])
            a1 = p.vec(lambda e, n=nl, t_=tl, o=mx: e.tensor_tensor_reduce(n, n, t_, 1.0, -BIG, ALU.add, ALU.max, o),
                       near, [a, toep_ok, sfr])
            if W > near:
                fl = lgt[:, 0:W - near]
                a2 = p.vec(lambda e, f=fl, t_=toep[:, hh, 0:1], o=mx2: e.tensor_scalar(f, f, t_, None, ALU.add, ALU.max, accum_out=o),
                           W - near, [a, toep_ok, sfr])
                a1 = p.tt(mx, mx, mx2, ALU.max, [a1, a2])
            a = p.ts(mx, mx, -1.0, None, ALU.mult, None, [a1])
            a = p.act(lb, lb, ACT.Exp, [a], bias=mx, accum=sm_)
            c = p.vec(lambda e, o=sm_: e.reciprocal(o, o), 1, [a], 8.0)
            a = p.act(lb, lb, ACT.Identity, [a, c], scale=sm_)
            ringS.done(s, [a])
            x, xfr = bankS.take()
            for n in range(b + 1):
                m = p.tr(SB[x], ps[:, SB[x], n * P:(n + 1) * P], lgt[:, n * P:(n + 1) * P], C["ident"], [a, xfr])
            E["lg"][hh % 2] = [m]
            c = p.act(pT[:, 0:W], ps[:, SB[x], 0:W], ACT.Identity, [m, E["pT"]])
            bankS.done(x, [c])
            x, xfr = bankS.take()
            B = SB[x]
            for n in range(b + 1):
                m = p.mm(B, ps[:, B, 0:P], ckvR[:, n, :], pT[:, n * P:(n + 1) * P], n == 0, n == b, [c, prep, xfr])
            c = p.act(ob, ps[:, B, 0:P], ACT.Identity, [m, E["ob"]])
            E["pT"] = [m]
            m = p.mm(B, ps[:, B, P:2 * P], wuv[:, hh, :], ob, True, True, [c, wuv_ok])
            E["ob"] = [m]
            c = p.tt(oT[:, 4 + hh, sl], oT[:, 4 + hh, sl], ps[:, B, P:2 * P], ALU.mult, [m, prep2])
            bankS.done(x, [c])
            res.append(c)
        if b == 0:
            E["mask"] = rd
        else:
            E["Wk"] = rd
        E["qb"] = qbs
        return res

    bankG, VBS = Ring(2), (VB, VB + 1)

    def finish(b, j, w2, after):
        ring, fb = (bankG, VBS) if b == NB - 1 else (bankD, DB)
        s, sfr = ringS.take()
        c = [small[:, s, k:k + 1] for k in range(3)]
        banks, lasts, sqs = [], [], []
        for n in range(2):
            i, fr = ring.take()
            for k, kc in enumerate((4, 5, 6, 7, 0, 1, 2, 3)):
                last = p.mm(fb[i], ps[:, fb[i], :], oT[:, kc, j * P:(j + 1) * P], w2[n].at(kc, 0, 512), k == 0, k == KC - 1,
                            [after[kc], w2[n].load(kc), fr])
                w2[n].use(kc, last)
            banks.append(i)
            lasts.append(last)
            sqs.append(p.act(X[0][:, n * 512:n * 512 + 512], ps[:, fb[i], :], ACT.Square, [last, sfr, free["X0"]], accum=c[n]))
        a = p.tt(c[2], c[0], c[1], ALU.add, sqs)
        a = p.act(c[2], c[2], ACT.Ln, [a], bias=eps, scale=1.0 / D)
        a = p.act(c[2], c[2], ACT.Exp, [a], scale=-0.5)
        new = []
        for n in range(2):
            half = slice(n * 512, n * 512 + 512)
            d = p.stt(X[0][:, half], ps[:, fb[banks[n]], :], c[2], row[1][:, half], ALU.mult, ALU.mult, [a, sqs, rp])
            ring.done(banks[n], [d])
            new.append(p.tt(h[:, b, half], h[:, b, half], X[0][:, half], ALU.add, [d, hw[b], hr[b]]))
        ringS.done(s, new)
        free["X0"] = new
        hw[b], hr[b] = new, []
        return lasts

    E = {k: [] for k in ("cin", "carry", "QKV", "sgE", "blk", "S", "pT", "baw", "iq", "qb", "score", "Wk", "ob", "mask")}
    E["lg"] = [[], []]
    for k in range(2):
        bankG.done(k, [free["V"]])
    if upto == "E":
        gate_e = p.fill(spot[:, :], 0.0, [usersC, gate_c])
        me = [mark(f"m_e{k}") for k in range(7)]
        cste_ok = p.dma("sp", cste, t["cste"], me[0], P * cste.shape[1] * 4, [gate_e])
        wuv_ok = p.dma("sp", wuv, t["wuv"], me[1], P * 512 * 4, [gate_e])
        ab = t["ab"]
        ab_ok = p.dma("sp", abr, bass.AP(ab.tensor, ab.offset, [[0, P], [1, 8]]), me[2], P * 32, [gate_e])
        a = p.act(nea, abr[:, 0:4], ACT.Exp, [ab_ok])
        nea_ok = p.ts(nea, nea, -1.0, None, ALU.mult, None, [a])
        abr_ok = ab_ok
        E["carry"] = [p.fill(carry, 0.0, [gate_e])]
        hot_ok = p.dma("sp", Wk[0:32, 0:384], t["hot"], me[3], 32 * 384 * 4, [gate_e])
        rel_ok = p.dma("sp", score[0:32, 0:4], t["rel"], me[4], 32 * 16, [gate_e])
        x, xfr = bankX.take()
        m = p.mm(XB[x], ps[0:4, XB[x], 0:384], score[0:32, 0:4], Wk[0:32, 0:384], True, True, [hot_ok, rel_ok, xfr])
        c = p.cp(pT[0:4, 0:384], ps[0:4, XB[x], 0:384], [m, gate_e])
        bankX.done(x, [c])
        scr = nc.dram_tensor("bias_rows", (4, 384), F32).ap()
        scr_ok = p.dma("sp", scr, pT[0:4, 0:384], me[5], 4 * 384 * 4, [c])
        back = p.dma("sp", qbT.rearrange("p a b -> p (a b)").rearrange("p (a b) -> p a b", a=4),
                     bass.AP(scr.tensor, 0, [[1, P], [384, 4], [1, 256]]), me[6], P * 4096, [scr_ok, gate_e])
        flip_ok = p.dma("sp", lg0[:, 0:P], t["flip"], mark("m_e7"), P * P * 4, [gate_e])
        toep_ok, ms = [], []
        for half in range(2):
            x, xfr = bankX.take()
            mf = p.mm(XB[x], ps[:, XB[x], :], lg0[:, 0:P], qbT.rearrange("p a b -> p (a b)")[:, half * 512:half * 512 + 512],
                      True, True, [back, flip_ok, xfr])
            c2 = p.act(toep[:, 2 * half:2 * half + 2, :].rearrange("p a b -> p (a b)"), ps[:, XB[x], :], ACT.Identity, [mf])
            bankX.done(x, [c2])
            toep_ok.append(c2)
            ms.append(mf)
        E["qb"], E["lg"][0] = ms, ms
        E["pT"], E["Wk"], E["score"] = [scr_ok], [m], [m]
        g_p = gain(5, mod2[:, 8:16], V("pre"), mv[1])
        gp = p.tt(mod2[:, 16:24], mod2[:, 16:24], V("post"), ALU.mult, [mv[2]])
        rf = broadcast_row(0, V("fin"), ld_v)
        rp = broadcast_row(1, mod2[:, 16:24], gp)
        hn_again()
        last_use = {"hn": [free["hn"]] * 2, "oT": [free["oT"]] * 2, "QKV": [[]] * 2, "iq": [[]] * 2, "qb": [E["qb"]] * 2, "baw": [[]] * 2}
        for chunk in CHUNKS_E:
            if chunk[0] == NB - 1:
                proj.ring, proj.banks = bankG, VBS
            for k, halves in last_use.items():
                (free if k in free else E)[k] = [halves[b % 2] for b in chunk]
            if chunk[0] == 3:
                out_proj()
            rh = []
            for j, b in placed(chunk):
                s, sfr = ringS.take()
                r1, s2, r2 = (small[:, s, k:k + 1] for k in range(3))
                spare = hn[:, :, j * P:(j + 1) * P]
                q1 = p.act(spare, h[:, b, :].rearrange("p (a b) -> p a b", a=KC), ACT.Square, [hw[b], free["hn"], sfr], accum=r1)
                t_ = p.tt(xs[:, :], h[:, b, :], row[0][:, :], ALU.mult, [rf, hw[b], free["xs"]])
                q2 = p.act(spare, xs.rearrange("p (a b) -> p a b", a=KC), ACT.Square, [t_, q1], accum=s2)
                a = p.act(r1, r1, ACT.Ln, [q1], bias=eps, scale=1.0 / D)
                a = p.act(r1, r1, ACT.Exp, [a], scale=-0.5)
                f = p.ts(h[:, b, :], xs[:, :], r1, None, ALU.mult, None, [a, t_, q1, hr[b]])
                d = p.stt(r2, r1, r1, s2, ALU.mult, ALU.mult, [a, q2, sfr])
                d = p.act(r2, r2, ACT.Ln, [d], bias=eps, scale=1.0 / D)
                d = p.act(r2, r2, ACT.Exp, [d], scale=-0.5)
                d = p.tt(r2, r2, r1, ALU.mult, [d])
                a = p.act(xs[:, :], xs[:, :], ACT.Identity, [d, q2, f], scale=r2)
                ringS.done(s, [a, f])
                hw[b], hr[b] = [f], []
                trs, evs = spread(a, j, [(hn, gT[:, 5, :], mod2[:, 0:8], [g_p, mv[0], free["hn"], q2])])
                free["xs"] = trs
                rh += evs[0]
            prep, bws = sparse_prep(chunk, rh)
            choice = {b: sparse_choice(b, j, prep, bws[b]) for j, b in placed(chunk)}
            scores = E["score"]
            if chunk[0] == 2:
                out_proj()
                free["oT"] = [last_use["oT"][b % 2] for b in chunk]
            heads, zs = gated_heads(chunk, rh)
            prep2 = sparse_rest(chunk, rh)
            for b in chunk:
                last_use["hn"][b % 2] = list(hn_users)
            hn_users.clear()
            mixed = {}
            bwu, qkvu = [], []
            for j, b in placed(chunk):
                mixed[b] = sparse_block(b, j, prep, prep2, choice[b])
            bwu.append(scores)
            for j, b in placed(chunk):
                r, u = gated_block(b, j, heads, zs, bws[b])
                mixed[b] = [r] * 4 + mixed[b]
                qkvu += u
                bwu.append(E["blk"])
            for b in chunk:
                for k, use in (("baw", bwu), ("QKV", qkvu), ("iq", E["iq"]), ("qb", E["qb"])):
                    last_use[k][b % 2] = use

            def out_proj(chunk=chunk, mixed=mixed):
                w2 = [Weights("wout2", 0), Weights("wout2", 1)]
                used = []
                for j, b in placed(chunk):
                    used += finish(b, j, w2, mixed[b])
                for w in w2:
                    w.done()
                for b in chunk:
                    last_use["oT"][b % 2] = used
        out_proj()

    m_o = [mark(f"m_o{b}") for b in range(NB)]
    last = []
    for b in range(NB):
        last.append(p.dma("sp", out[b * P:(b + 1) * P, :], h[:, b, :], m_o[b], P * D * 4, [hw[b]]))
    p.emit(nc, sems, last)
    ctx.close()
    return p


def tiles(w):
    k, n = w.shape
    g = -(-n // 512)
    if n % 512:
        w = np.concatenate([w, np.zeros((k, g * 512 - n), w.dtype)], axis=1)
    return np.ascontiguousarray(w.reshape(4, 2, P, g, 512).transpose(3, 0, 2, 1, 4))


def columns(v):
    return v.reshape(-1, P).T


def layout(i):
    i = {k: np.asarray(v) for k, v in i.items()}
    o = {"x": i["x"][0]}
    for l in range(2):
        o[f"pq{l}"] = tiles(i["peer_w_q"][l])
        o[f"sub{l}"] = np.ascontiguousarray(i["peer_subkeys"][l].reshape(8, P, P).transpose(2, 0, 1).reshape(P, 2, 512))
    w = i["hgrn_w_in"][0].reshape(D, 4, NH, P)
    o["win"] = tiles(np.stack([w[:, 0], w[:, 1], w[:, 3], w[:, 2]], axis=2).reshape(D, 4 * D))
    o["wout"] = tiles(i["hgrn_w_out"][0])
    o["ada0"] = tiles(i["ada_w"][0])
    o["ada1"] = i["ada_w"][1].T.reshape(-1, P, D)
    o["kvada"] = i["kv_ada_w"].T.reshape(-1, P, D)
    o["cc"] = np.concatenate([i["c"], i["c_2"]], axis=0)
    o["kvw"] = tiles(i["kv_w"])
    o["sbq"] = tiles(i["sb_w_q"][0])
    o["sbo"] = tiles(i["sb_w_out"][0])
    o["peer_u"] = i["peer_u"].reshape(-1, D)
    o["peer_v"] = i["peer_v"].reshape(-1, D)
    o["ada_2"] = i["w_ada_2"][0].T.reshape(-1, P, D)
    w = i["w_in_2"][0]
    qkv = w[:, 0:1536].reshape(D, 3, 4, P)
    z = w[:, 1536:2048].reshape(D, 1, 4, P)
    ba, qb, ckv, zb = w[:, 2048:2056], w[:, 2056:2568], w[:, 2568:2696], w[:, 2696:3208]
    iq, ik, iw = w[:, 3208:3720], w[:, 3720:3784], w[:, 3784:3792]
    heads = np.concatenate([qkv, z], axis=1).transpose(0, 2, 1, 3).reshape(D, 2048)
    o["win2"] = tiles(np.concatenate([heads, qb, zb, iq, ckv, ik, ik, ba, iw], axis=1))
    o["wout2"] = tiles(i["w_out_2"][0])
    o["wuv"] = np.ascontiguousarray(i["w_uv_2"][0].transpose(1, 0, 2))
    o["ab"] = np.stack([i["a_log_2"][0], i["dt_bias_2"][0]]).reshape(1, 8)
    o["rel"] = i["rel_bias_2"]
    v = {"c": i["c"], "ada_b0": i["ada_b"][0], "ada_b1": i["ada_b"][1],
         "mix0": i["norm_mix_g"][0], "mix1": i["norm_mix_g"][1], "ffn0": i["norm_ffn_g"][0], "ffn1": i["norm_ffn_g"][1],
         "lb0": i["hgrn_lb_logits"][0], "lb1": i["hgrn_lb_logits"][1], "onorm": i["hgrn_onorm_g"], "kv_b": i["kv_ada_b"],
         "kv_g": i["kv_norm_g"], "fin": i["final_norm_g"], "b_2": i["b_ada_2"], "pre": i["g_pre_2"], "post": i["g_post_2"],
         "conv": i["conv_w_2"], "gdn": i["g_gdn_2"], "gkv": i["g_kv_2"]}
    o["vecs"] = np.concatenate([columns(v[k]) for k in VECS], axis=1)
    o["cst"] = const_array(CONSTS)
    o["hot"] = constants()["hot"][0:32]
    o["flip"] = constants()["ident"][::-1]
    o["cste"] = const_array(CONSTS_E)
    return {k: np.ascontiguousarray(a) for k, a in o.items()}


def kernel(**inputs):
    import concourse.bacc as bacc
    from concourse.bass_utils import run_bass_kernel_spmd as run

    arrays = layout(inputs)
    nc = bacc.Bacc("TRN2", target_bir_lowering=False, num_devices=1)
    t = {k: nc.dram_tensor(f"in_{k}_dram", a.shape, mybir.dt.from_np(a.dtype), kind="ExternalInput").ap()
         for k, a in arrays.items()}
    out = nc.dram_tensor("out_0_dram", (S, D), F32, kind="ExternalOutput").ap()
    layer_stack_kernel(nc, t, out)
    r = run(nc, [{f"in_{k}_dram": a for k, a in arrays.items()}], core_ids=[0])
    return r.results[0]["out_0_dram"].reshape(1, S, D)
```
